# Optimizing a Trainium2 kernel written in Bass

```python
import functools
import jax
import jax.numpy as jnp
from jax import lax
import numpy as np

D_MODEL = 2048
BATCH = 1
SEQ = 256
DEPTH = 1
DEC_BATCH = 8
DEC_SEQ = 1
PAST_LEN = 2048
PAGE_SIZE = 128

NSA_HEADS = 16
NSA_KV_HEADS = 2
NSA_GROUP = NSA_HEADS // NSA_KV_HEADS
NSA_DH = 64
CMP_BLOCK = 32
CMP_STRIDE = 16
CMP_SPAN = CMP_BLOCK // CMP_STRIDE
CMP_HIDDEN = 64
SEL_BLOCK = 64
SEL_TOPK = 16
SEL_FORCE = 1.0e6
NSA_WINDOW = 512
DIL_PAIRS = ((128, 1), (512, 4), (2048, 16))
DIL_GROUPS = len(DIL_PAIRS)
DIL_HPG = 4
DIL_HEADS = DIL_GROUPS * DIL_HPG
DIL_DH = 128
ROPE_THETA = 500000.0
ROPE_FRACTION = 4
RMS_EPS = 1e-6
D_FF = ((8 * D_MODEL + 3 * 256 - 1) // (3 * 256)) * 256
Q_BLOCK = 128
NEG_INF = -1e30
NSA_Q_W = NSA_HEADS * NSA_DH
NSA_KV_W = 3 * 2 * NSA_KV_HEADS * NSA_DH
NSA_GATE_W = 3 * NSA_HEADS
DIL_QKV_W = 3 * DIL_HEADS * DIL_DH
MERGE_W = 2 * D_MODEL
PROJ_W = NSA_Q_W + NSA_KV_W + NSA_GATE_W + DIL_QKV_W + MERGE_W
PROJ_SPLITS = [NSA_Q_W, NSA_Q_W + NSA_KV_W, NSA_Q_W + NSA_KV_W + NSA_GATE_W,
               NSA_Q_W + NSA_KV_W + NSA_GATE_W + DIL_QKV_W]
DIL_OUT_W = DIL_HPG * DIL_DH

kernel_name = 'adaln_nsa_dilated_parallel_decoder_step'

def _rmsnorm(x, g):
    xf = x.astype(jnp.float32)
    y = xf * lax.rsqrt(jnp.mean(xf * xf, axis=-1, keepdims=True) + RMS_EPS)
    return (y * g.astype(jnp.float32)).astype(x.dtype)

def _rope(x, pos):
    rd = x.shape[-1] // ROPE_FRACTION
    half = rd // 2
    inv = ROPE_THETA ** (-jnp.arange(half, dtype=jnp.float32) * (2.0 / rd))
    ang = pos.astype(jnp.float32)[:, None] * inv[None, :]
    shape = (1, x.shape[1]) + (1,) * (x.ndim - 3) + (half,)
    cos = jnp.cos(ang).reshape(shape)
    sin = jnp.sin(ang).reshape(shape)
    xf = x.astype(jnp.float32)
    x1, x2 = xf[..., :half], xf[..., half:rd]
    out = jnp.concatenate([x1 * cos - x2 * sin, x2 * cos + x1 * sin, xf[..., rd:]], axis=-1)
    return out.astype(x.dtype)

def _masked_softmax(s, mask):
    s = jnp.where(mask, s.astype(jnp.float32), NEG_INF)
    m = jnp.max(s, axis=-1, keepdims=True)
    e = jnp.where(mask, jnp.exp(s - m), 0.0)
    den = jnp.maximum(jnp.sum(e, axis=-1, keepdims=True), 1e-30)
    return e / den, (m + jnp.log(den))[..., 0]

def _shared_attend(q, k, v, mask):
    s = jnp.einsum('bthgd,bkhd->bhgtk', q, k) * (q.shape[-1] ** -0.5)
    p, _ = _masked_softmax(s, mask)
    o = jnp.einsum('bhgtk,bkhd->bthgd', p.astype(v.dtype), v)
    return o, p

def _compress(kv, w1, w2, pe):
    B, L = kv.shape[:2]
    n_chunk = -(-L // CMP_STRIDE)
    kv = jnp.pad(kv, ((0, 0), (0, n_chunk * CMP_STRIDE - L), (0, 0), (0, 0), (0, 0)))
    ch = kv.reshape(B, n_chunk, CMP_STRIDE, 2, NSA_KV_HEADS, NSA_DH)
    n_blk = n_chunk - CMP_SPAN + 1
    hid = jnp.einsum('sld,slde->se', pe, w1)[None, None, :, None, :]
    for j in range(CMP_SPAN):
        hid = hid + jnp.einsum('bnlshd,slde->bnshe', ch[:, j:j + n_blk],
                               w1[:, j * CMP_STRIDE:(j + 1) * CMP_STRIDE])
    return jnp.einsum('bnshe,sed->bnshd', jax.nn.gelu(hid), w2)

def _cmp_attend(q, kvc, pos):
    kend = jnp.arange(kvc.shape[1]) * CMP_STRIDE + (CMP_BLOCK - 1)
    mask = kend[None, :] <= pos[:, None]
    return _shared_attend(q, kvc[:, :, 0], kvc[:, :, 1], mask)

def _select_blocks(p, pos, ns):
    imp = jnp.sum(p, axis=2)
    B, H, Tq, nb = imp.shape
    r = SEL_BLOCK // CMP_STRIDE
    imp = jnp.pad(imp, ((0, 0), (0, 0), (0, 0), (0, ns * r - nb))).reshape(B, H, Tq, ns, r)
    imp = imp.sum(-1) + jnp.pad(imp[..., :-1, r - 1], ((0, 0), (0, 0), (0, 0), (1, 0)))
    blk = jnp.arange(ns)[None, :]
    cur = (pos // SEL_BLOCK)[:, None]
    forced = (blk == 0) | (blk == cur) | (blk == cur - 1)
    score = jnp.where(forced, SEL_FORCE, imp)
    score = jnp.where(blk * SEL_BLOCK <= pos[:, None], score, NEG_INF)
    _, idx = lax.top_k(score, min(SEL_TOPK, ns))
    return idx

def _sel_attend(q, kvg, idx, pos):
    B, H, Tq, n = idx.shape
    k = kvg[..., 0, :].reshape(B, H, Tq, n * SEL_BLOCK, -1)
    v = kvg[..., 1, :].reshape(B, H, Tq, n * SEL_BLOCK, -1)
    kpos = (idx[..., None] * SEL_BLOCK + jnp.arange(SEL_BLOCK)).reshape(B, H, Tq, n * SEL_BLOCK)
    mask = kpos <= pos[None, None, :, None]
    s = jnp.einsum('bthgd,bhtkd->bhgtk', q, k) * (q.shape[-1] ** -0.5)
    p, _ = _masked_softmax(s, mask[:, :, None])
    return jnp.einsum('bhgtk,bhtkd->bthgd', p.astype(v.dtype), v)

def _window_prompt(q, kv):
    B, T = q.shape[:2]
    nq = T // Q_BLOCK
    span = Q_BLOCK + NSA_WINDOW
    kvp = jnp.pad(kv, ((0, 0), (NSA_WINDOW, 0), (0, 0), (0, 0), (0, 0)))
    kidx = jnp.arange(nq)[:, None] * Q_BLOCK + jnp.arange(span)[None, :]
    kvb = kvp[:, kidx]
    qb = q.reshape(B, nq, Q_BLOCK, NSA_KV_HEADS, NSA_GROUP, NSA_DH)
    qpos = jnp.arange(nq)[:, None] * Q_BLOCK + jnp.arange(Q_BLOCK)[None, :]
    kpos = (kidx - NSA_WINDOW)[:, None, :]
    mask = (kpos >= 0) & (kpos <= qpos[:, :, None]) & (kpos >= qpos[:, :, None] - NSA_WINDOW)
    s = jnp.einsum('bnthgd,bnkhd->bnhgtk', qb, kvb[:, :, :, 0]) * (NSA_DH ** -0.5)
    p, _ = _masked_softmax(s, mask[None, :, None, None])
    o = jnp.einsum('bnhgtk,bnkhd->bnthgd', p.astype(kv.dtype), kvb[:, :, :, 1])
    return o.reshape(q.shape)

def _nsa_combine(g, o_cmp, o_sel, o_win):
    return (g[:, :, 0, :, :, None] * o_cmp + g[:, :, 1, :, :, None] * o_sel
            + g[:, :, 2, :, :, None] * o_win)

def _dil_group(q, kv_seq, q_local, dil, n_keys):
    kl = q_local[:, None] - dil * jnp.arange(n_keys)[None, :]
    valid = kl >= 0
    kvg = kv_seq[:, jnp.maximum(kl, 0)]
    s = jnp.einsum('bthd,btkhd->bhtk', q, kvg[:, :, :, 0]) * (q.shape[-1] ** -0.5)
    p, lse = _masked_softmax(s, valid[None, None])
    o = jnp.einsum('bhtk,btkhd->bthd', p.astype(q.dtype), kvg[:, :, :, 1])
    return o, lse

def _dilated_mix(q, kv_seqs, q_locals):
    outs, lses = [], []
    for g, (w, d) in enumerate(DIL_PAIRS):
        o, l = _dil_group(q[:, :, g * DIL_HPG:(g + 1) * DIL_HPG], kv_seqs[g], q_locals[g], d, w // d + 1)
        outs.append(o)
        lses.append(l)
    wts = jnp.swapaxes(jax.nn.softmax(jnp.stack(lses), axis=0), -1, -2)
    out = sum(wts[g][..., None] * outs[g].astype(jnp.float32) for g in range(DIL_GROUPS))
    return out.astype(q.dtype)

def _project(h, w_in, pos):
    B, T, _ = h.shape
    p = jnp.einsum('btd,de->bte', h, w_in)
    q_nsa, kv_nsa, g_nsa, qkv_dil, g_merge = jnp.split(p, PROJ_SPLITS, axis=-1)
    q_nsa = _rope(q_nsa.reshape(B, T, NSA_KV_HEADS, NSA_GROUP, NSA_DH), pos)
    kv_nsa = kv_nsa.reshape(B, T, 3, 2, NSA_KV_HEADS, NSA_DH)
    kv_nsa = jnp.stack([_rope(kv_nsa[:, :, :, 0], pos), kv_nsa[:, :, :, 1]], axis=3)
    g_nsa = jax.nn.sigmoid(g_nsa.reshape(B, T, 3, NSA_KV_HEADS, NSA_GROUP))
    qkv_dil = qkv_dil.reshape(B, T, 3, DIL_HEADS, DIL_DH)
    q_dil = _rope(qkv_dil[:, :, 0], pos)
    kv_dil = jnp.stack([_rope(qkv_dil[:, :, 1], pos), qkv_dil[:, :, 2]], axis=2)
    g_merge = jax.nn.sigmoid(g_merge.reshape(B, T, 2, D_MODEL))
    return q_nsa, kv_nsa, g_nsa, q_dil, kv_dil, g_merge

def _mixer_prompt(q_nsa, kv_nsa, g_nsa, q_dil, kv_dil, *, cmp_w1, cmp_w2, cmp_pe):
    B, T = q_nsa.shape[:2]
    pos = jnp.arange(T)
    kv_cmp, kv_sel, kv_win = kv_nsa[:, :, 0], kv_nsa[:, :, 1], kv_nsa[:, :, 2]
    kvc = _compress(kv_cmp, cmp_w1, cmp_w2, cmp_pe)
    o_cmp, p_cmp = _cmp_attend(q_nsa, kvc, pos)
    ns = T // SEL_BLOCK
    idx = _select_blocks(p_cmp, pos, ns)
    blocks = kv_sel.reshape(B, ns, SEL_BLOCK, 2, NSA_KV_HEADS, NSA_DH)
    bidx = jnp.arange(B)[:, None, None, None]
    hidx = jnp.arange(NSA_KV_HEADS)[None, :, None, None]

    def sel_block(n):
        t0 = n * Q_BLOCK
        qb = lax.dynamic_slice_in_dim(q_nsa, t0, Q_BLOCK, axis=1)
        ib = lax.dynamic_slice_in_dim(idx, t0, Q_BLOCK, axis=2)
        kvg = blocks[bidx, ib, :, :, hidx]
        return _sel_attend(qb, kvg, ib, t0 + jnp.arange(Q_BLOCK))

    o_sel = lax.map(sel_block, jnp.arange(T // Q_BLOCK))
    o_sel = jnp.moveaxis(o_sel, 0, 1).reshape(q_nsa.shape)
    o_win = _window_prompt(q_nsa, kv_win)
    o_nsa = _nsa_combine(g_nsa, o_cmp, o_sel, o_win)

    kv_groups = [kv_dil[:, :, :, g * DIL_HPG:(g + 1) * DIL_HPG] for g in range(DIL_GROUPS)]

    def dil_block(n):
        t0 = n * Q_BLOCK
        qb = lax.dynamic_slice_in_dim(q_dil, t0, Q_BLOCK, axis=1)
        ql = t0 + jnp.arange(Q_BLOCK)
        return _dilated_mix(qb, kv_groups, [ql] * DIL_GROUPS)

    o_dil = lax.map(dil_block, jnp.arange(T // Q_BLOCK))
    o_dil = jnp.moveaxis(o_dil, 0, 1).reshape(B, T, DIL_HPG, DIL_DH)
    states = (kv_cmp, kv_sel, kv_win[:, T - min(NSA_WINDOW, T):],
              kv_groups[0][:, T - min(DIL_PAIRS[0][0], T):],
              kv_groups[1][:, T - min(DIL_PAIRS[1][0], T):],
              kv_groups[2][:, T - min(DIL_PAIRS[2][0], T):])
    return o_nsa, o_dil, states

def _mixer_sample(q_nsa, kv_nsa, g_nsa, q_dil, kv_dil, *, layer, cache_cmp, cache_sel, cache_win,
                  cache_dil1, cache_dil2, cache_dil3, page_table, cmp_w1, cmp_w2, cmp_pe):
    B, S = q_nsa.shape[:2]
    pos = PAST_LEN + jnp.arange(S)
    n_pages = page_table.shape[1]
    past_len = n_pages * PAGE_SIZE
    kv_cmp, kv_sel, kv_win = kv_nsa[:, :, 0], kv_nsa[:, :, 1], kv_nsa[:, :, 2]
    past_cmp = cache_cmp[layer, page_table].reshape(B, past_len, 2, NSA_KV_HEADS, NSA_DH)
    kvc = _compress(jnp.concatenate([past_cmp, kv_cmp], axis=1), cmp_w1, cmp_w2, cmp_pe)
    o_cmp, p_cmp = _cmp_attend(q_nsa, kvc, pos)
    ns = -(-(past_len + S) // SEL_BLOCK)
    idx = _select_blocks(p_cmp, pos, ns)
    n_sub = PAGE_SIZE // SEL_BLOCK
    nbp = n_pages * n_sub
    bidx = jnp.arange(B)[:, None, None, None]
    hidx = jnp.arange(NSA_KV_HEADS)[None, :, None, None]
    pool_blk = cache_sel.reshape(-1, SEL_BLOCK, 2, NSA_KV_HEADS, NSA_DH)
    jp = jnp.minimum(idx, nbp - 1)
    phys = (layer * cache_sel.shape[1] + page_table[bidx, jp // n_sub]) * n_sub + jp % n_sub
    g_past = pool_blk[phys, :, :, hidx]
    nbn = ns - nbp
    new_blk = jnp.pad(kv_sel, ((0, 0), (0, nbn * SEL_BLOCK - S), (0, 0), (0, 0), (0, 0)))
    new_blk = new_blk.reshape(B, nbn, SEL_BLOCK, 2, NSA_KV_HEADS, NSA_DH)
    g_new = new_blk[bidx, jnp.clip(idx - nbp, 0, nbn - 1), :, :, hidx]
    kvg = jnp.where((idx < nbp)[..., None, None, None], g_past, g_new)
    o_sel = _sel_attend(q_nsa, kvg, idx, pos)
    wb = cache_win.shape[1]
    kvw = jnp.concatenate([cache_win, kv_win], axis=1)
    ql = wb + jnp.arange(S)
    kl = jnp.arange(wb + S)
    wmask = (kl[None, :] <= ql[:, None]) & (kl[None, :] >= ql[:, None] - NSA_WINDOW)
    o_win, _ = _shared_attend(q_nsa, kvw[:, :, 0], kvw[:, :, 1], wmask)
    o_nsa = _nsa_combine(g_nsa, o_cmp, o_sel, o_win)
    bufs = (cache_dil1, cache_dil2, cache_dil3)
    seqs = [jnp.concatenate([bufs[g], kv_dil[:, :, :, g * DIL_HPG:(g + 1) * DIL_HPG]], axis=1)
            for g in range(DIL_GROUPS)]
    o_dil = _dilated_mix(q_dil, seqs, [bufs[g].shape[1] + jnp.arange(S) for g in range(DIL_GROUPS)])
    states = (kv_cmp, kv_sel, kvw[:, S:], seqs[0][:, S:], seqs[1][:, S:], seqs[2][:, S:])
    return o_nsa, o_dil, states

def _layer(x, c, pos, mixer, w_ada, b_ada, norm1_g, w_in, w_br_nsa, w_br_dil, w_out,
           norm2_g, w_gate, w_up, w_down):
    B, T = x.shape[:2]
    mod = jnp.einsum('bd,de->be', jax.nn.silu(c), w_ada) + b_ada
    shift1, scale1, gate1, shift2, scale2, gate2 = jnp.split(mod[:, None, :], 6, axis=-1)
    h = _rmsnorm(x, norm1_g) * (1 + scale1) + shift1
    q_nsa, kv_nsa, g_nsa, q_dil, kv_dil, g_merge = _project(h, w_in, pos)
    o_nsa, o_dil, states = mixer(q_nsa, kv_nsa, g_nsa, q_dil, kv_dil)
    y_a = jnp.einsum('btk,kd->btd', o_nsa.reshape(B, T, NSA_Q_W), w_br_nsa)
    y_b = jnp.einsum('btk,kd->btd', o_dil.reshape(B, T, DIL_OUT_W), w_br_dil)
    mix = jnp.einsum('btd,de->bte', g_merge[:, :, 0] * y_a + g_merge[:, :, 1] * y_b, w_out)
    x = x + gate1 * mix
    h = _rmsnorm(x, norm2_g) * (1 + scale2) + shift2
    f = jax.nn.silu(jnp.einsum('btd,df->btf', h, w_gate)) * jnp.einsum('btd,df->btf', h, w_up)
    x = x + gate2 * jnp.einsum('btf,fd->btd', f, w_down)
    return x, states

def setup_inputs(seed: int = 0) -> dict:
    key = jax.random.key(seed)
    ks = jax.random.split(key, 26)
    n_pages = PAST_LEN // PAGE_SIZE
    n_pool = (DEC_BATCH * n_pages * 5) // 4
    nsa_row = (2, NSA_KV_HEADS, NSA_DH)
    dil_row = (2, DIL_HPG, DIL_DH)

    def nrm(k, shape, scale=1.0):
        return jax.random.normal(k, shape, jnp.float32) * scale

    page_table = jax.random.permutation(ks[8], n_pool)[:DEC_BATCH * n_pages]
    page_table = page_table.reshape(DEC_BATCH, n_pages).astype(jnp.int32)
    return {
        'x_prompt': nrm(ks[0], (BATCH, SEQ, D_MODEL)),
        'x_sample': nrm(ks[1], (DEC_BATCH, DEC_SEQ, D_MODEL)),
        'cache_cmp_kv': nrm(ks[2], (DEPTH, n_pool, PAGE_SIZE) + nsa_row),
        'cache_sel_kv': nrm(ks[3], (DEPTH, n_pool, PAGE_SIZE) + nsa_row),
        'cache_win_kv': nrm(ks[4], (DEPTH, DEC_BATCH, min(NSA_WINDOW, PAST_LEN)) + nsa_row),
        'cache_dil1_kv': nrm(ks[5], (DEPTH, DEC_BATCH, min(DIL_PAIRS[0][0], PAST_LEN)) + dil_row),
        'cache_dil2_kv': nrm(ks[6], (DEPTH, DEC_BATCH, min(DIL_PAIRS[1][0], PAST_LEN)) + dil_row),
        'cache_dil3_kv': nrm(ks[7], (DEPTH, DEC_BATCH, min(DIL_PAIRS[2][0], PAST_LEN)) + dil_row),
        'page_table': page_table,
        'c_prompt': nrm(ks[9], (BATCH, D_MODEL)),
        'c_sample': nrm(ks[10], (DEC_BATCH, D_MODEL)),
        'w_ada': nrm(ks[11], (DEPTH, D_MODEL, 6 * D_MODEL), D_MODEL ** -0.5),
        'b_ada': nrm(ks[12], (DEPTH, 6 * D_MODEL), 0.02),
        'norm1_g': 1.0 + nrm(ks[13], (DEPTH, D_MODEL), 0.02),
        'w_in': nrm(ks[14], (DEPTH, D_MODEL, PROJ_W), D_MODEL ** -0.5),
        'cmp_w1': nrm(ks[15], (DEPTH, 2, CMP_BLOCK, NSA_DH, CMP_HIDDEN), (CMP_BLOCK * NSA_DH) ** -0.5),
        'cmp_w2': nrm(ks[16], (DEPTH, 2, CMP_HIDDEN, NSA_DH), CMP_HIDDEN ** -0.5),
        'cmp_pe': nrm(ks[17], (DEPTH, 2, CMP_BLOCK, NSA_DH), 0.5),
        'w_br_nsa': nrm(ks[18], (DEPTH, NSA_Q_W, D_MODEL), NSA_Q_W ** -0.5),
        'w_br_dil': nrm(ks[19], (DEPTH, DIL_OUT_W, D_MODEL), DIL_OUT_W ** -0.5),
        'w_out': nrm(ks[20], (DEPTH, D_MODEL, D_MODEL), D_MODEL ** -0.5),
        'norm2_g': 1.0 + nrm(ks[21], (DEPTH, D_MODEL), 0.02),
        'w_gate': nrm(ks[22], (DEPTH, D_MODEL, D_FF), D_MODEL ** -0.5),
        'w_up': nrm(ks[23], (DEPTH, D_MODEL, D_FF), D_MODEL ** -0.5),
        'w_down': nrm(ks[24], (DEPTH, D_FF, D_MODEL), D_FF ** -0.5),
        'normf_g': 1.0 + nrm(ks[25], (D_MODEL,), 0.02),
    }

def reference(x_prompt, x_sample, cache_cmp_kv, cache_sel_kv, cache_win_kv, cache_dil1_kv,
              cache_dil2_kv, cache_dil3_kv, page_table, c_prompt, c_sample, w_ada, b_ada, norm1_g,
              w_in, cmp_w1, cmp_w2, cmp_pe, w_br_nsa, w_br_dil, w_out, norm2_g, w_gate, w_up,
              w_down, normf_g):
    pos_p = jnp.arange(x_prompt.shape[1])
    pos_s = PAST_LEN + jnp.arange(x_sample.shape[1])
    xp, xs = x_prompt, x_sample
    p_states, s_states = [], []
    for l in range(DEPTH):
        mix_p = functools.partial(_mixer_prompt, cmp_w1=cmp_w1[l], cmp_w2=cmp_w2[l], cmp_pe=cmp_pe[l])
        xp, st = _layer(xp, c_prompt, pos_p, mix_p, w_ada[l], b_ada[l], norm1_g[l], w_in[l],
                        w_br_nsa[l], w_br_dil[l], w_out[l], norm2_g[l], w_gate[l], w_up[l], w_down[l])
        p_states.append(st)
        mix_s = functools.partial(_mixer_sample, layer=l, cache_cmp=cache_cmp_kv, cache_sel=cache_sel_kv,
                                  cache_win=cache_win_kv[l], cache_dil1=cache_dil1_kv[l],
                                  cache_dil2=cache_dil2_kv[l], cache_dil3=cache_dil3_kv[l],
                                  page_table=page_table, cmp_w1=cmp_w1[l], cmp_w2=cmp_w2[l],
                                  cmp_pe=cmp_pe[l])
        xs, st = _layer(xs, c_sample, pos_s, mix_s, w_ada[l], b_ada[l], norm1_g[l], w_in[l],
                        w_br_nsa[l], w_br_dil[l], w_out[l], norm2_g[l], w_gate[l], w_up[l], w_down[l])
        s_states.append(st)
    y_prompt = _rmsnorm(xp, normf_g)
    y_sample = _rmsnorm(xs, normf_g)
    p_cmp, p_sel, p_win, p_dil1, p_dil2, p_dil3 = [jnp.stack(a) for a in zip(*p_states)]
    s_cmp, s_sel, s_win, s_dil1, s_dil2, s_dil3 = [jnp.stack(a) for a in zip(*s_states)]
    return (y_prompt, y_sample, p_cmp, p_sel, p_win, p_dil1, p_dil2, p_dil3,
            s_cmp, s_sel, s_win, s_dil1, s_dil2, s_dil3)


_drawn_inputs = setup_inputs


def setup_inputs(seed=0):
    import zlib

    import numpy as np

    out = dict(_drawn_inputs(seed))
    spreads = {}
    factors = {'cache_cmp_kv': 3.433,
     'cache_sel_kv': 3.935,
     'norm1_g': 3.053,
     'norm2_g': 4.192,
     'normf_g': 2.729}
    for name, (base, spread) in spreads.items():
        noise = np.random.default_rng([zlib.crc32(name.encode()), seed]).standard_normal(out[name].shape)
        drawn = base * np.exp(spread * noise) if base else spread * noise
        out[name] = jnp.asarray(drawn.astype(out[name].dtype))
    for name, factor in factors.items():
        out[name] = (out[name] * factor).astype(out[name].dtype)
    return out
```

```python
from contextlib import ExitStack

import numpy as np

import concourse.bass as bass
import concourse.mybir as mybir
from concourse.alu_op_type import AluOpType as ALU

F32 = mybir.dt.float32
I32 = mybir.dt.int32
ACT = mybir.ActivationFunctionType
AX = mybir.AxisListType

P = 128
D = 2048
KT = D // P
TP, B = 256, 8
T = TP + B
QT = TP // P
PAST, PAGE = 2048, 128
NPG = PAST // PAGE
H, KVH, DH = 16, 2, 64
G = H // KVH
BLK, STRIDE, SELB, TOPK = 32, 16, 64, 16
NBP = TP // STRIDE - 1
NBS = PAST // STRIDE - 1
NSEL = PAST // SELB + 1
WIN = 512
DIL = ((128, 1), (512, 4), (2048, 16))
NG, HG, DD = 3, 4, 128
DHEADS = NG * HG
FF = 5632
FT = FF // P
Q_W, KV_W, GATE_W = H * DH, 3 * 2 * KVH * DH, 3 * H
C_KV, C_GATE = Q_W, Q_W + KV_W
C_DIL = C_GATE + GATE_W
C_MERGE = C_DIL + 3 * DHEADS * DD
PROJ_W = C_MERGE + 2 * D
CW = 256
SLOT = KT * CW
NEG = -1e30
SC_N, SC_D = DH ** -0.5, DD ** -0.5
EPS = 1e-6

CONST = {}
S0 = "new_nsa"
_c = 0
for _n, _w in (("ident", P), ("rot_nsa", P), ("rot_dil", P), ("ones", P), ("cos_nsa", T), ("sin_nsa", T),
               ("cos_dil", T), ("sin_dil", T), ("causal", 3 * P), ("dilmask", 9 * P),
               ("cmp_add", QT * NBP), ("cmp_mul", QT * NBP), ("new_nsa", B * B), ("new_dil", B * NG * B),
               ("group", B * H), ("spread", B * H), ("keep", NSEL), ("force", NSEL), ("before", NSEL * NSEL)):
    CONST[_n] = (_c, _w)
    _c += _w
CONST_W = _c
CONST_P = CONST[S0][0]


def constants():
    out = np.zeros((P, CONST_W), np.float32)

    def put(name, a):
        a = np.asarray(a, np.float32).reshape(a.shape[0], -1)
        c, w = CONST[name]
        out[:a.shape[0], c:c + w] = a

    put("ident", np.eye(P))
    put("ones", np.ones((P, P)))
    pos = np.concatenate([np.arange(TP), np.full(B, PAST)]).astype(np.float32)
    for name, dh in (("nsa", DH), ("dil", DD)):
        rd = dh // 4
        half = rd // 2
        inv = np.float32(500000.0) ** (-np.arange(half, dtype=np.float32) * np.float32(2.0 / rd))
        ang = (pos[:, None] * inv[None, :].astype(np.float32)).astype(np.float32)
        rot, cos, sin = np.zeros((P, P)), np.ones((P, T)), np.zeros((P, T))
        for base in range(0, P, dh):
            for i in range(half):
                rot[base + i + half, base + i] = -1
                rot[base + i, base + i + half] = 1
                for r in (base + i, base + i + half):
                    cos[r], sin[r] = np.cos(ang[:, i]), np.sin(ang[:, i])
        put("rot_" + name, rot)
        put("cos_" + name, cos)
        put("sin_" + name, sin)
    q, k = np.arange(TP)[:, None], np.arange(TP)[None, :]
    ok = [k <= q] + [(k <= q) & (q - k <= w) & ((q - k) % d == 0) for w, d in DIL]
    add = [np.where(m, 0.0, NEG) for m in ok]
    put("causal", np.concatenate([add[0][:P, :P], add[0][P:, :]], 1))
    put("dilmask", np.concatenate([m[:P, :P] for m in add[1:]] + [m[P:, :] for m in add[1:]], 1))
    kend = np.arange(NBP) * STRIDE + BLK - 1
    seen = (kend[None, :] <= np.arange(TP)[:, None]).reshape(QT, P, NBP).transpose(1, 0, 2)
    put("cmp_add", np.where(seen, 0.0, NEG))
    put("cmp_mul", seen.astype(np.float32))
    own = np.where(np.eye(B, dtype=bool), 0.0, NEG)
    put("new_nsa", np.broadcast_to(own, (H, B, B)))
    put("new_dil", np.broadcast_to(own[:, None, :], (HG, B, NG, B)))
    group = np.zeros((H, B, B, KVH))
    for h in range(H):
        for b in range(B):
            group[h, b, b, h // G] = 1
    put("group", group)
    put("spread", group.transpose(2, 3, 1, 0).reshape(B * KVH, B, H))
    forced = np.zeros(NSEL)
    forced[[0, NSEL - 2, NSEL - 1]] = 1
    put("keep", np.broadcast_to(1 - forced, (H, NSEL)))
    put("force", np.broadcast_to(forced * 1e6, (H, NSEL)))
    j = np.arange(NSEL)
    put("before", np.broadcast_to(j[None, :] < j[:, None], (H, NSEL, NSEL)))
    return out


class Signal:

    def __init__(self, sem, seen):
        self.sem, self.seen, self.marks, self.n = sem, seen, {}, 0

    def mark(self, *key, by=1):
        self.n += by
        if key:
            assert key not in self.marks, key
            self.marks[key] = self.n
        return self.sem, by

    def at(self, *key):
        if self.seen is None:
            return self.sem, 1
        return self.sem, self.seen[key]

    def last(self):
        return self.sem, self.n


INS = {"x_prompt": (1, TP, D), "x_sample": (B, 1, D), "cache_cmp_kv": (1, 160, PAGE, 2, KVH, DH),
       "cache_sel_kv": (1, 160, PAGE, 2, KVH, DH), "cache_win_kv": (1, B, WIN, 2, KVH, DH),
       "cache_dil1_kv": (1, B, 128, 2, HG, DD), "cache_dil2_kv": (1, B, 512, 2, HG, DD),
       "cache_dil3_kv": (1, B, 2048, 2, HG, DD), "page_table": (B, NPG), "c_prompt": (1, D),
       "c_sample": (B, D), "w_ada": (1, D, 6 * D), "b_ada": (1, 6 * D), "norm1_g": (1, D),
       "w_in": (1, D, PROJ_W), "cmp_w1": (1, 2, BLK, DH, 64), "cmp_w2": (1, 2, 64, DH),
       "cmp_pe": (1, 2, BLK, DH), "w_br_nsa": (1, H * DH, D), "w_br_dil": (1, HG * DD, D),
       "w_out": (1, D, D), "norm2_g": (1, D), "w_gate": (1, D, FF), "w_up": (1, D, FF),
       "w_down": (1, FF, D), "normf_g": (D,)}
NSA_ROW, DIL_ROW = (2, KVH, DH), (2, HG, DD)
OUTS = {"y_prompt": (1, TP, D), "y_sample": (B, 1, D), "p_cmp": (1, 1, TP) + NSA_ROW,
        "p_sel": (1, 1, TP) + NSA_ROW, "p_win": (1, 1, TP) + NSA_ROW, "p_dil1": (1, 1, P) + DIL_ROW,
        "p_dil2": (1, 1, TP) + DIL_ROW, "p_dil3": (1, 1, TP) + DIL_ROW,
        "s_cmp": (1, B, 1) + NSA_ROW, "s_sel": (1, B, 1) + NSA_ROW, "s_win": (1, B, WIN) + NSA_ROW,
        "s_dil1": (1, B, 128) + DIL_ROW, "s_dil2": (1, B, 512) + DIL_ROW, "s_dil3": (1, B, 2048) + DIL_ROW}


def program(nc, i_, o_, ctx, seen):
    signals = {}

    def sem(name):
        return ctx.enter_context(nc.semaphore(name))

    def signal(name):
        signals[name] = Signal(sem(name), None if seen is None else seen[name])
        return signals[name]

    WORDS = 53080
    mem = ctx.enter_context(nc.sbuf_tensor("mem", [P, WORDS], F32))
    top = [0]

    def part(words, at=None):
        a = top[0] if at is None else at
        if at is None:
            top[0] += words
        assert a + words <= WORDS, (a + words, WORDS)
        return mem[:, a:a + words]

    c_all = part(CONST_P)

    def const(name):
        c, w = CONST[name]
        return c_all[:, c:c + w] if c < CONST_P else c_sample[:, c - CONST_P:c - CONST_P + w]

    ident, ones = const("ident"), const("ones")
    biasT = part(96)
    gT = part(3 * KT)
    modT = part(96 * 9).rearrange("p (j c) -> p j c", c=9)
    facA = part(KT * 9).rearrange("p (j c) -> p j c", c=9)
    xT = part(KT * T).rearrange("p (j t) -> p j t", t=T)
    hT = part(KT * T).rearrange("p (j t) -> p j t", t=T)
    rstd = part(T)
    tmp = part(4 * T).rearrange("p (j t) -> p j t", t=T)
    oN = part(8 * T).rearrange("p (j t) -> p j t", t=T)
    oD = part(4 * T).rearrange("p (j t) -> p j t", t=T)
    ring0 = top[0]
    part(3 * SLOT)
    region = top[0]

    def slot(s, k=KT, n=CW):
        a = ring0 + s * SLOT if s < 3 else fourth
        return mem[:, a:a + k * n].rearrange("p (k n) -> p k n", n=n)

    qK = part(G * T).rearrange("p (j t) -> p j t", t=T)
    kT = part(3 * T).rearrange("p (j t) -> p j t", t=T)
    dqk0 = top[0]
    dqk = part(2 * DHEADS * T).rearrange("p (j t) -> p j t", t=T)
    tmN = part(QT * 6 * P).rearrange("p (q j f) -> p q j f", q=QT, j=6)
    tmV0 = top[0]
    tmV = part(QT * DHEADS * P).rearrange("p (q j f) -> p q j f", q=QT, j=DHEADS)
    tmS = part(30 * P).rearrange("p (j f) -> p j f", f=P)
    gates = part(QT * 48).rearrange("p (q j) -> p q j", q=QT)
    gatesS = part(3 * B).rearrange("p (j b) -> p j b", b=B)
    qbd = part(B * H).rearrange("p (b h) -> p b h", h=H)
    qpad = part(B * DHEADS * HG).rearrange("p (b j m) -> p b j m", b=B, m=HG)
    w1p = part(2 * 16 * 64).rearrange("p (s l j e) -> p s l j e", s=2, j=2, e=64)
    w2 = part(2 * 64).rearrange("p (s e) -> p s e", e=64)
    peT = part(32)
    peb = part(2)
    kcP, vcP = part(16), part(P)
    small = part(96)
    at0 = top[0]
    PB = 9 * P - 3 * P + 16
    E = part(2 * PB).rearrange("p (u k) -> p u k", u=2)
    PT = part(PB)
    rt = mem[:, at0 + 1024:at0 + 1024 + 2 * T].rearrange("p (j t) -> p j t", t=T)
    stage = mem[:, at0:at0 + 1024].rearrange("p (u q f) -> p u q f", u=2, q=QT)
    ctop = at0
    cbsh = mem[:, ctop:ctop + 508]
    chid = mem[:, ctop + 508:ctop + 1016]
    cgl = mem[:, ctop + 1016:ctop + 1524]
    flat = tmp.rearrange("p j t -> p (j t)")
    kTcP = flat[:, 0:512].rearrange("p (j n) -> p j n", j=4)
    pairsP = flat[:, 512:1024].rearrange("p (t f) -> p t f", t=1)

    sbase = [dqk0]

    def spart(words):
        a = sbase[0]
        sbase[0] += words
        assert sbase[0] <= tmV0 + QT * DHEADS * P, sbase[0]
        return mem[:, a:a + words]
    kTcS = spart(4096).rearrange("p (j n) -> p j n", j=4)
    KS = kTcS.rearrange("p j n -> p (j n)")
    vcS = spart(B * P).rearrange("p (b f) -> p b f", f=P)
    ptc = spart(B * H).rearrange("p (b h) -> p b h", h=H)
    SS = spart(2576)
    PS_ = spart(22 * H).rearrange("p (j h) -> p j h", h=H)
    pcmp = spart(P)
    kcS = spart(P)
    oS = spart(B * H).rearrange("p (b h) -> p b h", h=H)
    am = spart(B * NSEL).rearrange("p (b j) -> p b j", j=NSEL)
    rk = SS[:, 0:NSEL * NSEL].rearrange("p (j i) -> p j i", i=NSEL)
    c_sample = spart(CONST_W - CONST_P)
    imp = spart(4 * NSEL)
    sel = spart(4 * NSEL).rearrange("p (j i) -> p j i", i=NSEL)
    Ed = mem[:, at0:at0 + 408]
    Pd = mem[:, at0 + 408:at0 + 408 + 24]
    dknew = mem[:, at0 + 1540:at0 + 1540 + 96].rearrange("p (j b) -> p j b", b=B)

    prod = mem[:, region + KT * T:region + (KT + 4) * T].rearrange("p (j t) -> p j t", t=T)
    xs8 = rstd[:, 0:B].unsqueeze(1)
    mT = mem[:, region:region + KT * T].rearrange("p (j t) -> p j t", t=T)
    fT = mem[:, region:region + FT * T].rearrange("p (j t) -> p j t", t=T)
    fourth = region + FT * T
    assert fourth + SLOT <= WORDS
    c_rows = mem[:, region:region + D]
    c_silu = mem[:, region + D:region + 2 * D]
    x_tm = mem[:, region + 2 * D:region + 4 * D].rearrange("p (q f) -> p q f", q=QT)
    x_ts = mem[:, region + 4 * D:region + 5 * D]
    vec_rows = mem[:, region + 5 * D:region + 5 * D + 2 * P].rearrange("p (u f) -> p u f", u=2)
    siluT = mem[:, region + 5 * D + 256:region + 5 * D + 256 + KT * 9].rearrange("p (j c) -> p j c", c=9)
    assert region + 5 * D + 512 <= fourth
    y_tm, y_ts = x_tm, x_ts
    pages = ctx.enter_context(nc.sbuf_tensor("pages", [1, B * NPG], I32))

    bank = [ctx.enter_context(nc.psum_tensor(f"bank{n}", [P, 512], F32)) for n in range(8)]

    const_loaded = sem("const_loaded")
    rows_loaded = sem("rows_loaded")
    loaded = [signal(f"slot{s}_loaded") for s in range(4)]
    pe_, act_, dve_ = signal("pe_step"), signal("act_step"), signal("dve_step")
    outs_stored = signal("outs_stored")
    stage_stored = [signal(f"stage{s}_stored") for s in range(2)]
    cmp_stored, rows_stored = signal("cmp_stored"), signal("rows_stored")
    sample_const = sem("sample_const")
    pairs_loaded = signal("pairs_loaded")
    pages_in = [signal(f"pages{s}_in") for s in range(2)]
    pages_loaded = sem("pages_loaded")
    caches_copied = signal("caches_copied")
    ada_done, ada_kept = sem("ada_done"), sem("ada_kept")
    mg_gate, mg_y, mg_sig, mg_kept = sem("merge_gates"), sem("merge_y"), sem("merge_sigmoids"), sem("merge_kept")
    mg_t = sem("merge_products")
    wo_done, wo_t, wo_kept = sem("wout_done"), sem("wout_products"), sem("wout_kept")
    ff_gate, ff_up, ff_silu, ff_kept = sem("ffn_gate"), sem("ffn_up"), sem("ffn_silu"), sem("ffn_kept")
    dn_used = sem("down_chunks_used")
    dn_done, dn_t, dn_kept = sem("down_done"), sem("down_products"), sem("down_kept")
    w_ld = {ph: [sem(f"{ph}_loaded{s}") for s in range(4)] for ph in ("ada", "merge", "wout", "ffn", "down")}

    w_ada, w_in, w_out = i_["w_ada"][0], i_["w_in"][0], i_["w_out"][0]
    w_gate, w_up, w_down = i_["w_gate"][0], i_["w_up"][0], i_["w_down"][0]
    w_bn, w_bd = i_["w_br_nsa"][0], i_["w_br_dil"][0]

    def rows(w, c, n=CW):
        return w[:, c].rearrange("(k p) n -> p k n", p=P)

    CHUNKS = [(C_GATE, 48)] + [(C_KV + CW * j, CW) for j in range(3)] + [(CW * j, CW) for j in range(4)] \
        + [(C_DIL + CW * j, CW) for j in range(3 * DHEADS // 2)]
    TILES = [("gate", 0)] + [(("k", "v")[j % 2], j // 2) for j in range(6)] + [("q", j) for j in range(8)] \
        + [(k, h) for k in ("dq", "dk", "dv") for h in range(DHEADS)]
    NT = len(TILES)

    def chunk_of(n):
        return 0 if n == 0 else (n + 1) // 2

    ROPED = ("k", "q", "dq", "dk")
    TURNED = ("k", "v", "dk", "dv")

    def made(n):
        return dve_.at("roped", n) if TILES[n][0] in ROPED else act_.at("raw", n)

    LASTN = NT - 1
    UNITS = [("n", qt, h) for h in range(H) for qt in range(QT)] + [("d", qt, h) for h in range(HG) for qt in range(QT)]
    NU = len(UNITS)

    def blocks(u):
        kind, qt, h = UNITS[u]
        W = P * (qt + 1)
        if kind == "n":
            kv = h // G
            out = [(br * W + kb * P, P, tmN[:, kb, 2 * (br + 1) + 1, kv * DH:(kv + 1) * DH])
                   for br in range(2) for kb in range(qt + 1)]
            return out + [(2 * W, NBP, vcP[0:NBP, kv * DH:(kv + 1) * DH])]
        return [(g * W + kb * P, P, tmV[:, kb, g * HG + h, :]) for g in range(NG) for kb in range(qt + 1)]

    block = ctx.enter_context(nc.Block())

    @block.sync
    def _(sp):
        sp.dma_start(c_all, i_["const"][:, 0:CONST_P]).then_inc(const_loaded, 16)
        sp.dma_start(c_rows[0:1, :], i_["c_prompt"]).then_inc(rows_loaded, 16)
        sp.dma_start(c_rows[1:1 + B, :], i_["c_sample"]).then_inc(rows_loaded, 16)
        sp.dma_start(vec_rows[0:96, 0, :], i_["b_ada"][0].rearrange("(j f) -> j f", f=P)).then_inc(rows_loaded, 16)
        for n, v in enumerate((i_["norm1_g"][0], i_["norm2_g"][0], i_["normf_g"])):
            sp.dma_start(vec_rows[KT * n:KT * (n + 1), 1, :], v.rearrange("(j f) -> j f", f=P)).then_inc(rows_loaded, 16)
        sp.dma_start(x_tm, i_["x_prompt"][0].rearrange("(q p) f -> p q f", p=P)).then_inc(rows_loaded, 16)
        sp.dma_start(x_ts[0:B, :], i_["x_sample"].rearrange("b o f -> (b o) f")).then_inc(rows_loaded, 16)

        for s in range(4):
            sp.dma_start(slot(s), rows(w_ada, bass.ds(s * CW, CW))).then_inc(w_ld["ada"][s], 16)
        with sp.Fori(1, 12) as i:
            cols = [sp.snap(i * (4 * CW) + s * CW) for s in range(4)]
            for s in range(4):
                sp.wait_ge(ada_done, i * 4 + (s - 3))
                sp.dma_start(slot(s), rows(w_ada, bass.ds(cols[s], CW))).then_inc(w_ld["ada"][s], 16)
        for c, (col, n) in enumerate(CHUNKS):
            if c < 3:
                sp.wait_ge(ada_done, 45 + c)
            else:
                sp.wait_ge(*pe_.at("chunk", c - 3))
            sp.dma_start(slot(c % 3, KT, n), rows(w_in, slice(col, col + n))).then_inc(*loaded[c % 3].mark("proj", c, by=16))
            if c == 2:
                sp.wait_ge(*dve_.at("x_in"))
                sp.dma_start(pages[:], i_["page_table"].rearrange("(o b) n -> o (b n)", o=1)).then_inc(pages_loaded, 16)
                w1 = i_["cmp_w1"][0].rearrange("s (m l) d e -> (l d) s m e", l=2)
                for s in range(2):
                    for j in range(2):
                        sp.dma_start(w1p[:, s, :, j, :], w1[:, s, 8 * j:8 * j + 8, :]).then_inc(rows_loaded, 16)
                sp.dma_start(w2[0:64], i_["cmp_w2"][0].rearrange("s e d -> e s d")).then_inc(rows_loaded, 16)
                sp.dma_start(peT[:, 0:32], i_["cmp_pe"][0].rearrange("s (m l) d -> (l d) (s m)", l=2),
                             allow_slow_non_contiguous=True).then_inc(rows_loaded, 16)
        sp.wait_ge(*pe_.at("tm", LASTN))
        sp.wait_ge(*cmp_stored.at("p_cmp"))
        for l in range(2):
            sp.dma_start(pairsP[:, 0, :].rearrange("p (j l d) -> p j l d", j=4, l=2)[:, :, l, :],
                         o_["p_cmp"][0, 0].rearrange("(n l) s h d -> n l (s h) d", l=2)[:, l])\
                .then_inc(*pairs_loaded.mark(*(("p",) if l else ()), by=16))
        sp.wait_ge(*dve_.at("sample_q"))
        sp.dma_start(c_sample, i_["const"][:, CONST_P:CONST_W]).then_inc(sample_const, 16)
        for b in range(B):
            if b == 0:
                sp.wait_ge(*pe_.at("chunk", len(CHUNKS) - 1))
            else:
                sp.wait_ge(*pe_.at("pvD", b - 1))
            wd = slot(2).rearrange("p k n -> p (k n)")
            sp.dma_start(wd[:, 0:1024].rearrange("p (t f) -> p t f", t=4),
                         i_["cache_win_kv"][0, b].rearrange("(t p) s h d -> p t (s h d)", p=P))\
                .then_inc(*loaded[2].mark(by=16))
            for g, (w, d) in enumerate(DIL):
                src = i_[f"cache_dil{g + 1}_kv"][0, b].rearrange("(n r) s h d -> n r (s h d)", r=d)[:, 0, :]
                sp.dma_start(wd[:, 1024 * (g + 1):1024 * (g + 2)], src)\
                    .then_inc(*loaded[2].mark(*(("wd", b) if g == 2 else ()), by=16))
        def merge_load(s, col):
            if s < 2:
                sp.dma_start(slot(s), rows(w_in, bass.ds(col, CW))).then_inc(w_ld["merge"][s], 16)
            else:
                sp.dma_start(slot(2)[:, 0:8, :], rows(w_bn, slice(0, CW))).then_inc(w_ld["merge"][2], 16)
                sp.dma_start(slot(2)[:, 8:12, :], rows(w_bd, slice(0, CW))).then_inc(w_ld["merge"][2], 16)
        for s in range(3):
            sp.wait_ge(*(pe_.at("pvD", B - 1) if s == 2 else pe_.at("pvS", B - 2 + s)))
            merge_load(s, (C_MERGE, C_MERGE + D, 0)[s])
        with sp.Fori(1, 8) as i:
            cols = [sp.snap(i * CW + C_MERGE), sp.snap(i * CW + (C_MERGE + D))]
            sp.wait_ge(mg_gate, i * 2 - 1)
            merge_load(0, cols[0])
            sp.wait_ge(mg_gate, i * 2)
            merge_load(1, cols[1])
        for i in range(2):
            for s in range(4):
                if i == 0:
                    if s < 2:
                        sp.wait_ge(mg_gate, 15 + s)
                    elif s == 2:
                        sp.wait_ge(mg_y, 8)
                else:
                    sp.wait_ge(wo_done, s + 1)
                sp.dma_start(slot(s), rows(w_out, slice((4 * i + s) * CW, (4 * i + s + 1) * CW))).then_inc(w_ld["wout"][s], 16)
        for s in range(4):
            sp.wait_ge(wo_done, 5 + s)
            sp.dma_start(slot(s), rows((w_gate, w_up)[s % 2], bass.ds((s // 2) * CW, CW))).then_inc(w_ld["ffn"][s], 16)
        with sp.Fori(1, 11) as i:
            cols = [sp.snap(i * (2 * CW)), sp.snap(i * (2 * CW) + CW)]
            for s in range(4):
                done = (ff_gate, ff_up)[s % 2]
                sp.wait_ge(done, i * 2 + (s // 2 - 1))
                sp.dma_start(slot(s), rows((w_gate, w_up)[s % 2], bass.ds(cols[s // 2], CW)))\
                    .then_inc(w_ld["ffn"][s], 16)
        KD = FT // 4

        def down_load(s, col):
            sp.dma_start(slot(s, KD), w_down[s * KD * P:(s + 1) * KD * P, col].rearrange("(k p) n -> p k n", p=P))\
                .then_inc(w_ld["down"][s], 16)
        for s in range(4):
            sp.wait_ge((ff_gate, ff_up)[s % 2], 21 + s // 2)
            down_load(s, bass.ds(0, CW))
        with sp.Fori(1, 8) as i:
            col = sp.snap(i * CW)
            for s in range(4):
                sp.wait_ge(dn_used, i * 4 + (s - 3))
                down_load(s, bass.ds(col, CW))
        sp.wait_ge(*act_.at("y_out"))
        sp.wait_ge(*dve_.at("y_out"))
        sp.dma_start(o_["y_prompt"][0].rearrange("(q p) f -> p q f", p=P), y_tm).then_inc(*outs_stored.mark(by=16))
        sp.dma_start(o_["y_sample"].rearrange("b o f -> (b o) f"), y_ts[0:B, :]).then_inc(*outs_stored.mark("y", by=16))
        sp.wait_ge(*outs_stored.at("y"))
        sp.wait_ge(*caches_copied.at("all"))
        for s in range(2):
            sp.wait_ge(*stage_stored[s].at("last"))
        sp.wait_ge(*rows_stored.at("all"))

    @block.gpsimd
    def _(pool):
        pool.wait_ge(pages_loaded, 16)

        def gather(cache, b, s, by_pairs):
            flat = cache.rearrange("a n t s h d -> (a n) t (s h d)")
            for n in range(NPG):
                page = pool.value_load(pages[0:1, b * NPG + n:b * NPG + n + 1], min_val=0, max_val=159)
                if by_pairs:
                    src = cache[0].rearrange("n (t l) s h d -> n t l (s h) d", l=2)[bass.ds(page, 1)]
                    dst = slot(s).rearrange("p k n -> p (k n)").rearrange("p (t j l d) -> p t j l d", t=8, j=4, l=2)[
                        64 * (n % 2):64 * (n % 2) + 64, n // 2]
                    for l in range(2):
                        pool.dma_start(dst[:, :, l, :], src[:, :, l].rearrange("o t j d -> (o t) j d"))\
                            .then_inc(*pages_in[s].mark(*(("cmp", b) if (n, l) == (NPG - 1, 1) else ()), by=16))
                else:
                    pool.dma_start(slot(s)[:, n, :], flat[bass.ds(page, 1)].rearrange("o t f -> (o t) f"))\
                        .then_inc(*pages_in[s].mark(*(("sel", b) if n == NPG - 1 else ()), by=16))
        for b in range(B):
            if b < 2:
                pool.wait_ge(*pe_.at("chunk", len(CHUNKS) - 1))
            else:
                pool.wait_ge(*pe_.at("ctr", b - 2, 7))
            gather(i_["cache_cmp_kv"], b, b % 2, True)
            if b == 1:
                for name, n in (("win", WIN), ("dil1", 128), ("dil2", 512), ("dil3", 2048)):
                    src, dst = i_[f"cache_{name}_kv"][0], o_[f"s_{name}"][0]
                    for c in range(B):
                        f = "t s h d -> (t s h d)"
                        a, z = src[c, 1:n].rearrange(f), dst[c, 0:n - 1].rearrange(f)
                        pool.dma_start(z.rearrange("(q n) -> q n", q=16), a.rearrange("(q n) -> q n", q=16))\
                            .then_inc(*caches_copied.mark(*(("all",) if (name, c) == ("dil3", B - 1) else ()), by=16))
        for b in range(B):
            pool.wait_ge(*(pe_.at("ctr", B - 2 + b, 7) if b < 2 else pe_.at("pvS", b - 2)))
            gather(i_["cache_sel_kv"], b, b % 2, False)

    @block.tensor
    def _(pe):
        mm, turn = nc.tensor.matmul, nc.tensor.transpose
        pe.wait_ge(const_loaded, 16)
        pe.wait_ge(rows_loaded, 8 * 16)
        pe.wait_ge(*dve_.at("silu"))
        for k in range(KT):
            last = turn(bank[0][:, 9 * k:9 * k + 9], c_silu[0:9, k * P:(k + 1) * P], ident[0:9, 0:9])
        last.then_inc(*pe_.mark("siluT"))
        turn(bank[1][:, 0:96], vec_rows[0:96, 0, :], ident[0:96, 0:96])
        turn(bank[1][:, 96:144], vec_rows[0:48, 1, :], ident[0:48, 0:48]).then_inc(*pe_.mark("vecT"))
        for k in range(KT):
            if k >= 4:
                pe.wait_ge(*(dve_ if k % 2 else act_).at("xT", k - 4))
            z = bank[2 + k % 4]
            for q in range(QT):
                turn(z[:, q * P:(q + 1) * P], x_tm[:, q, k * P:(k + 1) * P], ident)
            turn(z[:, TP:T], x_ts[0:B, k * P:(k + 1) * P], ident[0:B, 0:B]).then_inc(*pe_.mark("xT", k))
        pe.wait_ge(*act_.at("siluT"))
        pe.wait_ge(*dve_.at("vecT"))
        pe.wait_ge(*dve_.at("xT", KT - 1))
        pe.wait_ge(*act_.at("xT", KT - 2))

        def ada(i, s, first):
            pe.wait_ge(w_ld["ada"][s], i * 16 + 16)
            if not first:
                pe.wait_ge(ada_kept, i * 4 + (s - 3))
            for f in range(2):
                for k in range(KT):
                    last = mm(bank[s][:, 16 * f:16 * f + 9], slot(s)[:, k, f * P:(f + 1) * P], siluT[:, k, :],
                              start=(k == 0), stop=(k == KT - 1))
            last.then_inc(ada_done, 1)
        for s in range(4):
            ada(0, s, True)
        with pe.Fori(1, 12) as i:
            for s in range(4):
                ada(i, s, False)

        def stats(tag):
            for k in range(KT):
                pe.wait_ge(*dve_.at("sq", tag, k))
                last = mm(bank[7][:, 0:T], ones, tmp[:, k % 4, :], start=(k == 0), stop=(k == KT - 1))
                last.then_inc(*pe_.mark("sq", tag, k))
        stats("n1")

        pe.wait_ge(*act_.at("h", "n1"))
        pe.wait_ge(*dve_.at("h", "n1"))

        def rope(n):
            kind = TILES[n][0]
            if kind not in ROPED:
                return
            pe.wait_ge(*act_.at("raw", n))
            if n >= 2:
                pe.wait_ge(*dve_.at("rope_bank", n))
            mm(bank[4 + n % 2][:, 0:T], const("rot_nsa" if kind in "kq" else "rot_dil"), tmp[:, n % 3, :],
               start=True, stop=True).then_inc(*pe_.mark("rot", n))

        def source(n):
            kind, j = TILES[n]
            return {"k": lambda: kT[:, j, :], "dk": lambda: dqk[:, DHEADS + j, :]}.get(kind, lambda: tmp[:, n % 3, :])()

        def token_major(n):
            kind = TILES[n][0]
            if kind not in TURNED:
                return
            pe.wait_ge(*made(n))
            pe.wait_ge(*act_.at("tm_bank", n))
            for q in range(QT):
                turn(bank[6 + n % 2][:, q * P:(q + 1) * P], source(n)[:, q * P:(q + 1) * P], ident)
            turn(bank[6 + n % 2][0:B, TP:TP + P], source(n)[:, TP:T], ident).then_inc(*pe_.mark("tm", n))

        for n in range(NT + 2):
            if n < NT:
                kind = TILES[n][0]
                c = chunk_of(n)
                w = CHUNKS[c][1]
                f = 0 if n == 0 else (n + 1) % 2
                m = 48 if n == 0 else P
                pe.wait_ge(*loaded[c % 3].at("proj", c))
                if n >= 4:
                    pe.wait_ge(*act_.at("raw", n - 4))
                for k in range(KT):
                    last = mm(bank[n % 4][0:m, 0:T], slot(c % 3, KT, w)[:, k, f * P:f * P + m], hT[:, k, :],
                              start=(k == 0), stop=(k == KT - 1))
                last.then_inc(*pe_.mark("acc", n))
                if n == 0 or f == 1:
                    pe_.marks["chunk", c] = pe_.n
            if n == 1:
                pe.wait_ge(*act_.at("raw", 0))
                for q in range(QT):
                    turn(bank[6][:, q * 48:(q + 1) * 48], tmp[0:48, 0, q * P:(q + 1) * P], ident[0:48, 0:48])
                turn(bank[6][0:B, 128:176], tmp[0:48, 0, TP:T], ident[0:48, 0:48]).then_inc(*pe_.mark("gateT"))
                pe.wait_ge(*act_.at("gateS"))
                for br in range(3):
                    last = turn(bank[7][0:H, br * B:(br + 1) * B], small[0:B, br * H:(br + 1) * H], ident[0:B, 0:B])
                last.then_inc(*pe_.mark("gateS"))
            if 1 <= n <= NT:
                rope(n - 1)
            if n >= 2:
                token_major(n - 2)

        def compress_turns(tag, pairs, kTc, nt):
            for sh in range(4):
                for half in range(max(1, nt // 4)):
                    i = sh * max(1, nt // 4) + half
                    for t in range(min(nt, 4)):
                        tt = half * 4 + t
                        src = pairs[:, tt, sh * P:(sh + 1) * P]
                        if t == 0:
                            e = (act_, dve_)[i % 2]
                            if i >= 2:
                                pe.wait_ge(*e.at("ctr", tag, i - 2))
                        last = turn(bank[4 + i % 2][:, t * P:(t + 1) * P], src, ident)
                    last.then_inc(*pe_.mark("ctr", tag, i))

        def compress(tag, kTc, nt):
            n_chunk = nt * 16
            nb = n_chunk - 1
            per = max(1, nt // 4)
            for sh in range(4):
                for i in range(sh * per, (sh + 1) * per):
                    pe.wait_ge(*(act_, dve_)[i % 2].at("ctr", tag, i))
                for l in range(8):
                    last = mm(bank[0][:, sh * P:sh * P + n_chunk],
                              w1p[:, sh // 2, l, :, :].rearrange("p j e -> p (j e)"), kTc[:, sh, 0:nt * P].rearrange("p (n l) -> p l n", l=8)[:, l, :],
                              start=(l == 0), stop=(l == 7))
            last.then_inc(*pe_.mark("hid", tag))
            pe.wait_ge(*act_.at("gelu", tag))
            gl = cgl[0:64].rearrange("p (j n) -> p j n", j=4)
            for h in range(2):
                mm(bank[1][h * 64:(h + 1) * 64, 0:nb], w2[0:64, 0, :], gl[:, h, 0:nb], start=True, stop=True)
            for h in range(2):
                last = mm(bank[2][0:nb, h * 64:(h + 1) * 64], gl[:, 2 + h, 0:nb], w2[0:64, 1, :], start=True, stop=True)
            last.then_inc(*pe_.mark("kvc", tag))

        pe.wait_ge(rows_loaded, 14 * 16)
        for s in range(2):
            for m in range(16):
                last = mm(bank[3][0:64, s:s + 1], w1p[:, s, m % 8, m // 8, :], peT[:, s * 16 + m:s * 16 + m + 1],
                          start=(m == 0), stop=(m == 15))
        last.then_inc(*pe_.mark("pe"))
        pe.wait_ge(*pairs_loaded.at("p"))
        pe.wait_ge(*act_.at("raw", LASTN))
        pe.wait_ge(*dve_.at("roped", NT - DHEADS - 1))
        compress_turns("p", pairsP, kTcP, 1)
        compress("p", kTcP, 1)

        def scores(u):
            kind, qt, h = UNITS[u]
            W = P * (qt + 1)
            if u >= 1:
                pe.wait_ge(*dve_.at("max", u - 1))
            if kind == "n":
                kv, g = h // G, h % G
                r = slice(kv * DH, (kv + 1) * DH)
                q = qK[r, g, qt * P:(qt + 1) * P]
                for br in range(2):
                    mm(bank[0][:, br * W:(br + 1) * W], q, kT[r, br + 1, 0:W], start=True, stop=True)
                mm(bank[1][:, 0:NBP], q, kcP[r, 0:NBP], start=True, stop=True).then_inc(*pe_.mark("s", u))
            else:
                for g in range(NG):
                    z = bank[0][:, g * W:(g + 1) * W] if g < 2 else bank[1][:, 0:W]
                    last = mm(z, dqk[:, g * HG + h, qt * P:(qt + 1) * P], dqk[:, DHEADS + g * HG + h, 0:W], start=True, stop=True)
                last.then_inc(*pe_.mark("s", u))

        def probs(u):
            pe.wait_ge(*dve_.at("p", u))
            if u >= 1:
                pe.wait_ge(*act_.at("pt", u - 1))
            for n, (c, k, _) in enumerate(blocks(u)):
                last = turn(bank[2 + n // 4][0:k, (n % 4) * P:(n % 4 + 1) * P], E[:, u % 2, c:c + k], ident)
            last.then_inc(*pe_.mark("pt", u))

        def pv(u):
            kind, qt, h = UNITS[u]
            pe.wait_ge(*act_.at("pt", u))
            if u >= 2:
                pe.wait_ge(*act_.at("o", u - 2))
            z = bank[4 + u % 2]
            out = z[(h % 2) * DH:(h % 2 + 1) * DH, 0:P] if kind == "n" else z[:, 0:P]
            bl = blocks(u)
            for n, (c, k, v) in enumerate(bl):
                last = mm(out, v, PT[0:k, n * P:(n + 1) * P], start=(n == 0), stop=(n == len(bl) - 1))
            last.then_inc(*pe_.mark("pv", u))

        pe.wait_ge(*act_.at("kvc", "p"))
        pe.wait_ge(*dve_.at("kvc", "p"))
        pe.wait_ge(*act_.at("tm", LASTN))
        for u in range(NU + 2):
            if u < NU:
                scores(u)
            if 1 <= u <= NU:
                probs(u - 1)
            if u >= 2:
                pv(u - 2)

        pe.wait_ge(sample_const, 16)
        pe.wait_ge(*act_.at("o", NU - 1))
        pe.wait_ge(*dve_.at("sample_q"))
        for b in range(B):
            s = b % 2
            pe.wait_ge(*pages_in[s].at("cmp", b))
            pairs = slot(s).rearrange("p k n -> p (k n)").rearrange("p (t f) -> p t f", t=8)
            if b >= 1:
                pe.wait_ge(*dve_.at("hid", b - 1))
            compress_turns(b, pairs, kTcS, 8)
            compress(b, kTcS, 8)
            pe.wait_ge(*act_.at("kvc", b))
            mm(bank[3][0:H, 0:NBS], qbd[:, b, :], kcS[:, 0:NBS], start=True, stop=True).then_inc(*pe_.mark("cs", b))
            pe.wait_ge(*dve_.at("cp", b))
            mm(bank[7][0:H, 0:NBS], const("group").rearrange("p (b r) -> p b r", b=B)[0:H, b, :], pcmp[0:H, 0:NBS],
               start=(b == 0), stop=(b == B - 1)).then_inc(*pe_.mark("imp", b))
            pe.wait_ge(*dve_.at("cpg", b))
            turn(bank[6][0:NBS, 0:H], pcmp[0:H, 0:NBS], ident[0:H, 0:H]).then_inc(*pe_.mark("cpt", b))
        pe.wait_ge(*dve_.at("sel"))
        for b in range(B):
            last = mm(bank[3][0:H, b * NSEL:(b + 1) * NSEL], const("spread").rearrange("p (b h) -> p b h", b=B)[0:H, b, :],
                      sel[0:H, 0, :], start=True, stop=True)
        last.then_inc(*pe_.mark("spread"))
        pe.wait_ge(*dve_.at("am"))

        for b in range(B):
            s = b % 2
            ks = slot(s)
            wd = slot(2).rearrange("p k n -> p (k n)")
            win = wd[:, 0:1024].rearrange("p (t f) -> p t f", t=4)
            dil = wd[:, 1024:4096].rearrange("p (g s h d) -> p g s h d", g=NG, s=2, h=HG)
            pe.wait_ge(*pages_in[s].at("sel", b))
            pe.wait_ge(*loaded[2].at("wd", b))
            for i in range(5):
                if i >= 2:
                    pe.wait_ge(*(act_, dve_)[i % 2].at("kt", b, i - 2))
                for t in range(4):
                    src = ks[:, 4 * i + t, 0:P] if i < 4 else win[:, t, 0:P]
                    last = turn(bank[4 + i % 2][:, t * P:(t + 1) * P], src, ident)
                last.then_inc(*pe_.mark("kt", b, i))
            for i in range(5):
                pe.wait_ge(*(act_, dve_)[i % 2].at("kt", b, i))
                if i == 4:
                    pe.wait_ge(*dve_.at("smax", b, 0))
                mm(bank[i % 4][0:H, :], qbd[:, b, :], KS[:, i * 512:(i + 1) * 512], start=True, stop=True)\
                    .then_inc(*pe_.mark("ss", b, i))
            for br in range(2):
                last = mm(bank[6][0:H, br * B:(br + 1) * B], qbd[:, b, :], kT[:, br + 1, TP:T], start=True, stop=True)
            last.then_inc(*pe_.mark("snew", b))
            pe.wait_ge(*dve_.at("sp", b))
            for t in range(20):
                c = t * P if t < 16 else 2056 + (t - 16) * P
                turn(bank[6][:, 16 + t * H:16 + (t + 1) * H], SS[0:H, c:c + P], ident[0:H, 0:H])
            for br, c in enumerate((2048, 2568)):
                last = turn(bank[6][0:B, 16 + (20 + br) * H:16 + (21 + br) * H], SS[0:H, c:c + B], ident[0:H, 0:H])
            last.then_inc(*pe_.mark("spt", b))
            pe.wait_ge(*act_.at("spt", b))
            for t in range(20):
                v = ks[:, t, P:2 * P] if t < 16 else win[:, t - 16, P:2 * P]
                mm(bank[7][:, 0:H], v, PS_[:, t, :], start=(t == 0), stop=False)
            for br in range(2):
                mm(bank[7][:, 0:H], tmS[0:B, 2 * (br + 1) + 1, :], PS_[0:B, 20 + br, :], start=False, stop=False)
            mm(bank[7][:, 0:H], vcS[0:NBS, b, :], ptc[0:NBS, b, :], start=False, stop=True).then_inc(*pe_.mark("pvS", b))
            for g in range(NG):
                pe.wait_ge(*(act_.at("kt", b, 4) if g == 0 else dve_.at("kt", b, 3) if g == 1 else act_.at("dt", b, 0)))
                for h in range(HG):
                    last = turn(bank[4 + g % 2][:, h * P:(h + 1) * P], dil[:, g, 0, h, :], ident)
                last.then_inc(*pe_.mark("dt", b, g))
            for g in range(NG):
                pe.wait_ge(*(act_, dve_)[g % 2].at("dt", b, g))
                for h in range(HG):
                    mm(bank[0][0:HG, g * P:(g + 1) * P], qpad[:, b, g * HG + h, :],
                       KS[:, (g * HG + h) * P:(g * HG + h + 1) * P], start=(h == 0), stop=(h == HG - 1))
                for h in range(HG):
                    last = mm(bank[0][0:HG, 384 + g * B:384 + (g + 1) * B], qpad[:, b, g * HG + h, :],
                              dknew[:, g * HG + h, :], start=(h == 0), stop=(h == HG - 1))
            last.then_inc(*pe_.mark("ds", b))
            pe.wait_ge(*dve_.at("dp", b))
            for g in range(NG):
                turn(bank[1][:, g * HG:(g + 1) * HG], Ed[0:HG, g * P:(g + 1) * P], ident[0:HG, 0:HG])
            for g in range(NG):
                last = turn(bank[1][0:B, 12 + g * HG:12 + (g + 1) * HG], Ed[0:HG, 384 + g * B:384 + (g + 1) * B], ident[0:HG, 0:HG])
            last.then_inc(*pe_.mark("dpt", b))
            pe.wait_ge(*act_.at("dpt", b))
            for h in range(HG):
                for g in range(NG):
                    mm(bank[2][:, h:h + 1], dil[:, g, 1, h, :], Pd[:, g * HG + h:g * HG + h + 1], start=(g == 0), stop=False)
                    last = mm(bank[2][:, h:h + 1], tmS[0:B, 6 + DHEADS + g * HG + h, :], Pd[0:B, 12 + g * HG + h:13 + g * HG + h],
                              start=False, stop=(g == NG - 1))
            last.then_inc(*pe_.mark("pvD", b))

        pe.wait_ge(*act_.at("oN"))
        pe.wait_ge(*act_.at("oD", B - 1))

        def merge(i, first):
            for s in range(2):
                pe.wait_ge(w_ld["merge"][s], i * 16 + 16)
                if not first:
                    pe.wait_ge(mg_sig, i * 4 + (2 * s - 2))
                for f in range(2):
                    for k in range(KT):
                        last = mm(bank[4 * f + s][:, 0:T], slot(s)[:, k, f * P:(f + 1) * P], hT[:, k, :],
                                  start=(k == 0), stop=(k == KT - 1))
                last.then_inc(mg_gate, 1)
            pe.wait_ge(w_ld["merge"][2], i * 32 + 32)
            if not first:
                pe.wait_ge(mg_t, i * 4)
            for f in range(2):
                for k in range(8):
                    mm(bank[4 * f + 2][:, 0:T], slot(2)[:, k, f * P:(f + 1) * P], oN[:, k, :], start=(k == 0), stop=(k == 7))
                for k in range(4):
                    last = mm(bank[4 * f + 3][:, 0:T], slot(2)[:, 8 + k, f * P:(f + 1) * P], oD[:, k, :],
                              start=(k == 0), stop=(k == 3))
            last.then_inc(mg_y, 1)
        merge(0, True)
        with pe.Fori(1, 8) as i:
            merge(i, False)
        pe.wait_ge(mg_kept, 16)
        pe.wait_ge(mg_sig, 32)
        for i in range(2):
            for s in range(4):
                pe.wait_ge(w_ld["wout"][s], 16 * i + 16)
                if i:
                    pe.wait_ge(wo_kept, 2 * (s + 1))
                for f in range(2):
                    for k in range(KT):
                        last = mm(bank[2 * s + f][:, 0:T], slot(s)[:, k, f * P:(f + 1) * P], mT[:, k, :],
                                  start=(k == 0), stop=(k == KT - 1))
                last.then_inc(wo_done, 1)
        pe.wait_ge(wo_kept, 16)
        stats("n2")
        pe.wait_ge(*act_.at("h", "n2"))
        pe.wait_ge(*dve_.at("h", "n2"))

        def ffn(i, first):
            for s in range(4):
                pe.wait_ge(w_ld["ffn"][s], i * 16 + 16)
                if not first:
                    if s % 2:
                        pe.wait_ge(ff_kept, i * 4 + (s - 3))
                    else:
                        pe.wait_ge(ff_silu, i * 4 + (s - 2))
                for f in range(2):
                    for k in range(KT):
                        last = mm(bank[2 * s + f][:, 0:T], slot(s)[:, k, f * P:(f + 1) * P], hT[:, k, :],
                                  start=(k == 0), stop=(k == KT - 1))
                last.then_inc((ff_gate, ff_up)[s % 2], 1)
        ffn(0, True)
        with pe.Fori(1, 11) as i:
            ffn(i, False)

        def down(i, u, first):
            for s in range(4):
                pe.wait_ge(w_ld["down"][s], i * 32 + (16 * u + 16))
                if s == 0 and not first:
                    pe.wait_ge(dn_kept, i * 4 + (2 * u - 2))
                for f in range(2):
                    for k in range(FT // 4):
                        last = mm(bank[2 * u + f][:, 0:T], slot(s, FT // 4)[:, k, f * P:(f + 1) * P], fT[:, s * (FT // 4) + k, :],
                                  start=(s == 0 and k == 0), stop=(s == 3 and k == FT // 4 - 1))
                last.then_inc(dn_used, 1)
        pe.wait_ge(ff_kept, 44)
        down(0, 0, True)
        down(0, 1, True)
        with pe.Fori(1, 4) as i:
            down(i, 0, False)
            down(i, 1, False)
        pe.wait_ge(dn_kept, 16)
        stats("nf")
        for k in range(KT):
            pe.wait_ge(*dve_.at("yT", k))
            if k >= 4:
                pe.wait_ge(*(dve_ if k % 2 else act_).at("y", k - 4))
            z = bank[k % 4]
            for q in range(QT):
                turn(z[:, q * P:(q + 1) * P], hT[:, k, q * P:(q + 1) * P], ident)
            turn(z[0:B, TP:TP + P], hT[:, k, TP:T], ident).then_inc(*pe_.mark("y", k))

    @block.scalar
    def _(act):
        A, cp = nc.scalar.activation, nc.scalar.copy
        act.wait_ge(rows_loaded, 8 * 16)
        A(c_silu[0:9, :], c_rows[0:9, :], ACT.Sigmoid).then_inc(*act_.mark("sig"))
        act.wait_ge(*pe_.at("siluT"))
        cp(siluT.rearrange("p j c -> p (j c)"), bank[0][:, 0:KT * 9]).then_inc(*act_.mark("siluT"))
        for k in range(0, KT, 2):
            act.wait_ge(*pe_.at("xT", k))
            cp(xT[:, k, :], bank[2 + k % 4][:, 0:T]).then_inc(*act_.mark("xT", k))

        def norm(tag, gate):
            act.wait_ge(*dve_.at("ms", tag))
            A(rstd, rstd, ACT.Sqrt).then_inc(*act_.mark("root", tag))
            if gate is None:
                return
            for k in range(KT):
                act.wait_ge(*dve_.at("hs", tag, k))
                A(hT[:, k, 0:TP], hT[:, k, 0:TP], ACT.Identity, bias=modT[:, gate * KT + k, 0:1])\
                    .then_inc(*act_.mark(*(("h", tag) if k == KT - 1 else ("h", tag, k))))
        norm("n1", 0)

        tiles = dict(enumerate(TILES))
        stores = [0, 0]

        def tm(n):
            kind, j = TILES[n]
            if kind not in TURNED:
                return
            act.wait_ge(*pe_.at("tm", n))
            z = bank[6 + n % 2]
            zq = z[:, 0:TP].rearrange("p (q f) -> p q f", q=QT)
            if kind in "kv":
                dst, row = tmN[:, :, 2 * j + (kind == "v"), :], 2 * j + (kind == "v")
            elif kind == "dv":
                dst, row = tmV[:, :, j, :], 6 + DHEADS + j
            else:
                u = (j // 2) % 2
                if j >= 4 and j % 2 == 0:
                    act.wait_ge(*stage_stored[u].last())
                dst, row = stage[:, u, :, (j % 2) * P:(j % 2 + 1) * P], 6 + j
            cp(dst, zq).then_inc(*act_.mark())
            cp(tmS[0:B, row, :], z[0:B, TP:TP + P]).then_inc(*act_.mark("tm", n))
            if kind == "dk" and j % 2:
                u, g, hh = (j // 2) % 2, j // HG, (j % HG) - 1
                act.wait_ge(*act_.last())
                o = o_[f"p_dil{g + 1}"][0, 0]
                if g == 0:
                    act.dma_start(o[:, 0, hh:hh + 2, :].rearrange("t h d -> t (h d)"), stage[:, u, 1, :])\
                        .then_inc(*stage_stored[u].mark(by=16))
                else:
                    act.dma_start(o[:, 0, hh:hh + 2, :].rearrange("(q p) h d -> p q (h d)", p=P), stage[:, u, :, :])\
                        .then_inc(*stage_stored[u].mark(*(("last",) if j >= DHEADS - 4 else ()), by=16))
            if kind == "v":
                act.wait_ge(*act_.last())
                name = ("cmp", "sel", "win")[j]
                act.dma_start(o_["p_" + name][0, 0].rearrange("(q p) s h d -> p q (s h d)", p=P),
                              tmN[:, :, 2 * j:2 * j + 2, :].rearrange("p q j f -> p q (j f)"))\
                    .then_inc(*(cmp_stored.mark("p_cmp", by=16) if j == 0 else rows_stored.mark(by=16)))
                dst = o_["s_" + name][0, :, 0] if j < 2 else o_["s_win"][0, :, WIN - 1]
                act.dma_start(dst.rearrange("b s h d -> b (s h d)"),
                              tmS[0:B, 2 * j:2 * j + 2, :].rearrange("p j f -> p (j f)")).then_inc(*rows_stored.mark(by=16))
            if kind == "dv" and j % HG == HG - 1:
                g = j // HG
                act.wait_ge(*act_.last())
                o = o_[f"p_dil{g + 1}"][0, 0, :, 1]
                if g == 0:
                    act.dma_start(o.rearrange("t h d -> t (h d)"), tmV[:, 1, 0:HG, :].rearrange("p j f -> p (j f)"))\
                        .then_inc(*rows_stored.mark(by=16))
                else:
                    act.dma_start(o.rearrange("(q p) h d -> p q (h d)", p=P),
                                  tmV[:, :, g * HG:(g + 1) * HG, :].rearrange("p q j f -> p q (j f)"))\
                        .then_inc(*rows_stored.mark(by=16))
                for kv in range(2):
                    r = 6 + kv * DHEADS + g * HG
                    act.dma_start(o_[f"s_dil{g + 1}"][0, :, DIL[g][0] - 1, kv].rearrange("b h d -> b (h d)"),
                                  tmS[0:B, r:r + HG, :].rearrange("p j f -> p (j f)"))\
                        .then_inc(*rows_stored.mark(*(("all",) if (g, kv) == (NG - 1, 1) else ()), by=16))

        for n in range(NT + 2):
            if n < NT:
                act.wait_ge(*pe_.at("acc", n))
                if n >= 3:
                    kind = TILES[n - 3][0]
                    if kind in ROPED:
                        act.wait_ge(*dve_.at("roped", n - 3))
                    elif kind in ("v", "dv"):
                        act.wait_ge(*pe_.at("tm", n - 3))
                    else:
                        act.wait_ge(*pe_.at("gateT"))
                m = 48 if n == 0 else P
                cp(tmp[0:m, n % 3, :], bank[n % 4][0:m, 0:T]).then_inc(*act_.mark("raw", n))
            if n == 1:
                act.wait_ge(*pe_.at("gateT"))
                A(gates.rearrange("p q j -> p (q j)"), bank[6][:, 0:96], ACT.Sigmoid).then_inc(*act_.mark())
                A(small[0:B, 0:48], bank[6][0:B, 128:176], ACT.Sigmoid).then_inc(*act_.mark("gateS"))
                act.wait_ge(*pe_.at("gateS"))
                cp(gatesS[0:H].rearrange("p j b -> p (j b)"), bank[7][0:H, 0:24]).then_inc(*act_.mark("gates"))
            if n >= 2:
                tm(n - 2)
        used = {}
        for n in range(NT):
            if TILES[n][0] in TURNED:
                act_.marks["tm_bank", n] = act_.marks[used.get(n % 2, ("gates",))]
                used[n % 2] = ("tm", n)

        def compress(tag, kTc, nt, kc):
            per = max(1, nt // 4)
            for i in range(0, 4 * per, 2):
                act.wait_ge(*pe_.at("ctr", tag, i))
                w = min(nt, 4) * P
                sh, half = i // per, i % per
                cp(kTc[:, sh, half * 512:half * 512 + w], bank[4 + i % 2][:, 0:w]).then_inc(*act_.mark("ctr", tag, i))
            nb = nt * 16 - 1
            act.wait_ge(*pe_.at("hid", tag))
            cp(cbsh[0:64].rearrange("p (j n) -> p j n", j=4)[:, :, 0:nb],
               bank[0][64:128, :].rearrange("p (j n) -> p j n", j=4)[:, :, 1:nb + 1]).then_inc(*act_.mark("bsh", tag))
            act.wait_ge(*dve_.at("hid", tag))
            A(cgl[0:64].rearrange("p (j n) -> p j n", j=4)[:, :, 0:nb],
              chid[0:64].rearrange("p (j n) -> p j n", j=4)[:, :, 0:nb], ACT.Gelu_apprx_tanh).then_inc(*act_.mark("gelu", tag))
            act.wait_ge(*pe_.at("kvc", tag))
            cp(kc, bank[1][:, 0:nb]).then_inc(*act_.mark("kvc", tag))
        for s in range(2):
            act.wait_ge(*stage_stored[s].last())
        act.wait_ge(*pe_.at("pe"))
        cp(peb[0:64, :], bank[3][0:64, 0:2]).then_inc(*act_.mark("peb"))
        compress("p", kTcP, 1, kcP[:, 0:NBP])

        def pt_copy(u):
            act.wait_ge(*pe_.at("pt", u))
            if u >= 1:
                act.wait_ge(*pe_.at("pv", u - 1))
            bl = blocks(u)
            full = sum(k == P for _, k, _ in bl)
            marks = []
            for c in range(0, full, 4):
                w = min(4, full - c) * P
                marks.append((PT[:, c * P:c * P + w], bank[2 + c // 4][:, 0:w]))
            if full < len(bl):
                n = len(bl) - 1
                marks.append((PT[0:NBP, n * P:(n + 1) * P], bank[2 + n // 4][0:NBP, (n % 4) * P:(n % 4 + 1) * P]))
            for n, (o, s) in enumerate(marks):
                cp(o, s).then_inc(*act_.mark(*(("pt", u) if n == len(marks) - 1 else ())))

        def o_copy(u):
            kind, qt, h = UNITS[u]
            act.wait_ge(*pe_.at("pv", u))
            z = bank[4 + u % 2]
            if kind == "n":
                r = slice((h % 2) * DH, (h % 2 + 1) * DH)
                cp(oN[r, h // 2, qt * P:(qt + 1) * P], z[r, 0:P]).then_inc(*act_.mark("o", u))
            else:
                cp(oD[:, h, qt * P:(qt + 1) * P], z[:, 0:P]).then_inc(*act_.mark("o", u))

        for u in range(NU + 2):
            if u < NU:
                kind, qt, h = UNITS[u]
                W = P * (qt + 1)
                act.wait_ge(*dve_.at("nm", u))
                e = E[:, u % 2, :]
                if kind == "n":
                    for br in range(3):
                        a, z = (br * W, (br + 1) * W) if br < 2 else (2 * W, 2 * W + NBP)
                        A(e[:, a:z], e[:, a:z], ACT.Exp, bias=small[:, 8 * (u % 2) + br:8 * (u % 2) + br + 1], scale=SC_N,
                          accum_out=small[:, 16 + 8 * (u % 2) + br:17 + 8 * (u % 2) + br])\
                            .then_inc(*act_.mark(*(("e", u) if br == 2 else ())))
                else:
                    A(e[:, 0:3 * W], e[:, 0:3 * W], ACT.Exp, bias=small[:, 8 * (u % 2):8 * (u % 2) + 1], scale=SC_D,
                      accum_out=small[:, 16 + 8 * (u % 2):17 + 8 * (u % 2)]).then_inc(*act_.mark("e", u))
            if 1 <= u <= NU:
                pt_copy(u - 1)
            if u >= 2:
                o_copy(u - 2)

        for b in range(B):
            compress(b, kTcS, 8, kcS[:, 0:NBS])
            act.wait_ge(*dve_.at("cm", b))
            A(pcmp[0:H, 0:NBS], bank[3][0:H, 0:NBS], ACT.Exp, bias=small[0:H, 1:2], scale=SC_N,
              accum_out=small[0:H, 2:3]).then_inc(*act_.mark("ce", b))
            act.wait_ge(*pe_.at("cpt", b))
            cp(ptc[0:NBS, b, :], bank[6][0:NBS, 0:H]).then_inc(*act_.mark("cpt", b))
        for b in range(B):
            for i in (0, 2, 4):
                act.wait_ge(*pe_.at("kt", b, i))
                if i == 0 and b:
                    act.wait_ge(*pe_.at("ds", b - 1))
                cp(KS[:, i * 512:(i + 1) * 512], bank[4 + i % 2][:, :]).then_inc(*act_.mark("kt", b, i))
            act.wait_ge(*dve_.at("sm", b))
            for br, (a, z) in enumerate(((0, 2056), (2056, 2576))):
                A(SS[0:H, a:z], SS[0:H, a:z], ACT.Exp, bias=small[0:H, 10 + br:11 + br], scale=SC_N,
                  accum_out=small[0:H, 12 + br:13 + br]).then_inc(*act_.mark(*(("se", b) if br else ())))
            act.wait_ge(*pe_.at("spt", b))
            cp(PS_[:, 0:20, :].rearrange("p j h -> p (j h)"), bank[6][:, 16:16 + 320]).then_inc(*act_.mark())
            cp(PS_[0:B, 20:22, :].rearrange("p j h -> p (j h)"), bank[6][0:B, 336:368]).then_inc(*act_.mark("spt", b))
            act.wait_ge(*pe_.at("pvS", b))
            cp(oS[:, b, :], bank[7][:, 0:H]).then_inc(*act_.mark("oS", b))
            for g in (0, 2):
                act.wait_ge(*pe_.at("dt", b, g))
                cp(KS[:, g * 512:(g + 1) * 512], bank[4 + g % 2][:, :]).then_inc(*act_.mark("dt", b, g))
            act.wait_ge(*dve_.at("dm", b))
            A(Ed[0:HG, 0:384], bank[0][0:HG, 0:384], ACT.Exp, bias=small[0:HG, 24:25], scale=SC_D,
              accum_out=small[0:HG, 26:27]).then_inc(*act_.mark())
            A(Ed[0:HG, 384:408], Ed[0:HG, 384:408], ACT.Exp, bias=small[0:HG, 24:25], scale=SC_D,
              accum_out=small[0:HG, 27:28]).then_inc(*act_.mark("de", b))
            act.wait_ge(*pe_.at("dpt", b))
            cp(Pd[:, 0:12], bank[1][:, 0:12]).then_inc(*act_.mark())
            cp(Pd[0:B, 12:24], bank[1][0:B, 12:24]).then_inc(*act_.mark("dpt", b))
            act.wait_ge(*pe_.at("pvD", b))
            cp(oD[:, :, TP + b], bank[2][:, 0:HG]).then_inc(*act_.mark("oD", b))
        act.wait_ge(*act_.at("oS", B - 1))
        for kv in range(2):
            for odd in range(2):
                cp(oN[odd * DH:(odd + 1) * DH, kv * 4:kv * 4 + 4, TP:T],
                   oS[kv * DH:(kv + 1) * DH, :, kv * G + odd:(kv + 1) * G:2].rearrange("p b h -> p h b"))\
                    .then_inc(*act_.mark(*(("oN",) if (kv, odd) == (1, 1) else ())))

        def merge(i, first):
            for s in range(2):
                act.wait_ge(mg_gate, i * 2 + (s + 1))
                for f in range(2):
                    if not first and f == 0 and s == 0:
                        act.wait_ge(mg_t, i * 4)
                    A(sig[:, 2 * s + f, :], bank[4 * f + s][:, 0:T], ACT.Sigmoid).then_inc(mg_sig, 1)
                if s == 0 and not first:
                    act.wait_ge(mg_y, i)
                    act.dma_start(slot(2)[:, 0:8, :], rows(w_bn, bass.ds(i * CW, CW))).then_inc(w_ld["merge"][2], 16)
                    act.dma_start(slot(2)[:, 8:12, :], rows(w_bd, bass.ds(i * CW, CW))).then_inc(w_ld["merge"][2], 16)
        sig = tmp
        merge(0, True)
        with act.Fori(1, 8) as i:
            merge(i, False)
        norm("n2", 3)

        def ffn(i, first):
            for s in (0, 2):
                act.wait_ge(ff_gate, i * 2 + (s // 2 + 1))
                for f in range(2):
                    if not first:
                        act.wait_ge(ff_kept, i * 4 + (s + f - 3))
                    A(tmp[:, s + f, :], bank[2 * s + f][:, 0:T], ACT.Silu).then_inc(ff_silu, 1)
        ffn(0, True)
        with act.Fori(1, 11) as i:
            ffn(i, False)
        norm("nf", None)
        for k in range(0, KT, 2):
            act.wait_ge(*pe_.at("y", k))
            z = bank[k % 4]
            cp(y_tm[:, :, k * P:(k + 1) * P], z[:, 0:TP].rearrange("p (q f) -> p q f", q=QT)).then_inc(*act_.mark())
            cp(y_ts[0:B, k * P:(k + 1) * P], z[0:B, TP:TP + P]).then_inc(*act_.mark("y", k))
        act_.marks["y_out",] = act_.n

    @block.vector
    def _(dve):
        v = nc.vector

        def link(ins):
            ins.then_inc(*dve_.mark())
            dve.wait_ge(*dve_.last())

        dve.wait_ge(rows_loaded, 8 * 16)
        dve.wait_ge(*act_.at("sig"))
        v.tensor_tensor(c_silu[0:9, :], c_rows[0:9, :], c_silu[0:9, :], ALU.mult).then_inc(*dve_.mark("silu"))
        dve.wait_ge(*pe_.at("vecT"))
        v.tensor_copy(biasT, bank[1][:, 0:96]).then_inc(*dve_.mark())
        v.tensor_copy(gT, bank[1][:, 96:144]).then_inc(*dve_.mark("vecT"))
        for k in range(1, KT, 2):
            dve.wait_ge(*pe_.at("xT", k))
            v.tensor_copy(xT[:, k, :], bank[2 + k % 4][:, 0:T]).then_inc(*dve_.mark("xT", k))
        dve_.marks["x_in",] = dve_.n
        dve.wait_ge(*dve_.at("vecT"))

        def ada(i, s):
            dve.wait_ge(ada_done, i * 4 + (s + 1))
            v.tensor_tensor(modT[:, bass.ds(i * 8 + 2 * s, 2), :], bank[s][:, 0:32].rearrange("p (f c) -> p f c", f=2)[:, :, 0:9],
                            biasT[:, bass.ds(i * 8 + 2 * s, 2)].unsqueeze(2).broadcast_to([P, 2, 9]), ALU.add).then_inc(ada_kept, 1)
        with dve.Fori(0, 12) as i:
            for s in range(4):
                ada(i, s)
        dve.wait_ge(ada_kept, 48)
        dve.wait_ge(*act_.at("xT", KT - 2))
        dve.wait_ge(*dve_.at("xT", KT - 1))

        def norm(tag, g, shift):
            for k in range(KT):
                if k >= 4:
                    dve.wait_ge(*pe_.at("sq", tag, k - 4))
                v.tensor_tensor(tmp[:, k % 4, :], xT[:, k, :], xT[:, k, :], ALU.mult).then_inc(*dve_.mark("sq", tag, k))
            dve.wait_ge(*pe_.at("sq", tag, KT - 1))
            v.tensor_scalar(rstd, bank[7][:, 0:T], 1.0 / D, EPS, ALU.mult, ALU.add).then_inc(*dve_.mark("ms", tag))
            if shift is not None:
                scale = modT[:, (shift + 1) * KT:(shift + 2) * KT, :]
                link(v.scalar_tensor_tensor(out=facA, in0=scale, scalar=1.0,
                                            in1=gT[:, g * KT:(g + 1) * KT].unsqueeze(2).broadcast_to([P, KT, 9]),
                                            op0=ALU.add, op1=ALU.mult))
            dve.wait_ge(*act_.at("root", tag))
            link(v.reciprocal(rstd, rstd))
            if shift is None:
                for k in range(KT):
                    v.scalar_tensor_tensor(out=hT[:, k, :], in0=xT[:, k, :], scalar=gT[:, g * KT + k:g * KT + k + 1],
                                           in1=rstd, op0=ALU.mult, op1=ALU.mult).then_inc(*dve_.mark("yT", k))
                return
            for k in range(KT):
                v.scalar_tensor_tensor(out=hT[:, k, 0:TP], in0=xT[:, k, 0:TP], scalar=facA[:, k, 0:1],
                                       in1=rstd[:, 0:TP], op0=ALU.mult, op1=ALU.mult).then_inc(*dve_.mark("hs", tag, k))
            hS = hT[:, :, TP:T]
            link(v.tensor_tensor(hS, xT[:, :, TP:T], facA[:, :, 1:9], ALU.mult))
            link(v.tensor_tensor(hS, hS, rstd[:, TP:T].unsqueeze(1).broadcast_to([P, KT, B]), ALU.mult))
            v.tensor_tensor(hS, hS, modT[:, shift * KT:(shift + 1) * KT, 1:9], ALU.add).then_inc(*dve_.mark("h", tag))
        norm("n1", 0, 0)

        roped = []
        for n in range(NT):
            kind, j = TILES[n]
            if kind not in ROPED:
                continue
            c = "nsa" if kind in "kq" else "dil"
            dve.wait_ge(*act_.at("raw", n))
            if roped:
                dve.wait_ge(*dve_.at("roped", roped[-1]))
            v.tensor_tensor(rt[:, 0, :], tmp[:, n % 3, :], const("cos_" + c), ALU.mult).then_inc(*dve_.mark())
            dve.wait_ge(*pe_.at("rot", n))
            link(v.tensor_tensor(rt[:, 1, :], bank[4 + n % 2][:, 0:T], const("sin_" + c), ALU.mult))
            if kind == "q":
                kv = j // 4
                for odd in range(2):
                    r = slice(odd * DH, (odd + 1) * DH)
                    last = v.tensor_tensor(qK[kv * DH:(kv + 1) * DH, (2 * j + odd) % G, :], rt[r, 0, :], rt[r, 1, :], ALU.add)
                    last.then_inc(*dve_.mark(*(("roped", n) if odd else ())))
            else:
                dst = {"k": lambda: kT[:, j, :], "dq": lambda: dqk[:, j, :], "dk": lambda: dqk[:, DHEADS + j, :]}[kind]()
                v.tensor_tensor(dst, rt[:, 0, :], rt[:, 1, :], ALU.add).then_inc(*dve_.mark("roped", n))
            roped.append(n)
        for n in roped:
            before = [m for m in roped if m < n and m % 2 == n % 2]
            dve_.marks["rope_bank", n] = dve_.marks["roped", before[-1]] if before else 1

        def compress(tag, kTc, nt, vc):
            per = max(1, nt // 4)
            for i in range(1, 4 * per, 2):
                dve.wait_ge(*pe_.at("ctr", tag, i))
                w = min(nt, 4) * P
                sh, half = i // per, i % per
                v.tensor_copy(kTc[:, sh, half * 512:half * 512 + w], bank[4 + i % 2][:, 0:w]).then_inc(*dve_.mark("ctr", tag, i))
            nb = nt * 16 - 1
            dve.wait_ge(*act_.at("bsh", tag))
            dve.wait_ge(*act_.at("peb"))
            for s in range(2):
                v.scalar_tensor_tensor(out=chid[0:64].rearrange("p (j n) -> p j n", j=4)[:, 2 * s:2 * s + 2, 0:nb],
                                       in0=bank[0][0:64, :].rearrange("p (j n) -> p j n", j=4)[:, 2 * s:2 * s + 2, 0:nb],
                                       scalar=peb[0:64, s:s + 1],
                                       in1=cbsh[0:64].rearrange("p (j n) -> p j n", j=4)[:, 2 * s:2 * s + 2, 0:nb],
                                       op0=ALU.add, op1=ALU.add).then_inc(*dve_.mark(*(("hid", tag) if s else ())))
            dve.wait_ge(*pe_.at("kvc", tag))
            v.tensor_copy(vc, bank[2][0:nb, 0:P]).then_inc(*dve_.mark("kvc", tag))
        compress("p", kTcP, 1, vcP[0:NBP, :])

        for u in range(NU):
            kind, qt, h = UNITS[u]
            W = P * (qt + 1)
            c = 8 * (u % 2)
            mx, nm, den = small[:, 32:35], small[:, c:c + 3], small[:, 16 + c:19 + c]
            e = E[:, u % 2, :]
            if u == 0:
                dve.wait_ge(*act_.at("kvc", "p"))
            if u >= 2:
                dve.wait_ge(*pe_.at("pt", u - 2))
            dve.wait_ge(*pe_.at("s", u))
            if kind == "n":
                mask = const("causal")[:, 0:P] if qt == 0 else const("causal")[:, P:3 * P]
                for br in range(2):
                    v.tensor_tensor_reduce(e[:, br * W:(br + 1) * W], bank[0][:, br * W:(br + 1) * W], mask, 1.0, -3e38,
                                           ALU.add, ALU.max, mx[:, br:br + 1]).then_inc(*dve_.mark())
                v.tensor_tensor_reduce(e[:, 2 * W:2 * W + NBP], bank[1][:, 0:NBP], const("cmp_add")[:, qt * NBP:(qt + 1) * NBP],
                                       1.0, -3e38, ALU.add, ALU.max, mx[:, 2:3]).then_inc(*dve_.mark("max", u))
                dve.wait_ge(*dve_.last())
                v.tensor_scalar(nm, mx, -SC_N, None, ALU.mult).then_inc(*dve_.mark("nm", u))
                dve.wait_ge(*act_.at("e", u))
                link(v.tensor_tensor_reduce(e[:, 2 * W:2 * W + NBP], e[:, 2 * W:2 * W + NBP],
                                            const("cmp_mul")[:, qt * NBP:(qt + 1) * NBP], 1.0, 0.0, ALU.mult, ALU.add,
                                            den[:, 2:3]))
                link(v.tensor_scalar(den, den, 1e-30, None, ALU.max))
                link(v.reciprocal(den, den))
                g3 = gates[:, qt, :].rearrange("p (r h) -> p r h", h=H)[:, :, h]
                v.tensor_tensor(den[:, 0:2], den[:, 0:2], g3[:, 1:3], ALU.mult).then_inc(*dve_.mark())
                link(v.tensor_tensor(den[:, 2:3], den[:, 2:3], g3[:, 0:1], ALU.mult))
                for br in range(3):
                    a, z = (br * W, (br + 1) * W) if br < 2 else (2 * W, 2 * W + NBP)
                    v.tensor_scalar(e[:, a:z], e[:, a:z], den[:, br:br + 1], None, ALU.mult)\
                        .then_inc(*dve_.mark(*(("p", u) if br == 2 else ())))
            else:
                mask = const("dilmask")[:, 0:3 * P] if qt == 0 else const("dilmask")[:, 3 * P:9 * P]
                v.tensor_tensor_reduce(e[:, 0:2 * W], bank[0][:, 0:2 * W], mask[:, 0:2 * W], 1.0, -3e38, ALU.add, ALU.max,
                                       mx[:, 0:1]).then_inc(*dve_.mark())
                v.tensor_tensor_reduce(e[:, 2 * W:3 * W], bank[1][:, 0:W], mask[:, 2 * W:3 * W], 1.0, -3e38, ALU.add, ALU.max,
                                       mx[:, 1:2]).then_inc(*dve_.mark("max", u))
                dve.wait_ge(*dve_.last())
                link(v.tensor_tensor(mx[:, 0:1], mx[:, 0:1], mx[:, 1:2], ALU.max))
                v.tensor_scalar(nm[:, 0:1], mx[:, 0:1], -SC_D, None, ALU.mult).then_inc(*dve_.mark("nm", u))
                dve.wait_ge(*act_.at("e", u))
                link(v.reciprocal(den[:, 0:1], den[:, 0:1]))
                v.tensor_scalar(e[:, 0:3 * W], e[:, 0:3 * W], den[:, 0:1], None, ALU.mult).then_inc(*dve_.mark("p", u))

        dve.wait_ge(*pe_.at("pv", NU - 1))
        dve.wait_ge(*rows_stored.at("all"))
        link(v.memset(qbd, 0.0))
        for kv in range(2):
            r = slice(kv * DH, (kv + 1) * DH)
            v.tensor_copy(qbd[r, :, kv * G:(kv + 1) * G], qK[r, :, TP:T].rearrange("p g b -> p b g")).then_inc(*dve_.mark())
        link(v.memset(qpad, 0.0))
        for h in range(HG):
            v.tensor_copy(qpad[:, :, h:DHEADS:HG, h], dqk[:, h:DHEADS:HG, TP:T].rearrange("p g b -> p b g")).then_inc(*dve_.mark())
        v.tensor_copy(dknew, dqk[:, DHEADS:2 * DHEADS, TP:T]).then_inc(*dve_.mark("sample_q"))
        dve.wait_ge(*dve_.last())
        link(v.memset(imp[0:H, :], 0.0))

        sm = small[0:H]
        dve.wait_ge(sample_const, 16)
        for b in range(B):
            compress(b, kTcS, 8, vcS[0:NBS, b, :])
            dve.wait_ge(*pe_.at("cs", b))
            link(v.tensor_reduce(sm[:, 0:1], bank[3][0:H, 0:NBS], AX.X, ALU.max))
            if b:
                dve.wait_ge(*pe_.at("cpt", b - 1))
            v.tensor_scalar(sm[:, 1:2], sm[:, 0:1], -SC_N, None, ALU.mult).then_inc(*dve_.mark("cm", b))
            dve.wait_ge(*act_.at("ce", b))
            link(v.tensor_scalar(sm[:, 2:3], sm[:, 2:3], 1e-30, None, ALU.max))
            link(v.reciprocal(sm[:, 2:3], sm[:, 2:3]))
            v.tensor_scalar(pcmp[0:H, 0:NBS], pcmp[0:H, 0:NBS], sm[:, 2:3], None, ALU.mult).then_inc(*dve_.mark("cp", b))
            dve.wait_ge(*pe_.at("imp", b))
            v.tensor_scalar(pcmp[0:H, 0:NBS], pcmp[0:H, 0:NBS], gatesS[0:H, 0, b:b + 1], None, ALU.mult).then_inc(*dve_.mark("cpg", b))
        link(v.tensor_copy(imp[0:H, 0:NBS], bank[7][0:H, 0:NBS]))
        sc, rank = sel[0:H, 1, :], sel[0:H, 2, :]
        link(v.tensor_reduce(sc, imp[0:H, :].rearrange("p (j r) -> p j r", r=4), AX.X, ALU.add))
        link(v.tensor_tensor(sel[0:H, 1, 1:NSEL], sel[0:H, 1, 1:NSEL],
                             imp[0:H, :].rearrange("p (j r) -> p j r", r=4)[:, 0:NSEL - 1, 3], ALU.add))
        link(v.tensor_tensor(sc, sc, const("keep")[0:H], ALU.mult))
        link(v.tensor_tensor(sc, sc, const("force")[0:H], ALU.add))
        mine = sc.unsqueeze(2).broadcast_to([H, NSEL, NSEL])
        other = sc.unsqueeze(1).broadcast_to([H, NSEL, NSEL])
        before = const("before")[0:H].rearrange("p (j i) -> p j i", i=NSEL)
        link(v.tensor_tensor(rk[0:H], other, mine, ALU.is_equal))
        link(v.tensor_tensor(rk[0:H], rk[0:H], before, ALU.mult))
        link(v.tensor_reduce(rank, rk[0:H], AX.X, ALU.add))
        link(v.tensor_tensor(rk[0:H], other, mine, ALU.is_gt))
        link(v.tensor_reduce(sel[0:H, 3, :], rk[0:H], AX.X, ALU.add))
        link(v.tensor_tensor(rank, rank, sel[0:H, 3, :], ALU.add))
        v.tensor_scalar(sel[0:H, 0, :], rank, float(TOPK), None, ALU.is_lt).then_inc(*dve_.mark("sel"))
        dve.wait_ge(*pe_.at("spread"))
        v.tensor_scalar(am[0:H].rearrange("p b j -> p (b j)"), bank[3][0:H, 0:B * NSEL], -1.0, -NEG, ALU.add, ALU.mult)\
            .then_inc(*dve_.mark("am"))
        dve.wait_ge(*dve_.last())

        for b in range(B):
            for i in (1, 3):
                dve.wait_ge(*pe_.at("kt", b, i))
                if i == 1 and b:
                    dve.wait_ge(*pe_.at("ds", b - 1))
                v.tensor_copy(KS[:, i * 512:(i + 1) * 512], bank[4 + i % 2][:, :]).then_inc(*dve_.mark("kt", b, i))
            if b:
                dve.wait_ge(*pe_.at("spt", b - 1))
            for i in range(4):
                dve.wait_ge(*pe_.at("ss", b, i))
                mask = am[0:H, b, 8 * i:8 * i + 8].unsqueeze(2).broadcast_to([H, 8, SELB])
                v.tensor_tensor(SS[0:H, i * 512:(i + 1) * 512].rearrange("p (j k) -> p j k", k=SELB),
                                bank[i % 4][0:H, :].rearrange("p (j k) -> p j k", k=SELB), mask, ALU.add)\
                    .then_inc(*dve_.mark("smax", b, i))
            dve.wait_ge(*pe_.at("ss", b, 4))
            v.tensor_copy(SS[0:H, 2056:2568], bank[0][0:H, :]).then_inc(*dve_.mark())
            dve.wait_ge(*pe_.at("snew", b))
            own = const("new_nsa")[0:H].rearrange("p (b k) -> p b k", b=B)[:, b, :]
            for br, c in enumerate((2048, 2568)):
                v.tensor_tensor(SS[0:H, c:c + B], bank[6][0:H, br * B:(br + 1) * B], own, ALU.add).then_inc(*dve_.mark())
            dve.wait_ge(*dve_.last())
            v.tensor_reduce(sm[:, 8:9], SS[0:H, 0:2056], AX.X, ALU.max).then_inc(*dve_.mark())
            link(v.tensor_reduce(sm[:, 9:10], SS[0:H, 2056:2576], AX.X, ALU.max))
            v.tensor_scalar(sm[:, 10:12], sm[:, 8:10], -SC_N, None, ALU.mult).then_inc(*dve_.mark("sm", b))
            dve.wait_ge(*act_.at("se", b))
            link(v.tensor_scalar(sm[:, 12:14], sm[:, 12:14], 1e-30, None, ALU.max))
            link(v.reciprocal(sm[:, 12:14], sm[:, 12:14]))
            link(v.tensor_tensor(sm[:, 12:14], sm[:, 12:14], gatesS[0:H, 1:3, b], ALU.mult))
            v.tensor_scalar(SS[0:H, 0:2056], SS[0:H, 0:2056], sm[:, 12:13], None, ALU.mult).then_inc(*dve_.mark())
            v.tensor_scalar(SS[0:H, 2056:2576], SS[0:H, 2056:2576], sm[:, 13:14], None, ALU.mult).then_inc(*dve_.mark("sp", b))
            dve.wait_ge(*pe_.at("dt", b, 1))
            v.tensor_copy(KS[:, 512:1024], bank[5][:, :]).then_inc(*dve_.mark("dt", b, 1))
            dve.wait_ge(*pe_.at("ds", b))
            if b:
                dve.wait_ge(*pe_.at("dpt", b - 1))
            own = const("new_dil")[0:HG].rearrange("p (b k) -> p b k", b=B)[:, b, :]
            v.tensor_tensor(Ed[0:HG, 384:408], bank[0][0:HG, 384:408], own, ALU.add).then_inc(*dve_.mark())
            link(v.tensor_reduce(small[0:HG, 24:25], bank[0][0:HG, 0:384], AX.X, ALU.max))
            link(v.tensor_reduce(small[0:HG, 25:26], Ed[0:HG, 384:408], AX.X, ALU.max))
            link(v.tensor_tensor(small[0:HG, 24:25], small[0:HG, 24:25], small[0:HG, 25:26], ALU.max))
            v.tensor_scalar(small[0:HG, 24:25], small[0:HG, 24:25], -SC_D, None, ALU.mult).then_inc(*dve_.mark("dm", b))
            dve.wait_ge(*act_.at("de", b))
            link(v.tensor_tensor(small[0:HG, 26:27], small[0:HG, 26:27], small[0:HG, 27:28], ALU.add))
            link(v.reciprocal(small[0:HG, 26:27], small[0:HG, 26:27]))
            v.tensor_scalar(Ed[0:HG, :], Ed[0:HG, :], small[0:HG, 26:27], None, ALU.mult).then_inc(*dve_.mark("dp", b))

        def merge(i):
            dve.wait_ge(mg_y, i + 1)
            dve.wait_ge(mg_sig, i * 4 + 4)
            for f in range(2):
                for s in range(2):
                    v.tensor_tensor(prod[:, 2 * f + s, :], tmp[:, 2 * s + f, :], bank[4 * f + 2 + s][:, 0:T], ALU.mult).then_inc(mg_t, 1)
            dve.wait_ge(mg_t, i * 4 + 4)
            for f in range(2):
                v.tensor_tensor(mT[:, bass.ds(i * 2 + f, 1), :], prod[:, 2 * f, :].unsqueeze(1), prod[:, 2 * f + 1, :].unsqueeze(1),
                                ALU.add).then_inc(mg_kept, 1)
            dve.wait_ge(mg_kept, i * 2 + 2)
        with dve.Fori(0, 8) as i:
            merge(i)

        def residual(j, z, gate, products, n_products, kept):
            one = bass.ds(j, 1)
            v.tensor_tensor(xs8, z[:, TP:T].unsqueeze(1), modT[:, bass.ds(j + gate * KT, 1), 1:9], ALU.mult).then_inc(products, 1)
            v.scalar_tensor_tensor(out=xT[:, one, 0:TP], in0=z[:, 0:TP].unsqueeze(1), scalar=modT[:, bass.ds(j + gate * KT, 1), 0],
                                   in1=xT[:, one, 0:TP], op0=ALU.mult, op1=ALU.add).then_inc(products, 1)
            dve.wait_ge(products, n_products)
            v.tensor_tensor(xT[:, one, TP:T], xT[:, one, TP:T], xs8, ALU.add).then_inc(kept, 1)
        for i in range(2):
            for s in range(4):
                dve.wait_ge(wo_done, 4 * i + s + 1)
                for f in range(2):
                    j = 8 * i + 2 * s + f
                    if j:
                        dve.wait_ge(wo_kept, j)
                    residual(j, bank[2 * s + f], 2, wo_t, 2 * (j + 1), wo_kept)
        dve.wait_ge(wo_kept, 16)
        norm("n2", 1, 3)
        dve.wait_ge(*pe_.at("sq", "n2", KT - 1))
        with dve.Fori(0, 11) as i:
            for s in (0, 2):
                dve.wait_ge(ff_up, i * 2 + (s // 2 + 1))
                dve.wait_ge(ff_silu, i * 4 + (s + 2))
                for f in range(2):
                    v.tensor_tensor(fT[:, bass.ds(i * 4 + s + f, 1), :], tmp[:, s + f, :].unsqueeze(1),
                                    bank[2 * s + 2 + f][:, 0:T].unsqueeze(1), ALU.mult).then_inc(ff_kept, 1)

        def down(i, u, f, first):
            if f == 0:
                dve.wait_ge(dn_used, i * 8 + (4 * u + 4))
            if not first:
                dve.wait_ge(dn_kept, i * 4 + (2 * u + f))
            residual(i * 4 + (2 * u + f), bank[2 * u + f], 5, dn_t, i * 8 + (4 * u + 2 * f + 2), dn_kept)
        for u in range(2):
            for f in range(2):
                down(0, u, f, u == f == 0)
        with dve.Fori(1, 4) as i:
            for u in range(2):
                for f in range(2):
                    down(i, u, f, False)
        dve.wait_ge(dn_kept, 16)
        norm("nf", 2, None)
        for k in range(1, KT, 2):
            dve.wait_ge(*pe_.at("y", k))
            z = bank[k % 4]
            v.tensor_copy(y_tm[:, :, k * P:(k + 1) * P], z[:, 0:TP].rearrange("p (q f) -> p q f", q=QT)).then_inc(*dve_.mark())
            v.tensor_copy(y_ts[0:B, k * P:(k + 1) * P], z[0:B, TP:TP + P]).then_inc(*dve_.mark("y", k))
        dve_.marks["y_out",] = dve_.n

    return {name: s.marks for name, s in signals.items()}


def kernel(**inputs):
    from concourse import bacc
    from concourse.bass_utils import run_bass_kernel_spmd

    seen = None
    for _ in range(2):
        nc = bacc.Bacc("TRN2", target_bir_lowering=False, num_devices=1)
        ins = {n: nc.dram_tensor("in_" + n, s, I32 if n == "page_table" else F32, kind="ExternalInput").ap()
               for n, s in INS.items()}
        ins["const"] = nc.dram_tensor("in_const", (P, CONST_W), F32, kind="ExternalInput").ap()
        outs = {n: nc.dram_tensor("out_" + n, s, F32, kind="ExternalOutput").ap() for n, s in OUTS.items()}
        with ExitStack() as ctx:
            seen = program(nc, ins, outs, ctx, seen)
    arrays = {"in_" + n: np.ascontiguousarray(inputs[n]) for n in INS}
    arrays["in_const"] = constants()
    r = run_bass_kernel_spmd(nc, [arrays], core_ids=[0])
    return tuple(r.results[0]["out_" + n] for n in OUTS)
```

```python
from contextlib import ExitStack

import numpy as np

import concourse.bass as bass
import concourse.mybir as mybir
from concourse.alu_op_type import AluOpType as ALU

F32 = mybir.dt.float32
F32R = mybir.dt.float32r
I32 = mybir.dt.int32
U32 = mybir.dt.uint32
ACT = mybir.ActivationFunctionType
AX = mybir.AxisListType

P = 128
D = 2048
KT = D // P
RD = 32
TP, B = 256, 8
T = TP + B
QT = TP // P
PAST, PAGE = 2048, 128
NPG = PAST // PAGE
H, KVH, DH = 16, 2, 64
G = H // KVH
BLK, STRIDE, SELB, TOPK = 32, 16, 64, 16
NBP = TP // STRIDE - 1
NBS = PAST // STRIDE - 1
NSEL = PAST // SELB + 1
WIN = 512
DIL = ((128, 1), (512, 4), (2048, 16))
NG, HG, DD = 3, 4, 128
DHEADS = NG * HG
FF = 5632
FT = FF // P
Q_W, KV_W, GATE_W = H * DH, 3 * 2 * KVH * DH, 3 * H
C_KV, C_GATE = Q_W, Q_W + KV_W
C_DIL = C_GATE + GATE_W
C_MERGE = C_DIL + 3 * DHEADS * DD
PROJ_W = C_MERGE + 2 * D
CW = 256
SLOT = KT * CW
NEG = -1e30
SC_N, SC_D = DH ** -0.5, DD ** -0.5
EPS = 1e-6

CONST = {}
S0 = "new_nsa"
_c = 0
for _n, _w in (("ident", P), ("rot_nsa", P), ("rot_dil", P), ("ones", P), ("cos_nsa", T), ("sin_nsa", T),
               ("cos_dil", T), ("sin_dil", T), ("causal", 3 * P), ("dilmask", 9 * P),
               ("cmp_add", QT * NBP), ("cmp_mul", QT * NBP), ("part8", 1), ("rowsel", P), ("head_of", H),
               ("new_nsa", B), ("new_dil", B), ("group", B * KVH), ("spread", P), ("keep", NSEL), ("force", NSEL),
               ("head_cols", HG * RD), ("before", NSEL * NSEL), ("eye", RD * RD)):
    CONST[_n] = (_c, _w)
    _c += _w
CONST_W = _c
CONST_P = CONST[S0][0]


def constants():
    out = np.zeros((P, CONST_W), np.float32)

    def put(name, a):
        a = np.asarray(a, np.float32).reshape(a.shape[0], -1)
        c, w = CONST[name]
        out[:a.shape[0], c:c + w] = a

    put("ident", np.eye(P))
    put("ones", np.ones((P, P)))
    pos = np.concatenate([np.arange(TP), np.full(B, PAST)]).astype(np.float32)
    for name, dh in (("nsa", DH), ("dil", DD)):
        rd = dh // 4
        half = rd // 2
        inv = np.float32(500000.0) ** (-np.arange(half, dtype=np.float32) * np.float32(2.0 / rd))
        ang = (pos[:, None] * inv[None, :].astype(np.float32)).astype(np.float32)
        rot, cos, sin = np.zeros((P, P)), np.ones((P, T)), np.zeros((P, T))
        for base in range(0, P, dh):
            for i in range(half):
                rot[base + i + half, base + i] = -1
                rot[base + i, base + i + half] = 1
                for r in (base + i, base + i + half):
                    cos[r], sin[r] = np.cos(ang[:, i]), np.sin(ang[:, i])
        put("rot_" + name, rot)
        put("cos_" + name, cos)
        put("sin_" + name, sin)
    q, k = np.arange(TP)[:, None], np.arange(TP)[None, :]
    ok = [k <= q] + [(k <= q) & (q - k <= w) & ((q - k) % d == 0) for w, d in DIL]
    add = [np.where(m, 0.0, NEG) for m in ok]
    put("causal", np.concatenate([add[0][:P, :P], add[0][P:, :]], 1))
    put("dilmask", np.concatenate([m[:P, :P] for m in add[1:]] + [m[P:, :] for m in add[1:]], 1))
    kend = np.arange(NBP) * STRIDE + BLK - 1
    seen = (kend[None, :] <= np.arange(TP)[:, None]).reshape(QT, P, NBP).transpose(1, 0, 2)
    put("cmp_add", np.where(seen, 0.0, NEG))
    put("cmp_mul", seen.astype(np.float32))
    own = np.where(np.eye(B, dtype=bool), 0.0, NEG)
    row = np.arange(P)
    put("part8", row[:, None] % 8)
    put("rowsel", row[None, :] // H == np.arange(B)[:, None])
    put("head_of", row[:, None] % H == np.arange(H)[None, :])
    put("new_nsa", own[row // H])
    rd = np.arange(RD)
    put("new_dil", own[rd // HG])
    group = (row // G)[:, None] == np.arange(B * KVH)[None, :]
    put("group", group)
    put("spread", group.T)
    forced = np.zeros(NSEL)
    forced[[0, NSEL - 2, NSEL - 1]] = 1
    put("keep", np.broadcast_to(1 - forced, (H, NSEL)))
    put("force", np.broadcast_to(forced * 1e6, (H, NSEL)))
    put("head_cols", np.broadcast_to(rd[None, :] % HG == np.arange(HG)[:, None], (B, HG, RD)))
    j = np.arange(NSEL)
    put("before", np.broadcast_to(j[None, :] < j[:, None], (H, NSEL, NSEL)))
    put("eye", np.broadcast_to(np.eye(RD), (P, RD, RD)))
    return out


class Signal:

    def __init__(self, sem, seen):
        self.sem, self.seen, self.marks, self.n = sem, seen, {}, 0

    def mark(self, *key, by=1):
        self.n += by
        if key:
            assert key not in self.marks, key
            self.marks[key] = self.n
        return self.sem, by

    def at(self, *key):
        if self.seen is None:
            return self.sem, 1
        return self.sem, self.seen[key]

    def last(self):
        return self.sem, self.n


INS = {"x_prompt": (1, TP, D), "x_sample": (B, 1, D), "cache_cmp_kv": (1, 160, PAGE, 2, KVH, DH),
       "cache_sel_kv": (1, 160, PAGE, 2, KVH, DH), "cache_win_kv": (1, B, WIN, 2, KVH, DH),
       "cache_dil1_kv": (1, B, 128, 2, HG, DD), "cache_dil2_kv": (1, B, 512, 2, HG, DD),
       "cache_dil3_kv": (1, B, 2048, 2, HG, DD), "page_table": (B, NPG), "c_prompt": (1, D),
       "c_sample": (B, D), "w_ada": (1, D, 6 * D), "b_ada": (1, 6 * D), "norm1_g": (1, D),
       "w_in": (1, D, PROJ_W), "cmp_w1": (1, 2, BLK, DH, 64), "cmp_w2": (1, 2, 64, DH),
       "cmp_pe": (1, 2, BLK, DH), "w_br_nsa": (1, H * DH, D), "w_br_dil": (1, HG * DD, D),
       "w_out": (1, D, D), "norm2_g": (1, D), "w_gate": (1, D, FF), "w_up": (1, D, FF),
       "w_down": (1, FF, D), "normf_g": (D,)}
NSA_ROW, DIL_ROW = (2, KVH, DH), (2, HG, DD)
OUTS = {"y_prompt": (1, TP, D), "y_sample": (B, 1, D), "p_cmp": (1, 1, TP) + NSA_ROW,
        "p_sel": (1, 1, TP) + NSA_ROW, "p_win": (1, 1, TP) + NSA_ROW, "p_dil1": (1, 1, P) + DIL_ROW,
        "p_dil2": (1, 1, TP) + DIL_ROW, "p_dil3": (1, 1, TP) + DIL_ROW,
        "s_cmp": (1, B, 1) + NSA_ROW, "s_sel": (1, B, 1) + NSA_ROW, "s_win": (1, B, WIN) + NSA_ROW,
        "s_dil1": (1, B, 128) + DIL_ROW, "s_dil2": (1, B, 512) + DIL_ROW, "s_dil3": (1, B, 2048) + DIL_ROW}


def program(nc, i_, o_, ctx, seen):
    signals = {}

    def sem(name):
        return ctx.enter_context(nc.semaphore(name))

    def signal(name):
        signals[name] = Signal(sem(name), None if seen is None else seen[name])
        return signals[name]

    WORDS = 53192
    mem_at = -(-nc.sbuf_base // 32) * 32
    mem = ctx.enter_context(nc.sbuf_tensor("mem", [P, WORDS], F32))
    pieces = {}

    def piece(a, words, dtype):
        if (a, words, dtype) not in pieces:
            pieces[a, words, dtype] = nc.alloc_sbuf_tensor_at(f"piece{len(pieces)}", [P, words], dtype, offset=mem_at + 4 * a)
        return pieces[a, words, dtype]
    top = [0]

    def part(words, at=None):
        a = top[0] if at is None else at
        if at is None:
            top[0] += -(-words // 8) * 8
        assert a + words <= WORDS, (a + words, WORDS)
        return mem[:, a:a + words]

    c_all = part(CONST_P)

    def const(name):
        c, w = CONST[name]
        if c < CONST_P:
            return c_all[:, c:c + w]
        return {"before": before_c, "eye": eye_c}.get(name) if name in ("before", "eye") \
            else c_sample[:, c - CONST_P:c - CONST_P + w]

    ident, ones = const("ident"), const("ones")
    biasT = part(96)
    gT = part(3 * KT)
    modT = part(96 * 9).rearrange("p (j c) -> p j c", c=9)
    facA = part(KT * 9).rearrange("p (j c) -> p j c", c=9)
    xT = part(KT * T).rearrange("p (j t) -> p j t", t=T)
    hT0 = top[0]
    hT = part(KT * T).rearrange("p (j t) -> p j t", t=T)
    rstd = part(T)
    tmp = part(4 * T).rearrange("p (j t) -> p j t", t=T)
    oN0 = top[0]
    oN = part(8 * T).rearrange("p (j t) -> p j t", t=T)
    oD = part(4 * T).rearrange("p (j t) -> p j t", t=T)
    ring0 = top[0]
    part(3 * SLOT)
    region = top[0]

    def slot(s, k=KT, n=CW):
        a = ring0 + s * SLOT if s < 3 else fourth
        return piece(a, SLOT, F32)[:, 0:k * n].rearrange("p (k n) -> p k n", n=n)

    qk0 = top[0]
    qK = part(G * T).rearrange("p (j t) -> p j t", t=T)
    kT = part(3 * T).rearrange("p (j t) -> p j t", t=T)
    dqk0 = top[0]
    dqk = part(2 * DHEADS * T).rearrange("p (j t) -> p j t", t=T)
    tmN = part(QT * 6 * P).rearrange("p (q j f) -> p q j f", q=QT, j=6)
    tmV0 = top[0]
    tmV = part(QT * DHEADS * P).rearrange("p (q j f) -> p q j f", q=QT, j=DHEADS)
    tmS = part(30 * P).rearrange("p (j f) -> p j f", f=P)
    gates = part(QT * 48).rearrange("p (q j) -> p q j", q=QT)
    gatesS = part(3)
    w1p = part(2 * 16 * 64).rearrange("p (s l j e) -> p s l j e", s=2, j=2, e=64)
    w2 = part(2 * 64).rearrange("p (s e) -> p s e", e=64)
    peT = part(32)
    peb = part(2)
    kcP, vcP = part(16), part(P)
    small = part(96)
    at0 = top[0]
    PB = 9 * P - 3 * P + 16
    E = part(2 * PB).rearrange("p (u k) -> p u k", u=2)
    PT = part(PB)
    rt = mem[:, at0 + 1024:at0 + 1024 + 2 * T].rearrange("p (j t) -> p j t", t=T)
    stage = mem[:, at0:at0 + 1024].rearrange("p (u q f) -> p u q f", u=2, q=QT)
    ctop = at0
    cbsh = mem[:, ctop:ctop + 508]
    chid = mem[:, ctop + 508:ctop + 1016]
    cgl = mem[:, ctop + 1016:ctop + 1524]
    flat = tmp.rearrange("p j t -> p (j t)")
    kTcP = flat[:, 0:512].rearrange("p (j n) -> p j n", j=4)
    pairsP = flat[:, 512:1024].rearrange("p (t f) -> p t f", t=1)

    sbase = [qk0]

    def spart(words):
        a = sbase[0]
        sbase[0] += words
        assert sbase[0] <= tmV0 + QT * DHEADS * P, sbase[0] - tmV0 - QT * DHEADS * P
        return mem[:, a:a + words]
    KS = spart(4096)
    wide = spart(3072)
    SS = wide[:, 0:2576]
    rk = wide[:, 0:NSEL * NSEL].rearrange("p (j i) -> p j i", i=NSEL)
    qpad = wide.rearrange("p (j b r) -> p j b r", j=DHEADS, b=B)
    wide2 = spart(3072)
    before_c = wide2[:, 0:NSEL * NSEL]
    PTn = wide2[:, 0:22 * P].rearrange("p (j r) -> p j r", r=P)
    PTm = wide2.rearrange("p (g r c) -> p g r c", g=NG, r=RD)
    c_sample = spart(CONST["before"][0] - CONST_P)
    vcS = spart(B * P).rearrange("p (b f) -> p b f", f=P)
    qbd = spart(B * P).rearrange("p (b r) -> p b r", r=P)
    ptc = spart(P)
    pcmp = spart(P)
    kcS = spart(P)
    am = spart(NSEL)
    imp = spart(4 * NSEL)
    sel = spart(4 * NSEL).rearrange("p (j i) -> p j i", i=NSEL)
    eye_c = w1p.rearrange("p s l j e -> p (s l j e)")[:, 0:RD * RD]
    late = mem[:, at0 + 1540:at0 + 2352]
    qfull, dqnew = late[:, 0:P], late[:, P:P + 96].rearrange("p (j b) -> p j b", b=B)
    dknew = late[:, 224:320].rearrange("p (j b) -> p j b", b=B)
    knew = late[:, 320:336].rearrange("p (j b) -> p j b", b=B)
    Ed = late[:, 336:336 + 408]
    qn = mem[:, at0:at0 + 384].rearrange("p (j r) -> p j r", r=RD)
    Pn = mem[:, at0 + 384:at0 + 768].rearrange("p (g h r) -> p g h r", g=NG, h=HG)
    oR = wide[:, 0:B * P].rearrange("p (b f) -> p b f", f=P)
    win = mem[:, at0:at0 + 1024].rearrange("p (u t f) -> p u t f", u=2, t=4)
    oRd = mem[:, at0 + 768:at0 + 768 + P]

    prod = mem[:, region + KT * T:region + (KT + 4) * T].rearrange("p (j t) -> p j t", t=T)
    xs8 = rstd[:, 0:B].unsqueeze(1)
    mT = mem[:, region:region + KT * T].rearrange("p (j t) -> p j t", t=T)
    fT = mem[:, region:region + FT * T].rearrange("p (j t) -> p j t", t=T)
    fourth = region + FT * T
    assert fourth + SLOT <= WORDS
    spare = fourth + SLOT
    dead_consts = CONST["cos_nsa"][0]

    def tiles_at(*runs):
        return [a + j * T for a, n in runs for j in range(n)]
    ffn_high = [spare, spare + 2048, spare + 4096 + 4 * T, dead_consts]
    h_high = tiles_at((oN0, 12), (spare + 4096, 4))
    KD = FT // 4
    down_high = [spare, spare + KD * P, dead_consts, dead_consts + KD * P]
    f_high = tiles_at((hT0, 16), (oN0, 12), (spare + 2 * KD * P, 16))
    assert ffn_high[2] + 2048 <= WORDS and f_high[-1] + T <= WORDS
    assert dead_consts + 2 * KD * P <= CONST_P + 96

    def half_chunk(a, k, f=0, n=P):
        return piece(a, k * n, F32R)[:, :].rearrange("p (k n) -> p k n", n=n)[:, :, f * P:(f + 1) * P]

    def half_tile(a):
        return piece(a, T, F32R)[:, :]

    def slot_at(s):
        return ring0 + s * SLOT if s < 3 else fourth
    c_rows = mem[:, region:region + D]
    c_silu = mem[:, region + D:region + 2 * D]
    x_tm = mem[:, region + 2 * D:region + 4 * D].rearrange("p (q f) -> p q f", q=QT)
    x_ts = mem[:, region + 4 * D:region + 5 * D]
    vec_rows = mem[:, region + 5 * D:region + 5 * D + 2 * P].rearrange("p (u f) -> p u f", u=2)
    siluT = mem[:, region + 5 * D + 256:region + 5 * D + 256 + KT * 9].rearrange("p (j c) -> p j c", c=9)
    assert region + 5 * D + 512 <= fourth
    ada_row = tmp.rearrange("p j t -> p (j t)")[:, 0:4 * CW].rearrange("p (s n) -> p s n", s=4)
    y_tm, y_ts = x_tm, x_ts
    pages = ctx.enter_context(nc.sbuf_tensor("pages", [P, B], I32))
    runs = ctx.enter_context(nc.sbuf_tensor("runs", [P, B], U32))

    bank = [ctx.enter_context(nc.psum_tensor(f"bank{n}", [P, 512], F32)) for n in range(8)]

    const_loaded = sem("const_loaded")
    rows_loaded = sem("rows_loaded")
    loaded = [signal(f"slot{s}_loaded") for s in range(4)]
    pe_, act_, dve_ = signal("pe_step"), signal("act_step"), signal("dve_step")
    outs_stored = signal("outs_stored")
    stage_stored = [signal(f"stage{s}_stored") for s in range(2)]
    cmp_stored, rows_stored = signal("cmp_stored"), signal("rows_stored")
    sample_const = sem("sample_const")
    pairs_loaded = signal("pairs_loaded")
    pages_loaded = sem("pages_loaded")
    pages_in = [signal(f"pages{s}_in") for s in range(3)]
    win_in = [signal(f"window{s}_in") for s in range(2)]
    caches_copied = signal("caches_copied")
    ada_done, ada_kept, ada_rows, ada_turned = sem("ada_done"), sem("ada_kept"), sem("ada_rows"), sem("ada_turned")
    mg_gate, mg_y, mg_sig, mg_kept = sem("merge_gates"), sem("merge_y"), sem("merge_sigmoids"), sem("merge_kept")
    mg_t = sem("merge_products")
    wo_done, wo_t, wo_kept = sem("wout_done"), sem("wout_products"), sem("wout_kept")
    ff_silu, ff_kept = sem("ffn_silu"), sem("ffn_kept")
    ff_high, ff_low, ff_half = sem("ffn_high_parts"), sem("ffn_low_parts"), sem("ffn_halves_used")
    dn_high, dn_low, dn_half = sem("down_high_parts"), sem("down_low_parts"), sem("down_halves_used")
    dn_t, dn_kept = sem("down_products"), sem("down_kept")
    w_ld = {ph: [sem(f"{ph}_loaded{s}") for s in range(4)] for ph in ("ada", "merge", "wout", "ffn", "down")}

    w_ada, w_in, w_out = i_["w_ada"][0], i_["w_in"][0], i_["w_out"][0]
    w_gate, w_up, w_down = i_["w_gate"][0], i_["w_up"][0], i_["w_down"][0]
    w_bn, w_bd = i_["w_br_nsa"][0], i_["w_br_dil"][0]

    def rows(w, c, n=CW):
        return w[:, c].rearrange("(k p) n -> p k n", p=P)

    CHUNKS = [(C_GATE, 48)] + [(C_KV + CW * j, CW) for j in range(3)] + [(CW * j, CW) for j in range(4)] \
        + [(C_DIL + CW * j, CW) for j in range(3 * DHEADS // 2)]
    TILES = [("gate", 0)] + [(("k", "v")[j % 2], j // 2) for j in range(6)] + [("q", j) for j in range(8)] \
        + [(k, h) for k in ("dq", "dk", "dv") for h in range(DHEADS)]
    NT = len(TILES)

    def chunk_of(n):
        return 0 if n == 0 else (n + 1) // 2

    ROPED = ("k", "q", "dq", "dk")
    TURNED = ("k", "v", "dk", "dv")

    def made(n):
        return dve_.at("roped", n) if TILES[n][0] in ROPED else act_.at("raw", n)

    LASTN = NT - 1
    UNITS = [("n", qt, h) for h in range(H) for qt in range(QT)] + [("d", qt, h) for h in range(HG) for qt in range(QT)]
    NU = len(UNITS)

    def blocks(u):
        kind, qt, h = UNITS[u]
        W = P * (qt + 1)
        if kind == "n":
            kv = h // G
            out = [(br * W + kb * P, P, tmN[:, kb, 2 * (br + 1) + 1, kv * DH:(kv + 1) * DH])
                   for br in range(2) for kb in range(qt + 1)]
            return out + [(2 * W, NBP, vcP[0:NBP, kv * DH:(kv + 1) * DH])]
        return [(g * W + kb * P, P, tmV[:, kb, g * HG + h, :]) for g in range(NG) for kb in range(qt + 1)]

    block = ctx.enter_context(nc.Block())

    @block.sync
    def _(sp):
        sp.dma_start(c_all, i_["const"][:, 0:CONST_P]).then_inc(const_loaded, 16)
        sp.dma_start(c_rows[0:1, :], i_["c_prompt"]).then_inc(rows_loaded, 16)
        sp.dma_start(c_rows[1:1 + B, :], i_["c_sample"]).then_inc(rows_loaded, 16)
        sp.dma_start(vec_rows[0:96, 0, :], i_["b_ada"][0].rearrange("(j f) -> j f", f=P)).then_inc(rows_loaded, 16)
        for n, v in enumerate((i_["norm1_g"][0], i_["norm2_g"][0], i_["normf_g"])):
            sp.dma_start(vec_rows[KT * n:KT * (n + 1), 1, :], v.rearrange("(j f) -> j f", f=P)).then_inc(rows_loaded, 16)
        sp.dma_start(x_tm, i_["x_prompt"][0].rearrange("(q p) f -> p q f", p=P)).then_inc(rows_loaded, 16)
        sp.dma_start(x_ts[0:B, :], i_["x_sample"].rearrange("b o f -> (b o) f")).then_inc(rows_loaded, 16)

        for s in range(4):
            sp.dma_start(slot(s), rows(w_ada, bass.ds(s * CW, CW))).then_inc(w_ld["ada"][s], 16)
        with sp.Fori(1, 12) as i:
            cols = [sp.snap(i * (4 * CW) + s * CW) for s in range(4)]
            for s in range(4):
                sp.wait_ge(ada_done, i * 4 + (s - 3))
                sp.dma_start(slot(s), rows(w_ada, bass.ds(cols[s], CW))).then_inc(w_ld["ada"][s], 16)
        for c, (col, n) in enumerate(CHUNKS):
            if c < 3:
                sp.wait_ge(ada_done, 45 + c)
            else:
                sp.wait_ge(*pe_.at("chunk", c - 3))
            sp.dma_start(slot(c % 3, KT, n), rows(w_in, slice(col, col + n))).then_inc(*loaded[c % 3].mark("proj", c, by=16))
            if c == 2:
                sp.wait_ge(*dve_.at("x_in"))
                for j in range(8):
                    sp.dma_start(pages[j:P:8, :], i_["page_table"].rearrange("b n -> n b"),
                                 allow_slow_non_contiguous=True).then_inc(pages_loaded, 16)
                w1 = i_["cmp_w1"][0].rearrange("s (m l) d e -> (l d) s m e", l=2)
                for s in range(2):
                    for j in range(2):
                        sp.dma_start(w1p[:, s, :, j, :], w1[:, s, 8 * j:8 * j + 8, :]).then_inc(rows_loaded, 16)
                sp.dma_start(w2[0:64], i_["cmp_w2"][0].rearrange("s e d -> e s d")).then_inc(rows_loaded, 16)
                sp.dma_start(peT[:, 0:32], i_["cmp_pe"][0].rearrange("s (m l) d -> (l d) (s m)", l=2),
                             allow_slow_non_contiguous=True).then_inc(rows_loaded, 16)
        sp.wait_ge(*pe_.at("tm", LASTN))
        sp.wait_ge(*cmp_stored.at("p_cmp"))
        for l in range(2):
            sp.dma_start(pairsP[:, 0, :].rearrange("p (j l d) -> p j l d", j=4, l=2)[:, :, l, :],
                         o_["p_cmp"][0, 0].rearrange("(n l) s h d -> n l (s h) d", l=2)[:, l])\
                .then_inc(*pairs_loaded.mark(*(("p",) if l else ()), by=16))
        sp.wait_ge(*dve_.at("sample_q"))
        before_at, eye_at = CONST["before"][0], CONST["eye"][0]
        sp.dma_start(c_sample, i_["const"][:, CONST_P:before_at]).then_inc(sample_const, 16)
        sp.dma_start(before_c, i_["const"][:, before_at:eye_at]).then_inc(sample_const, 16)

        for u in range(5 * B):
            s, b, kind = u % 3, u % B, u // B
            flat = slot(s).rearrange("p k n -> p (k n)")
            if kind in (1, 2):
                kv, w = kind - 1, u % 2
                if u < B + 2:
                    sp.wait_ge(*pe_.at("kvc", B - 1))
                else:
                    sp.wait_ge(*pe_.at("win_used", u - 2))
                sp.dma_start(win[:, w], i_["cache_win_kv"][0, b].rearrange("(p t) s h d -> p t s (h d)", t=4)[:, :, kv])\
                    .then_inc(*win_in[w].mark("use", u, by=16))
            elif kind >= 3:
                sp.wait_ge(*pe_.at("used", u - 3))
                kv = kind - 3
                for g, (w, d) in enumerate(DIL):
                    src = i_[f"cache_dil{g + 1}_kv"][0, b].rearrange("(n r) s h d -> n r s (h d)", r=d)[:, 0, kv]
                    sp.dma_start(flat[:, g * 512:(g + 1) * 512], src)\
                        .then_inc(*loaded[s].mark(*(("use", u) if g == 2 else ()), by=16))
            if u == B:
                sp.wait_ge(*pe_.at("hid", B - 1))
                sp.dma_start(eye_c, i_["const"][:, eye_at:CONST_W]).then_inc(sample_const, 16)
        def merge_load(s, col):
            if s < 2:
                sp.dma_start(slot(s), rows(w_in, bass.ds(col, CW))).then_inc(w_ld["merge"][s], 16)
            else:
                sp.dma_start(slot(2)[:, 0:8, :], rows(w_bn, slice(0, CW))).then_inc(w_ld["merge"][2], 16)
                sp.dma_start(slot(2)[:, 8:12, :], rows(w_bd, slice(0, CW))).then_inc(w_ld["merge"][2], 16)
        for s in range(3):
            sp.wait_ge(*pe_.at("used", 5 * B - 1 - (5 * B - 1 - s) % 3))
            merge_load(s, (C_MERGE, C_MERGE + D, 0)[s])
        with sp.Fori(1, 8) as i:
            cols = [sp.snap(i * CW + C_MERGE), sp.snap(i * CW + (C_MERGE + D))]
            sp.wait_ge(mg_gate, i * 2 - 1)
            merge_load(0, cols[0])
            sp.wait_ge(mg_gate, i * 2)
            merge_load(1, cols[1])
        for i in range(2):
            for s in range(4):
                if i == 0:
                    if s < 2:
                        sp.wait_ge(mg_gate, 15 + s)
                    elif s == 2:
                        sp.wait_ge(mg_y, 8)
                else:
                    sp.wait_ge(wo_done, s + 1)
                sp.dma_start(slot(s), rows(w_out, slice((4 * i + s) * CW, (4 * i + s + 1) * CW))).then_inc(w_ld["wout"][s], 16)
        for s in range(4):
            sp.wait_ge(wo_done, 5 + s)
            sp.dma_start(slot(s), rows((w_gate, w_up)[s % 2], bass.ds((s // 2) * CW, CW))).then_inc(w_ld["ffn"][s], 16)
        with sp.Fori(1, 11) as i:
            cols = [sp.snap(i * (2 * CW)), sp.snap(i * (2 * CW) + CW)]
            for s in range(4):
                sp.wait_ge(ff_half, i * 8 + (2 * s - 6))
                sp.dma_start(slot(s), rows((w_gate, w_up)[s % 2], bass.ds(cols[s // 2], CW)))\
                    .then_inc(w_ld["ffn"][s], 16)

        def down_load(s, col):
            sp.dma_start(slot(s, KD), w_down[s * KD * P:(s + 1) * KD * P, col].rearrange("(k p) n -> p k n", p=P))\
                .then_inc(w_ld["down"][s], 16)
        for s in range(4):
            sp.wait_ge(ff_half, 80 + 2 * s + 2)
            down_load(s, bass.ds(0, CW))
        with sp.Fori(1, 8) as i:
            col = sp.snap(i * CW)
            for s in range(4):
                sp.wait_ge(dn_half, i * 8 + (2 * s - 6))
                down_load(s, bass.ds(col, CW))
        sp.wait_ge(*act_.at("y_out"))
        sp.wait_ge(*dve_.at("y_out"))
        sp.dma_start(o_["y_prompt"][0].rearrange("(q p) f -> p q f", p=P), y_tm).then_inc(*outs_stored.mark(by=16))
        sp.dma_start(o_["y_sample"].rearrange("b o f -> (b o) f"), y_ts[0:B, :]).then_inc(*outs_stored.mark("y", by=16))
        sp.wait_ge(*outs_stored.at("y"))
        sp.wait_ge(*caches_copied.at("all"))
        for s in range(2):
            sp.wait_ge(*stage_stored[s].at("last"))
        sp.wait_ge(*rows_stored.at("all"))

    @block.gpsimd
    def _(pool):
        n_copy = 0

        def gathers():
            pool.wait_ge(*dve_.at("runs"))
            for u in range(3 * B):
                s, b = u % 3, u % B
                if u < 3:
                    pool.wait_ge(*pe_.at("chunk", len(CHUNKS) - 1))
                else:
                    pool.wait_ge(*pe_.at("used", u - 3))
                flat = slot(s).rearrange("p k n -> p (k n)")
                src = i_[("cache_cmp_kv", "cache_sel_kv")[min(u // B, 1)]][0].rearrange("n (j t) s h d -> (n j) (t s h d)", j=8)
                pool.indirect_dma_start(flat, None, src, bass.IndirectOffsetOnAxis(runs[:, b:b + 1], 0))\
                    .then_inc(*pages_in[s].mark("use", u, by=16))
        for name, n in (("dil3", 2048), ("dil2", 512), ("dil1", 128), ("win", WIN)):
            src, dst = i_[f"cache_{name}_kv"][0], o_[f"s_{name}"][0]
            for c in range(B):
                if n_copy < 8:
                    pool.wait_ge(*pe_.at("chunk", 3 + 3 * n_copy))
                elif n_copy < 16:
                    if n_copy == 8:
                        gathers()
                    pool.wait_ge(ff_half, 4 + 8 * (n_copy - 8))
                f = "t s h d -> (t s h d)"
                a, z = src[c, 1:n].rearrange(f), dst[c, 0:n - 1].rearrange(f)
                pool.dma_start(z.rearrange("(q n) -> q n", q=16), a.rearrange("(q n) -> q n", q=16))\
                    .then_inc(*caches_copied.mark(*(("all",) if (name, c) == ("win", B - 1) else ()), by=16))
                n_copy += 1

    @block.tensor
    def _(pe):
        mm, turn = nc.tensor.matmul, nc.tensor.transpose
        pe.wait_ge(const_loaded, 16)
        pe.wait_ge(rows_loaded, 8 * 16)
        pe.wait_ge(*dve_.at("silu"))
        for k in range(KT):
            last = turn(bank[0][:, 9 * k:9 * k + 9], c_silu[0:9, k * P:(k + 1) * P], ident[0:9, 0:9])
        last.then_inc(*pe_.mark("siluT"))
        turn(bank[1][:, 0:96], vec_rows[0:96, 0, :], ident[0:96, 0:96])
        turn(bank[1][:, 96:144], vec_rows[0:48, 1, :], ident[0:48, 0:48]).then_inc(*pe_.mark("vecT"))
        for k in range(KT):
            if k >= 4:
                pe.wait_ge(*(dve_ if k % 2 else act_).at("xT", k - 4))
            z = bank[2 + k % 4]
            for q in range(QT):
                turn(z[:, q * P:(q + 1) * P], x_tm[:, q, k * P:(k + 1) * P], ident)
            turn(z[:, TP:T], x_ts[0:B, k * P:(k + 1) * P], ident[0:B, 0:B]).then_inc(*pe_.mark("xT", k))
        pe.wait_ge(*act_.at("siluT"))
        pe.wait_ge(*dve_.at("vecT"))
        pe.wait_ge(*dve_.at("xT", KT - 1))
        pe.wait_ge(*act_.at("xT", KT - 2))

        def ada(i, s, first):
            pe.wait_ge(w_ld["ada"][s], i * 16 + 16)
            if not first:
                pe.wait_ge(ada_kept, i * 4 + (s - 3))
            for k in range(KT):
                last = mm(bank[s][0:9, 0:CW], siluT[:, k, :], slot(s)[:, k, :], start=(k == 0), stop=(k == KT - 1))
            last.then_inc(ada_done, 1)

        def ada_turn(i, s):
            pe.wait_ge(const_loaded, 16)
            pe.wait_ge(ada_rows, i * 4 + (s + 1))
            for f in range(2):
                last = turn(bank[4 + s][:, f * P:(f + 1) * P], ada_row[:, s, f * P:(f + 1) * P], ident)
            last.then_inc(ada_turned, 1)
        for s in range(4):
            ada(0, s, True)
            if s:
                ada_turn(0, s - 1)
        with pe.Fori(1, 12) as i:
            for s in range(4):
                ada(i, s, False)
                ada_turn(i + (-1 if s == 0 else 0), (s - 1) % 4)
        ada_turn(11, 3)

        def stats(tag):
            for k in range(KT):
                pe.wait_ge(*dve_.at("sq", tag, k))
                last = mm(bank[7][:, 0:T], ones, tmp[:, k % 4, :], start=(k == 0), stop=(k == KT - 1))
                last.then_inc(*pe_.mark("sq", tag, k))
        stats("n1")

        pe.wait_ge(*act_.at("h", "n1"))
        pe.wait_ge(*dve_.at("h", "n1"))

        def rope(n):
            kind = TILES[n][0]
            if kind not in ROPED:
                return
            pe.wait_ge(*act_.at("raw", n))
            if n >= 2:
                pe.wait_ge(*dve_.at("rope_bank", n))
            mm(bank[4 + n % 2][:, 0:T], const("rot_nsa" if kind in "kq" else "rot_dil"), tmp[:, n % 3, :],
               start=True, stop=True).then_inc(*pe_.mark("rot", n))

        def source(n):
            kind, j = TILES[n]
            return {"k": lambda: kT[:, j, :], "dk": lambda: dqk[:, DHEADS + j, :]}.get(kind, lambda: tmp[:, n % 3, :])()

        def token_major(n):
            kind = TILES[n][0]
            if kind not in TURNED:
                return
            pe.wait_ge(*made(n))
            pe.wait_ge(*act_.at("tm_bank", n))
            for q in range(QT):
                turn(bank[6 + n % 2][:, q * P:(q + 1) * P], source(n)[:, q * P:(q + 1) * P], ident)
            turn(bank[6 + n % 2][0:B, TP:TP + P], source(n)[:, TP:T], ident).then_inc(*pe_.mark("tm", n))

        for n in range(NT + 2):
            if n < NT:
                kind = TILES[n][0]
                c = chunk_of(n)
                w = CHUNKS[c][1]
                f = 0 if n == 0 else (n + 1) % 2
                m = 48 if n == 0 else P
                pe.wait_ge(*loaded[c % 3].at("proj", c))
                if n >= 4:
                    pe.wait_ge(*act_.at("raw", n - 4))
                for k in range(KT):
                    last = mm(bank[n % 4][0:m, 0:T], slot(c % 3, KT, w)[:, k, f * P:f * P + m], hT[:, k, :],
                              start=(k == 0), stop=(k == KT - 1))
                last.then_inc(*pe_.mark("acc", n))
                if n == 0 or f == 1:
                    pe_.marks["chunk", c] = pe_.n
            if n == 1:
                pe.wait_ge(*act_.at("raw", 0))
                for q in range(QT):
                    turn(bank[6][:, q * 48:(q + 1) * 48], tmp[0:48, 0, q * P:(q + 1) * P], ident[0:48, 0:48])
                turn(bank[6][0:B, 128:176], tmp[0:48, 0, TP:T], ident[0:48, 0:48]).then_inc(*pe_.mark("gateT"))
                pe.wait_ge(*act_.at("gateS"))
                mm(bank[7][:, 0:48], const("rowsel")[0:B, :], small[0:B, 0:48], start=True, stop=True)\
                    .then_inc(*pe_.mark("gateS"))
            if 1 <= n <= NT:
                rope(n - 1)
            if n >= 2:
                token_major(n - 2)

        def compress_turns(tag, pairs, kTc, nt):
            for sh in range(4):
                for half in range(max(1, nt // 4)):
                    i = sh * max(1, nt // 4) + half
                    for t in range(min(nt, 4)):
                        tt = half * 4 + t
                        src = pairs[:, tt, sh * P:(sh + 1) * P]
                        if t == 0:
                            e = (act_, dve_)[i % 2]
                            if i >= 2:
                                pe.wait_ge(*e.at("ctr", tag, i - 2))
                        last = turn(bank[4 + i % 2][:, t * P:(t + 1) * P], src, ident)
                    last.then_inc(*pe_.mark("ctr", tag, i))

        def compress(tag, kTc, nt):
            n_chunk = nt * 16
            nb = n_chunk - 1
            per = max(1, nt // 4)
            for sh in range(4):
                for i in range(sh * per, (sh + 1) * per):
                    pe.wait_ge(*(act_, dve_)[i % 2].at("ctr", tag, i))
                for l in range(8):
                    last = mm(bank[0][:, sh * P:sh * P + n_chunk],
                              w1p[:, sh // 2, l, :, :].rearrange("p j e -> p (j e)"), kTc[:, sh, 0:nt * P].rearrange("p (n l) -> p l n", l=8)[:, l, :],
                              start=(l == 0), stop=(l == 7))
            last.then_inc(*pe_.mark("hid", tag))
            pe.wait_ge(*act_.at("gelu", tag))
            gl = cgl[0:64].rearrange("p (j n) -> p j n", j=4)
            for h in range(2):
                mm(bank[1][h * 64:(h + 1) * 64, 0:nb], w2[0:64, 0, :], gl[:, h, 0:nb], start=True, stop=True)
            for h in range(2):
                last = mm(bank[2][0:nb, h * 64:(h + 1) * 64], gl[:, 2 + h, 0:nb], w2[0:64, 1, :], start=True, stop=True)
            last.then_inc(*pe_.mark("kvc", tag))

        pe.wait_ge(rows_loaded, 14 * 16)
        for s in range(2):
            for m in range(16):
                last = mm(bank[3][0:64, s:s + 1], w1p[:, s, m % 8, m // 8, :], peT[:, s * 16 + m:s * 16 + m + 1],
                          start=(m == 0), stop=(m == 15))
        last.then_inc(*pe_.mark("pe"))
        pe.wait_ge(*pairs_loaded.at("p"))
        pe.wait_ge(*act_.at("raw", LASTN))
        pe.wait_ge(*dve_.at("roped", NT - DHEADS - 1))
        compress_turns("p", pairsP, kTcP, 1)
        compress("p", kTcP, 1)

        def scores(u):
            kind, qt, h = UNITS[u]
            W = P * (qt + 1)
            if u >= 1:
                pe.wait_ge(*dve_.at("max", u - 1))
            if kind == "n":
                kv, g = h // G, h % G
                r = slice(kv * DH, (kv + 1) * DH)
                q = qK[r, g, qt * P:(qt + 1) * P]
                for br in range(2):
                    mm(bank[0][:, br * W:(br + 1) * W], q, kT[r, br + 1, 0:W], start=True, stop=True)
                mm(bank[1][:, 0:NBP], q, kcP[r, 0:NBP], start=True, stop=True).then_inc(*pe_.mark("s", u))
            else:
                for g in range(NG):
                    z = bank[0][:, g * W:(g + 1) * W] if g < 2 else bank[1][:, 0:W]
                    last = mm(z, dqk[:, g * HG + h, qt * P:(qt + 1) * P], dqk[:, DHEADS + g * HG + h, 0:W], start=True, stop=True)
                last.then_inc(*pe_.mark("s", u))

        def probs(u):
            pe.wait_ge(*dve_.at("p", u))
            if u >= 1:
                pe.wait_ge(*act_.at("pt", u - 1))
            for n, (c, k, _) in enumerate(blocks(u)):
                last = turn(bank[2 + n // 4][0:k, (n % 4) * P:(n % 4 + 1) * P], E[:, u % 2, c:c + k], ident)
            last.then_inc(*pe_.mark("pt", u))

        def pv(u):
            kind, qt, h = UNITS[u]
            pe.wait_ge(*act_.at("pt", u))
            if u >= 2:
                pe.wait_ge(*act_.at("o", u - 2))
            z = bank[4 + u % 2]
            out = z[(h % 2) * DH:(h % 2 + 1) * DH, 0:P] if kind == "n" else z[:, 0:P]
            bl = blocks(u)
            for n, (c, k, v) in enumerate(bl):
                last = mm(out, v, PT[0:k, n * P:(n + 1) * P], start=(n == 0), stop=(n == len(bl) - 1))
            last.then_inc(*pe_.mark("pv", u))

        pe.wait_ge(*act_.at("kvc", "p"))
        pe.wait_ge(*dve_.at("kvc", "p"))
        pe.wait_ge(*act_.at("tm", LASTN))
        for u in range(NU + 2):
            if u < NU:
                scores(u)
            if 1 <= u <= NU:
                probs(u - 1)
            if u >= 2:
                pv(u - 2)

        pe.wait_ge(sample_const, 32)
        pe.wait_ge(*act_.at("o", NU - 1))
        pe.wait_ge(*dve_.at("sample_q"))
        NX = 4 * B
        for x in range(NX + 2):
            if x < NX:
                b, kv, eighth = x // 4, x % 4 // 2, x % 2
                if x % 4 == 0:
                    pe.wait_ge(*pages_in[b % 3].at("use", b))
                for half, e in enumerate((act_, dve_)):
                    if x >= 2:
                        pe.wait_ge(*e.at("cx", x - 2))
                    for t in range(4):
                        last = turn(bank[4 + 2 * (x % 2) + half][:, t * P:(t + 1) * P],
                                    slot(b % 3)[:, 8 * eighth + 4 * half + t, kv * P:(kv + 1) * P], ident)
                    last.then_inc(*pe_.mark("cx", x, half))
                if x % 4 == 3:
                    pe_.marks["used", b] = pe_.n
            if x >= 2 and x % 2 == 0:
                b, kv = (x - 2) // 4, (x - 2) % 4 // 2
                for e in (act_, dve_):
                    pe.wait_ge(*e.at("cx", x - 1))
                for sh in (2 * kv, 2 * kv + 1):
                    for l in range(8):
                        last = mm(bank[b % 2][:, sh * P:(sh + 1) * P], w1p[:, kv, l, :, :].rearrange("p j e -> p (j e)"),
                                  KS[:, sh * 1024 + l * P:sh * 1024 + (l + 1) * P], start=(l == 0), stop=(l == 7))
                last.then_inc(*pe_.mark("hid" if kv else "hx", b))
            if x >= 5 and (x - 5) % 4 == 0 and (x - 5) // 4 < B:
                b = (x - 5) // 4
                pe.wait_ge(*act_.at("gelu", b))
                gl = cgl[0:64].rearrange("p (j n) -> p j n", j=4)
                for h in range(2):
                    mm(bank[2][h * 64:(h + 1) * 64, 0:NBS], w2[0:64, 0, :], gl[:, h, 0:NBS], start=True, stop=True)
                for h in range(2):
                    last = mm(bank[2][0:NBS, P + h * 64:P + (h + 1) * 64], gl[:, 2 + h, 0:NBS], w2[0:64, 1, :], start=True, stop=True)
                last.then_inc(*pe_.mark("kvc", b))
            if x >= 6 and (x - 6) % 4 == 0 and (x - 6) // 4 < B - 1:
                b = (x - 6) // 4
                pe.wait_ge(*act_.at("kvc", b))
                mm(bank[3][:, 0:NBS], qbd[:, b, :], kcS[:, 0:NBS], start=(b == 0), stop=(b == B - 1)).then_inc(*pe_.mark("cs", b))
        b = B - 1
        pe.wait_ge(*act_.at("kvc", b))
        mm(bank[3][:, 0:NBS], qbd[:, b, :], kcS[:, 0:NBS], start=False, stop=True).then_inc(*pe_.mark("cs", b))
        pe.wait_ge(*dve_.at("cp"))
        mm(bank[0][0:H, 0:NBS], const("group"), pcmp[:, 0:NBS], start=True, stop=True).then_inc(*pe_.mark("imp"))
        pe.wait_ge(*dve_.at("cpg"))
        turn(bank[1][0:NBS, 0:P], pcmp[:, 0:NBS], ident).then_inc(*pe_.mark("cpt"))
        pe.wait_ge(*dve_.at("sel"))
        mm(bank[0][:, 256:256 + NSEL], const("spread")[0:H, :], sel[0:H, 0, :], start=True, stop=True).then_inc(*pe_.mark("spread"))
        pe.wait_ge(*dve_.at("am"))
        pe.wait_ge(*act_.at("cpt"))

        NY = 5 * B
        for y in range(NY + 2):
            if y < NY:
                b, i = y // 5, y % 5
                u = B + b
                if i == 0:
                    pe.wait_ge(*pages_in[u % 3].at("use", u))
                if i == 4:
                    pe.wait_ge(*win_in[u % 2].at("use", u))
                if y >= 3:
                    pe.wait_ge(*(act_, dve_)[(y - 3) % 2].at("ky", y - 3))
                for t in range(4):
                    keys = slot(u % 3)[:, 4 * i + t, 0:P] if i < 4 else win[:, u % 2, t, :]
                    last = turn(bank[4 + y % 3][:, t * P:(t + 1) * P], keys, ident)
                last.then_inc(*pe_.mark("ky", y))
                if i == 3:
                    pe_.marks["used", u] = pe_.n
                if i == 4:
                    pe_.marks["win_used", u] = pe_.n
            if y >= 2:
                x = y - 2
                b, i = x // 5, x % 5
                pe.wait_ge(*(act_, dve_)[x % 2].at("ky", x))
                last = mm(bank[i if i < 4 else 7][:, :], qbd[:, b, :], KS[:, (x % 8) * 512:(x % 8 + 1) * 512],
                          start=(b == 0), stop=(b == B - 1))
                last.then_inc(*pe_.mark("sy", x))
        for br in range(2):
            last = mm(bank[4][:, br * B:(br + 1) * B], qfull, knew[:, br, :], start=True, stop=True)
        last.then_inc(*pe_.mark("snew"))
        pe.wait_ge(*dve_.at("sp"))
        for i in range(5):
            if i >= 3:
                pe.wait_ge(*(act_, dve_)[(i - 3) % 2].at("pt", "s", i - 3))
            for t in range(4):
                c = (4 * i + t) * P if i < 4 else 2056 + t * P
                last = turn(bank[5 + i % 3][:, t * P:(t + 1) * P], SS[:, c:c + P], ident)
            last.then_inc(*pe_.mark("spt", i))
        pe.wait_ge(*dve_.at("sp"))
        for br, c in enumerate((2048, 2568)):
            last = turn(bank[4][0:B, br * P:(br + 1) * P], SS[:, c:c + B], ident)
        last.then_inc(*pe_.mark("spt", 5))
        for i in range(5):
            pe.wait_ge(*(act_, dve_)[i % 2].at("pt", "s", i))
        pe.wait_ge(*dve_.at("pt", "s", 5))
        for b in range(B):
            u = 2 * B + b
            pe.wait_ge(*pages_in[u % 3].at("use", u))
            pe.wait_ge(*win_in[u % 2].at("use", u))
            out = bank[b // 4][0:H, (b % 4) * P:(b % 4 + 1) * P]
            rows_b = slice(b * H, (b + 1) * H)
            for t in range(20):
                values = slot(u % 3)[:, t, P:2 * P] if t < 16 else win[:, u % 2, t - 16, :]
                mm(out, PTn[:, t, rows_b], values, start=(t == 0), stop=False)
            pe_.marks["used", u] = pe_.marks["win_used", u] = pe_.n + 1
            for br in range(2):
                mm(out, PTn[0:B, 20 + br, rows_b], tmS[0:B, 2 * (br + 1) + 1, :], start=False, stop=False)
            mm(out, ptc[0:NBS, rows_b], vcS[0:NBS, b, :], start=False, stop=True).then_inc(*pe_.mark("pvS", b))
        pe.wait_ge(*act_.at("oR"))
        for b in range(B):
            last = turn(bank[4][:, b * H:(b + 1) * H], oR[0:H, b, :], ident[0:H, 0:H])
        last.then_inc(*pe_.mark("oT"))

        pe.wait_ge(*dve_.at("qpad"))
        NZ = NG * B
        for z in range(NZ + 2):
            if z < NZ:
                b, g = z // NG, z % NG
                u = 3 * B + b
                if g == 0:
                    pe.wait_ge(*loaded[u % 3].at("use", u))
                if z >= 3:
                    pe.wait_ge(*(act_, dve_)[(z - 3) % 2].at("kz", z - 3))
                for h in range(HG):
                    last = turn(bank[5 + z % 3][:, h * P:(h + 1) * P],
                                slot(u % 3).rearrange("p k n -> p (k n)")[:, (g * HG + h) * P:(g * HG + h + 1) * P], ident)
                last.then_inc(*pe_.mark("kz", z))
                if g == NG - 1:
                    pe_.marks["used", u] = pe_.n
            if z >= 2:
                x = z - 2
                b, g = x // NG, x % NG
                pe.wait_ge(*(act_, dve_)[x % 2].at("kz", x))
                for h in range(HG):
                    last = mm(bank[g][0:RD, 0:P], qpad[:, g * HG + h, b, :], KS[:, (x % 8) * 512 + h * P:(x % 8) * 512 + (h + 1) * P],
                              start=(b == 0 and h == 0), stop=(b == B - 1 and h == HG - 1))
                last.then_inc(*pe_.mark("sz", x))
        for g in range(NG):
            for h in range(HG):
                last = mm(bank[3][0:RD, g * B:(g + 1) * B], qn[:, g * HG + h, :], dknew[:, g * HG + h, :],
                          start=(h == 0), stop=(h == HG - 1))
        last.then_inc(*pe_.mark("dnew"))
        pe.wait_ge(*dve_.at("dp"))
        pe.wait_ge(*act_.at("oN"))
        for g in range(NG):
            turn(bank[4][:, g * RD:(g + 1) * RD], Ed[0:RD, g * P:(g + 1) * P], ident[0:RD, 0:RD])
        for g in range(NG):
            last = turn(bank[4][0:B, 96 + g * RD:96 + (g + 1) * RD], Ed[0:RD, 384 + g * B:384 + (g + 1) * B], ident[0:RD, 0:RD])
        last.then_inc(*pe_.mark("dpt"))
        pe.wait_ge(*dve_.at("PTm"))
        for b in range(B):
            u = 4 * B + b
            pe.wait_ge(*loaded[u % 3].at("use", u))
            for g in range(NG):
                for h in range(HG):
                    last = mm(bank[0][0:RD, 0:P], PTm[:, g, b * HG + h, :],
                              slot(u % 3).rearrange("p k n -> p (k n)")[:, (g * HG + h) * P:(g * HG + h + 1) * P],
                              start=(b == g == h == 0), stop=False)
            last.then_inc(*pe_.mark("used", u))
        for g in range(NG):
            for h in range(HG):
                last = mm(bank[0][0:RD, 0:P], Pn[0:B, g, h, :], tmS[0:B, 6 + DHEADS + g * HG + h, :],
                          start=False, stop=(g == NG - 1 and h == HG - 1))
        last.then_inc(*pe_.mark("pvD"))
        pe.wait_ge(*act_.at("oRd"))
        turn(bank[1][:, 0:RD], oRd[0:RD, :], ident[0:RD, 0:RD]).then_inc(*pe_.mark("oTd"))

        pe.wait_ge(*act_.at("oD"))

        def merge(i, first):
            for s in range(2):
                pe.wait_ge(w_ld["merge"][s], i * 16 + 16)
                if not first:
                    pe.wait_ge(mg_sig, i * 4 + (2 * s - 2))
                for f in range(2):
                    for k in range(KT):
                        last = mm(bank[4 * f + s][:, 0:T], slot(s)[:, k, f * P:(f + 1) * P], hT[:, k, :],
                                  start=(k == 0), stop=(k == KT - 1))
                last.then_inc(mg_gate, 1)
            pe.wait_ge(w_ld["merge"][2], i * 32 + 32)
            if not first:
                pe.wait_ge(mg_t, i * 4)
            for f in range(2):
                for k in range(8):
                    mm(bank[4 * f + 2][:, 0:T], slot(2)[:, k, f * P:(f + 1) * P], oN[:, k, :], start=(k == 0), stop=(k == 7))
                for k in range(4):
                    last = mm(bank[4 * f + 3][:, 0:T], slot(2)[:, 8 + k, f * P:(f + 1) * P], oD[:, k, :],
                              start=(k == 0), stop=(k == 3))
            last.then_inc(mg_y, 1)
        merge(0, True)
        with pe.Fori(1, 8) as i:
            merge(i, False)
        pe.wait_ge(mg_kept, 16)
        pe.wait_ge(mg_sig, 32)
        for i in range(2):
            for s in range(4):
                pe.wait_ge(w_ld["wout"][s], 16 * i + 16)
                if i:
                    pe.wait_ge(wo_kept, 2 * (s + 1))
                for f in range(2):
                    for k in range(KT):
                        last = mm(bank[2 * s + f][:, 0:T], slot(s)[:, k, f * P:(f + 1) * P], mT[:, k, :],
                                  start=(k == 0), stop=(k == KT - 1))
                last.then_inc(wo_done, 1)
        pe.wait_ge(wo_kept, 16)
        stats("n2")

        def split_products(out, a, high, f, k_tiles, x_high, x_low, start, stop, tiles_ready=None):
            w_low = half_chunk(a, k_tiles, f, CW)
            w_high = half_chunk(high, k_tiles)
            for k in range(k_tiles):
                if tiles_ready is not None:
                    pe.wait_ge(*dve_.at(tiles_ready, k))
                mm(out, w_high[:, k, :], half_tile(x_high[k]), start=(start and k == 0), stop=False)
                mm(out, w_high[:, k, :], half_tile(x_low[k]), start=False, stop=False)
                last = mm(out, w_low[:, k, :], half_tile(x_high[k]), start=False, stop=(stop and k == k_tiles - 1))
            return last
        h_low = tiles_at((hT0, KT))
        f_low = tiles_at((region, FT))

        def ffn(i, first):
            for s in range(4):
                if not first:
                    if s % 2:
                        pe.wait_ge(ff_kept, i * 4 + (s - 3))
                    else:
                        pe.wait_ge(ff_silu, i * 4 + (s - 2))
                for f in range(2):
                    pe.wait_ge(ff_low, i * 8 + (2 * s + f + 1))
                    split_products(bank[2 * s + f][:, 0:T], slot_at(s), ffn_high[(2 * s + f) % 4], f, KT, h_high, h_low,
                                   True, True, "h_low" if first and s == f == 0 else None).then_inc(ff_half, 1)
        ffn(0, True)
        with pe.Fori(1, 11) as i:
            ffn(i, False)

        def down(i, u, first, very_first=False):
            if not first:
                pe.wait_ge(dn_kept, i * 4 + (2 * u - 2))
            for s in range(4):
                for f in range(2):
                    pe.wait_ge(dn_low, i * 16 + (8 * u + 2 * s + f + 1))
                    split_products(bank[2 * u + f][:, 0:T], slot_at(s), down_high[(2 * s + f) % 4], f, KD,
                                   f_high[s * KD:(s + 1) * KD], f_low[s * KD:(s + 1) * KD], s == 0, s == 3,
                                   f"f_low{s}" if very_first and f == 0 else None).then_inc(dn_half, 1)
        down(0, 0, True, True)
        down(0, 1, True)
        with pe.Fori(1, 4) as i:
            down(i, 0, False)
            down(i, 1, False)
        pe.wait_ge(dn_kept, 16)
        stats("nf")
        for k in range(KT):
            pe.wait_ge(*dve_.at("yT", k))
            if k >= 4:
                pe.wait_ge(*(dve_ if k % 2 else act_).at("y", k - 4))
            z = bank[k % 4]
            for q in range(QT):
                turn(z[:, q * P:(q + 1) * P], hT[:, k, q * P:(q + 1) * P], ident)
            turn(z[0:B, TP:TP + P], hT[:, k, TP:T], ident).then_inc(*pe_.mark("y", k))

    PARTS = [(h, l) for h in range(2) for l in range(2)]

    def pair_columns(x, half, h, l):
        sh, m = 2 * (x % 4 // 2) + h, 4 * (x % 2) + 2 * half
        return KS[l * DH:(l + 1) * DH, sh * 1024 + m * P:sh * 1024 + (m + 2) * P].rearrange("p (m n) -> p m n", n=P)

    def turned_tokens(x, half, h, l):
        return bank[4 + 2 * (x % 2) + half][h * DH:(h + 1) * DH, :].rearrange("p (m l n) -> p m l n", m=2, l=2)[:, :, l, :]

    @block.scalar
    def _(act):
        A, cp = nc.scalar.activation, nc.scalar.copy
        act.wait_ge(rows_loaded, 8 * 16)
        A(c_silu[0:9, :], c_rows[0:9, :], ACT.Sigmoid).then_inc(*act_.mark("sig"))
        act.wait_ge(*pe_.at("siluT"))
        cp(siluT.rearrange("p j c -> p (j c)"), bank[0][:, 0:KT * 9]).then_inc(*act_.mark("siluT"))
        for k in range(0, KT, 2):
            act.wait_ge(*pe_.at("xT", k))
            cp(xT[:, k, :], bank[2 + k % 4][:, 0:T]).then_inc(*act_.mark("xT", k))

        act.wait_ge(*dve_.at("ada_row"))
        with act.Fori(0, 12) as i:
            for s in range(4):
                act.wait_ge(ada_done, i * 4 + (s + 1))
                cp(ada_row[0:9, s, :], bank[s][0:9, 0:CW]).then_inc(ada_rows, 1)

        def norm(tag, gate):
            act.wait_ge(*dve_.at("ms", tag))
            A(rstd, rstd, ACT.Sqrt).then_inc(*act_.mark("root", tag))
            if gate is None:
                return
            for k in range(KT):
                act.wait_ge(*dve_.at("hs", tag, k))
                A(hT[:, k, 0:TP], hT[:, k, 0:TP], ACT.Identity, bias=modT[:, gate * KT + k, 0:1])\
                    .then_inc(*act_.mark(*(("h", tag) if k == KT - 1 else ("h", tag, k))))
        norm("n1", 0)

        tiles = dict(enumerate(TILES))
        stores = [0, 0]

        def tm(n):
            kind, j = TILES[n]
            if kind not in TURNED:
                return
            act.wait_ge(*pe_.at("tm", n))
            z = bank[6 + n % 2]
            zq = z[:, 0:TP].rearrange("p (q f) -> p q f", q=QT)
            if kind in "kv":
                dst, row = tmN[:, :, 2 * j + (kind == "v"), :], 2 * j + (kind == "v")
            elif kind == "dv":
                dst, row = tmV[:, :, j, :], 6 + DHEADS + j
            else:
                u = (j // 2) % 2
                if j >= 4 and j % 2 == 0:
                    act.wait_ge(*stage_stored[u].last())
                dst, row = stage[:, u, :, (j % 2) * P:(j % 2 + 1) * P], 6 + j
            cp(dst, zq).then_inc(*act_.mark())
            cp(tmS[0:B, row, :], z[0:B, TP:TP + P]).then_inc(*act_.mark("tm", n))
            if kind == "dk" and j % 2:
                u, g, hh = (j // 2) % 2, j // HG, (j % HG) - 1
                act.wait_ge(*act_.last())
                o = o_[f"p_dil{g + 1}"][0, 0]
                if g == 0:
                    act.dma_start(o[:, 0, hh:hh + 2, :].rearrange("t h d -> t (h d)"), stage[:, u, 1, :])\
                        .then_inc(*stage_stored[u].mark(by=16))
                else:
                    act.dma_start(o[:, 0, hh:hh + 2, :].rearrange("(q p) h d -> p q (h d)", p=P), stage[:, u, :, :])\
                        .then_inc(*stage_stored[u].mark(*(("last",) if j >= DHEADS - 4 else ()), by=16))
            if kind == "v":
                act.wait_ge(*act_.last())
                name = ("cmp", "sel", "win")[j]
                act.dma_start(o_["p_" + name][0, 0].rearrange("(q p) s h d -> p q (s h d)", p=P),
                              tmN[:, :, 2 * j:2 * j + 2, :].rearrange("p q j f -> p q (j f)"))\
                    .then_inc(*(cmp_stored.mark("p_cmp", by=16) if j == 0 else rows_stored.mark(by=16)))
                dst = o_["s_" + name][0, :, 0] if j < 2 else o_["s_win"][0, :, WIN - 1]
                act.dma_start(dst.rearrange("b s h d -> b (s h d)"),
                              tmS[0:B, 2 * j:2 * j + 2, :].rearrange("p j f -> p (j f)")).then_inc(*rows_stored.mark(by=16))
            if kind == "dv" and j % HG == HG - 1:
                g = j // HG
                act.wait_ge(*act_.last())
                o = o_[f"p_dil{g + 1}"][0, 0, :, 1]
                if g == 0:
                    act.dma_start(o.rearrange("t h d -> t (h d)"), tmV[:, 1, 0:HG, :].rearrange("p j f -> p (j f)"))\
                        .then_inc(*rows_stored.mark(by=16))
                else:
                    act.dma_start(o.rearrange("(q p) h d -> p q (h d)", p=P),
                                  tmV[:, :, g * HG:(g + 1) * HG, :].rearrange("p q j f -> p q (j f)"))\
                        .then_inc(*rows_stored.mark(by=16))
                for kv in range(2):
                    r = 6 + kv * DHEADS + g * HG
                    act.dma_start(o_[f"s_dil{g + 1}"][0, :, DIL[g][0] - 1, kv].rearrange("b h d -> b (h d)"),
                                  tmS[0:B, r:r + HG, :].rearrange("p j f -> p (j f)"))\
                        .then_inc(*rows_stored.mark(*(("all",) if (g, kv) == (NG - 1, 1) else ()), by=16))

        for n in range(NT + 2):
            if n < NT:
                act.wait_ge(*pe_.at("acc", n))
                if n >= 3:
                    kind = TILES[n - 3][0]
                    if kind in ROPED:
                        act.wait_ge(*dve_.at("roped", n - 3))
                    elif kind in ("v", "dv"):
                        act.wait_ge(*pe_.at("tm", n - 3))
                    else:
                        act.wait_ge(*pe_.at("gateT"))
                m = 48 if n == 0 else P
                cp(tmp[0:m, n % 3, :], bank[n % 4][0:m, 0:T]).then_inc(*act_.mark("raw", n))
            if n == 1:
                act.wait_ge(*pe_.at("gateT"))
                A(gates.rearrange("p q j -> p (q j)"), bank[6][:, 0:96], ACT.Sigmoid).then_inc(*act_.mark())
                A(small[0:B, 0:48], bank[6][0:B, 128:176], ACT.Sigmoid).then_inc(*act_.mark("gateS"))
            if n >= 2:
                tm(n - 2)
        used = {}
        for n in range(NT):
            if TILES[n][0] in TURNED:
                act_.marks["tm_bank", n] = act_.marks[used.get(n % 2, ("gateS",))]
                used[n % 2] = ("tm", n)

        def compress(tag, kTc, nt, kc):
            per = max(1, nt // 4)
            for i in range(0, 4 * per, 2):
                act.wait_ge(*pe_.at("ctr", tag, i))
                w = min(nt, 4) * P
                sh, half = i // per, i % per
                cp(kTc[:, sh, half * 512:half * 512 + w], bank[4 + i % 2][:, 0:w]).then_inc(*act_.mark("ctr", tag, i))
            nb = nt * 16 - 1
            act.wait_ge(*pe_.at("hid", tag))
            cp(cbsh[0:64].rearrange("p (j n) -> p j n", j=4)[:, :, 0:nb],
               bank[0][64:128, :].rearrange("p (j n) -> p j n", j=4)[:, :, 1:nb + 1]).then_inc(*act_.mark("bsh", tag))
            act.wait_ge(*dve_.at("hid", tag))
            A(cgl[0:64].rearrange("p (j n) -> p j n", j=4)[:, :, 0:nb],
              chid[0:64].rearrange("p (j n) -> p j n", j=4)[:, :, 0:nb], ACT.Gelu_apprx_tanh).then_inc(*act_.mark("gelu", tag))
            act.wait_ge(*pe_.at("kvc", tag))
            cp(kc, bank[1][:, 0:nb]).then_inc(*act_.mark("kvc", tag))
        for s in range(2):
            act.wait_ge(*stage_stored[s].last())
        act.wait_ge(*pe_.at("pe"))
        cp(peb[0:64, :], bank[3][0:64, 0:2]).then_inc(*act_.mark("peb"))
        compress("p", kTcP, 1, kcP[:, 0:NBP])

        def pt_copy(u):
            act.wait_ge(*pe_.at("pt", u))
            if u >= 1:
                act.wait_ge(*pe_.at("pv", u - 1))
            bl = blocks(u)
            full = sum(k == P for _, k, _ in bl)
            marks = []
            for c in range(0, full, 4):
                w = min(4, full - c) * P
                marks.append((PT[:, c * P:c * P + w], bank[2 + c // 4][:, 0:w]))
            if full < len(bl):
                n = len(bl) - 1
                marks.append((PT[0:NBP, n * P:(n + 1) * P], bank[2 + n // 4][0:NBP, (n % 4) * P:(n % 4 + 1) * P]))
            for n, (o, s) in enumerate(marks):
                cp(o, s).then_inc(*act_.mark(*(("pt", u) if n == len(marks) - 1 else ())))

        def o_copy(u):
            kind, qt, h = UNITS[u]
            act.wait_ge(*pe_.at("pv", u))
            z = bank[4 + u % 2]
            if kind == "n":
                r = slice((h % 2) * DH, (h % 2 + 1) * DH)
                cp(oN[r, h // 2, qt * P:(qt + 1) * P], z[r, 0:P]).then_inc(*act_.mark("o", u))
            else:
                cp(oD[:, h, qt * P:(qt + 1) * P], z[:, 0:P]).then_inc(*act_.mark("o", u))

        for u in range(NU + 2):
            if u < NU:
                kind, qt, h = UNITS[u]
                W = P * (qt + 1)
                act.wait_ge(*dve_.at("nm", u))
                e = E[:, u % 2, :]
                if kind == "n":
                    for br in range(3):
                        a, z = (br * W, (br + 1) * W) if br < 2 else (2 * W, 2 * W + NBP)
                        A(e[:, a:z], e[:, a:z], ACT.Exp, bias=small[:, 8 * (u % 2) + br:8 * (u % 2) + br + 1], scale=SC_N,
                          accum_out=small[:, 16 + 8 * (u % 2) + br:17 + 8 * (u % 2) + br])\
                            .then_inc(*act_.mark(*(("e", u) if br == 2 else ())))
                else:
                    A(e[:, 0:3 * W], e[:, 0:3 * W], ACT.Exp, bias=small[:, 8 * (u % 2):8 * (u % 2) + 1], scale=SC_D,
                      accum_out=small[:, 16 + 8 * (u % 2):17 + 8 * (u % 2)]).then_inc(*act_.mark("e", u))
            if 1 <= u <= NU:
                pt_copy(u - 1)
            if u >= 2:
                o_copy(u - 2)

        act.wait_ge(*dve_.at("sample_q"))
        NX = 4 * B
        for x in range(NX + 3):
            if x < NX:
                act.wait_ge(*pe_.at("cx", x, 0))
                for h, l in PARTS:
                    cp(pair_columns(x, 0, h, l), turned_tokens(x, 0, h, l)).then_inc(*act_.mark(*(("cx", x) if (h, l) == (1, 1) else ())))
            if x >= 4 and x % 4 == 0:
                b = x // 4 - 1
                act.wait_ge(*pe_.at("hid", b))
                cp(cbsh[0:64].rearrange("p (j n) -> p j n", j=4)[:, :, 0:NBS],
                   bank[b % 2][64:128, :].rearrange("p (j n) -> p j n", j=4)[:, :, 1:NBS + 1]).then_inc(*act_.mark("bsh", b))
                act.wait_ge(*dve_.at("hid", b))
                A(cgl[0:64].rearrange("p (j n) -> p j n", j=4)[:, :, 0:NBS],
                  chid[0:64].rearrange("p (j n) -> p j n", j=4)[:, :, 0:NBS], ACT.Gelu_apprx_tanh).then_inc(*act_.mark("gelu", b))
            if x >= 5 and x % 4 == 1:
                b = x // 4 - 1
                act.wait_ge(*pe_.at("kvc", b))
                cp(kcS[:, 0:NBS], bank[2][:, 0:NBS]).then_inc(*act_.mark())
                cp(vcS[0:NBS, b, :], bank[2][0:NBS, P:2 * P]).then_inc(*act_.mark("kvc", b))
        act.wait_ge(*dve_.at("cm"))
        A(pcmp[:, 0:NBS], bank[3][:, 0:NBS], ACT.Exp, bias=small[:, 1:2], scale=SC_N,
          accum_out=small[:, 2:3]).then_inc(*act_.mark("ce"))
        act.wait_ge(*pe_.at("cpt"))
        cp(ptc[0:NBS, :], bank[1][0:NBS, 0:P]).then_inc(*act_.mark("cpt"))
        for y in range(0, 5 * B, 2):
            act.wait_ge(*pe_.at("ky", y))
            cp(KS[:, (y % 8) * 512:(y % 8 + 1) * 512], bank[4 + y % 3][:, :]).then_inc(*act_.mark("ky", y))
        act.wait_ge(*dve_.at("sm"))
        for br, (a, z) in enumerate(((0, 2056), (2056, 2576))):
            A(SS[:, a:z], SS[:, a:z], ACT.Exp, bias=small[:, 10 + br:11 + br], scale=SC_N,
              accum_out=small[:, 12 + br:13 + br]).then_inc(*act_.mark(*(("se",) if br else ())))
        for i in (0, 2, 4):
            act.wait_ge(*pe_.at("spt", i))
            cp(PTn[:, 4 * i:4 * i + 4, :].rearrange("p j r -> p (j r)"), bank[5 + i % 3][:, :]).then_inc(*act_.mark("pt", "s", i))
        act.wait_ge(*pe_.at("pvS", B - 1))
        for n in range(2):
            cp(oR[0:H, 4 * n:4 * n + 4, :].rearrange("p b f -> p (b f)"), bank[n][0:H, :]).then_inc(*act_.mark())
        act_.marks["oR",] = act_.n
        act.wait_ge(*pe_.at("oT"))
        for kv in range(2):
            for odd in range(2):
                cp(oN[odd * DH:(odd + 1) * DH, kv * 4:kv * 4 + 4, TP:T],
                   bank[4][kv * DH:(kv + 1) * DH, 0:P].rearrange("p (b h) -> p h b", b=B)[:, kv * G + odd:(kv + 1) * G:2, :])\
                    .then_inc(*act_.mark(*(("oN",) if (kv, odd) == (1, 1) else ())))
        for z in range(0, NG * B, 2):
            act.wait_ge(*pe_.at("kz", z))
            cp(KS[:, (z % 8) * 512:(z % 8 + 1) * 512], bank[5 + z % 3][:, :]).then_inc(*act_.mark("kz", z))
        act.wait_ge(*dve_.at("dm"))
        for g in range(NG):
            A(Ed[0:RD, g * P:(g + 1) * P], bank[g][0:RD, 0:P], ACT.Exp, bias=small[0:RD, 24:25], scale=SC_D,
              accum_out=small[0:RD, 28 + g:29 + g]).then_inc(*act_.mark())
        A(Ed[0:RD, 384:408], Ed[0:RD, 384:408], ACT.Exp, bias=small[0:RD, 24:25], scale=SC_D,
          accum_out=small[0:RD, 31:32]).then_inc(*act_.mark("de"))
        act.wait_ge(*pe_.at("pvD"))
        cp(oRd[0:RD, :], bank[0][0:RD, 0:P]).then_inc(*act_.mark("oRd"))
        act.wait_ge(*pe_.at("oTd"))
        cp(oD[:, :, TP:T], bank[1][:, 0:RD].rearrange("p (b h) -> p h b", b=B)).then_inc(*act_.mark("oD"))

        def merge(i, first):
            for s in range(2):
                act.wait_ge(mg_gate, i * 2 + (s + 1))
                for f in range(2):
                    if not first and f == 0 and s == 0:
                        act.wait_ge(mg_t, i * 4)
                    A(sig[:, 2 * s + f, :], bank[4 * f + s][:, 0:T], ACT.Sigmoid).then_inc(mg_sig, 1)
                if s == 0 and not first:
                    act.wait_ge(mg_y, i)
                    act.dma_start(slot(2)[:, 0:8, :], rows(w_bn, bass.ds(i * CW, CW))).then_inc(w_ld["merge"][2], 16)
                    act.dma_start(slot(2)[:, 8:12, :], rows(w_bd, bass.ds(i * CW, CW))).then_inc(w_ld["merge"][2], 16)
        sig = tmp
        merge(0, True)
        with act.Fori(1, 8) as i:
            merge(i, False)
        norm("n2", 3)

        for k in range(KT):
            act.wait_ge(*(act_.at("h", "n2", k) if k < KT - 1 else act_.at("h", "n2")))
            act.wait_ge(*dve_.at("h", "n2"))
            cp(half_tile(h_high[k]), hT[:, k, :]).then_inc(*act_.mark("h_high", k))

        def high(a, buffer, f, k_tiles, done):
            raw = piece(a, SLOT, F32)[:, 0:k_tiles * CW].rearrange("p (k n) -> p k n", n=CW)[:, :, f * P:(f + 1) * P]
            cp(half_chunk(buffer, k_tiles), raw).then_inc(done, 1)

        def ffn(i, first):
            for s in range(4):
                act.wait_ge(w_ld["ffn"][s], i * 16 + 16)
                for f in range(2):
                    n = 2 * s + f
                    if not first or n >= 4:
                        act.wait_ge(ff_half, i * 8 + (n - 3))
                    high(slot_at(s), ffn_high[n % 4], f, KT, ff_high)
                if s < 2:
                    continue
                g = 2 * (s - 2)
                for f in range(2):
                    act.wait_ge(ff_half, i * 8 + (2 * g + f + 1))
                    if not first:
                        act.wait_ge(ff_kept, i * 4 + (g + f - 3))
                    A(tmp[:, g + f, :], bank[2 * g + f][:, 0:T], ACT.Silu).then_inc(ff_silu, 1)
        ffn(0, True)
        with act.Fori(1, 11) as i:
            ffn(i, False)

        def down(i, u, very_first=False):
            for s in range(4):
                act.wait_ge(w_ld["down"][s], i * 32 + (16 * u + 16))
                for f in range(2):
                    n = 2 * s + f
                    if not very_first or n >= 4:
                        act.wait_ge(dn_half, i * 16 + (8 * u + n - 3))
                    high(slot_at(s), down_high[n % 4], f, KD, dn_high)
                    if very_first and f == 0:
                        for k in range(KD):
                            cp(half_tile(f_high[s * KD + k]), fT[:, s * KD + k, :]).then_inc(*act_.mark(f"f_high{s}", k))
        act.wait_ge(ff_half, 88)
        act.wait_ge(ff_kept, 44)
        down(0, 0, True)
        down(0, 1)
        with act.Fori(1, 4) as i:
            down(i, 0)
            down(i, 1)
        norm("nf", None)
        for k in range(0, KT, 2):
            act.wait_ge(*pe_.at("y", k))
            z = bank[k % 4]
            cp(y_tm[:, :, k * P:(k + 1) * P], z[:, 0:TP].rearrange("p (q f) -> p q f", q=QT)).then_inc(*act_.mark())
            cp(y_ts[0:B, k * P:(k + 1) * P], z[0:B, TP:TP + P]).then_inc(*act_.mark("y", k))
        act_.marks["y_out",] = act_.n

    @block.vector
    def _(dve):
        v = nc.vector

        def link(ins):
            ins.then_inc(*dve_.mark())
            dve.wait_ge(*dve_.last())

        v.memset(ada_row, 0.0).then_inc(*dve_.mark("ada_row"))
        dve.wait_ge(rows_loaded, 8 * 16)
        dve.wait_ge(*act_.at("sig"))
        v.tensor_tensor(c_silu[0:9, :], c_rows[0:9, :], c_silu[0:9, :], ALU.mult).then_inc(*dve_.mark("silu"))
        dve.wait_ge(*pe_.at("vecT"))
        v.tensor_copy(biasT, bank[1][:, 0:96]).then_inc(*dve_.mark())
        v.tensor_copy(gT, bank[1][:, 96:144]).then_inc(*dve_.mark("vecT"))
        for k in range(1, KT, 2):
            dve.wait_ge(*pe_.at("xT", k))
            v.tensor_copy(xT[:, k, :], bank[2 + k % 4][:, 0:T]).then_inc(*dve_.mark("xT", k))
        dve_.marks["x_in",] = dve_.n
        dve.wait_ge(*dve_.at("vecT"))

        def ada(i, s):
            dve.wait_ge(ada_turned, i * 4 + (s + 1))
            v.tensor_tensor(modT[:, bass.ds(i * 8 + 2 * s, 2), :], bank[4 + s][:, 0:CW].rearrange("p (f c) -> p f c", f=2)[:, :, 0:9],
                            biasT[:, bass.ds(i * 8 + 2 * s, 2)].unsqueeze(2).broadcast_to([P, 2, 9]), ALU.add).then_inc(ada_kept, 1)
        with dve.Fori(0, 12) as i:
            for s in range(4):
                ada(i, s)
        dve.wait_ge(ada_kept, 48)
        dve.wait_ge(*act_.at("xT", KT - 2))
        dve.wait_ge(*dve_.at("xT", KT - 1))

        def norm(tag, g, shift):
            for k in range(KT):
                if k >= 4:
                    dve.wait_ge(*pe_.at("sq", tag, k - 4))
                v.tensor_tensor(tmp[:, k % 4, :], xT[:, k, :], xT[:, k, :], ALU.mult).then_inc(*dve_.mark("sq", tag, k))
            dve.wait_ge(*pe_.at("sq", tag, KT - 1))
            v.tensor_scalar(rstd, bank[7][:, 0:T], 1.0 / D, EPS, ALU.mult, ALU.add).then_inc(*dve_.mark("ms", tag))
            if shift is not None:
                scale = modT[:, (shift + 1) * KT:(shift + 2) * KT, :]
                link(v.scalar_tensor_tensor(out=facA, in0=scale, scalar=1.0,
                                            in1=gT[:, g * KT:(g + 1) * KT].unsqueeze(2).broadcast_to([P, KT, 9]),
                                            op0=ALU.add, op1=ALU.mult))
            dve.wait_ge(*act_.at("root", tag))
            link(v.reciprocal(rstd, rstd))
            if shift is None:
                for k in range(KT):
                    v.scalar_tensor_tensor(out=hT[:, k, :], in0=xT[:, k, :], scalar=gT[:, g * KT + k:g * KT + k + 1],
                                           in1=rstd, op0=ALU.mult, op1=ALU.mult).then_inc(*dve_.mark("yT", k))
                return
            for k in range(KT):
                v.scalar_tensor_tensor(out=hT[:, k, 0:TP], in0=xT[:, k, 0:TP], scalar=facA[:, k, 0:1],
                                       in1=rstd[:, 0:TP], op0=ALU.mult, op1=ALU.mult).then_inc(*dve_.mark("hs", tag, k))
            hS = hT[:, :, TP:T]
            link(v.tensor_tensor(hS, xT[:, :, TP:T], facA[:, :, 1:9], ALU.mult))
            link(v.tensor_tensor(hS, hS, rstd[:, TP:T].unsqueeze(1).broadcast_to([P, KT, B]), ALU.mult))
            v.tensor_tensor(hS, hS, modT[:, shift * KT:(shift + 1) * KT, 1:9], ALU.add).then_inc(*dve_.mark("h", tag))
        norm("n1", 0, 0)

        roped = []
        for n in range(NT):
            kind, j = TILES[n]
            if n == 1:
                dve.wait_ge(*pe_.at("gateS"))
                g48 = rt[:, 0, 0:48].rearrange("p (j h) -> p j h", j=3)
                link(v.tensor_tensor(g48, bank[7][:, 0:48].rearrange("p (j h) -> p j h", j=3),
                                     const("head_of").unsqueeze(1).broadcast_to([P, 3, H]), ALU.mult))
                link(v.tensor_reduce(gatesS, g48, AX.X, ALU.add))
            if kind not in ROPED:
                continue
            c = "nsa" if kind in "kq" else "dil"
            dve.wait_ge(*act_.at("raw", n))
            if roped:
                dve.wait_ge(*dve_.at("roped", roped[-1]))
            v.tensor_tensor(rt[:, 0, :], tmp[:, n % 3, :], const("cos_" + c), ALU.mult).then_inc(*dve_.mark())
            dve.wait_ge(*pe_.at("rot", n))
            link(v.tensor_tensor(rt[:, 1, :], bank[4 + n % 2][:, 0:T], const("sin_" + c), ALU.mult))
            if kind == "q":
                kv = j // 4
                for odd in range(2):
                    r = slice(odd * DH, (odd + 1) * DH)
                    last = v.tensor_tensor(qK[kv * DH:(kv + 1) * DH, (2 * j + odd) % G, :], rt[r, 0, :], rt[r, 1, :], ALU.add)
                    last.then_inc(*dve_.mark(*(("roped", n) if odd else ())))
            else:
                dst = {"k": lambda: kT[:, j, :], "dq": lambda: dqk[:, j, :], "dk": lambda: dqk[:, DHEADS + j, :]}[kind]()
                v.tensor_tensor(dst, rt[:, 0, :], rt[:, 1, :], ALU.add).then_inc(*dve_.mark("roped", n))
            roped.append(n)
        for n in roped:
            before = [m for m in roped if m < n and m % 2 == n % 2]
            dve_.marks["rope_bank", n] = dve_.marks["roped", before[-1]] if before else 1

        def compress(tag, kTc, nt, vc):
            per = max(1, nt // 4)
            for i in range(1, 4 * per, 2):
                dve.wait_ge(*pe_.at("ctr", tag, i))
                w = min(nt, 4) * P
                sh, half = i // per, i % per
                v.tensor_copy(kTc[:, sh, half * 512:half * 512 + w], bank[4 + i % 2][:, 0:w]).then_inc(*dve_.mark("ctr", tag, i))
            nb = nt * 16 - 1
            dve.wait_ge(*act_.at("bsh", tag))
            dve.wait_ge(*act_.at("peb"))
            for s in range(2):
                v.scalar_tensor_tensor(out=chid[0:64].rearrange("p (j n) -> p j n", j=4)[:, 2 * s:2 * s + 2, 0:nb],
                                       in0=bank[0][0:64, :].rearrange("p (j n) -> p j n", j=4)[:, 2 * s:2 * s + 2, 0:nb],
                                       scalar=peb[0:64, s:s + 1],
                                       in1=cbsh[0:64].rearrange("p (j n) -> p j n", j=4)[:, 2 * s:2 * s + 2, 0:nb],
                                       op0=ALU.add, op1=ALU.add).then_inc(*dve_.mark(*(("hid", tag) if s else ())))
            dve.wait_ge(*pe_.at("kvc", tag))
            v.tensor_copy(vc, bank[2][0:nb, 0:P]).then_inc(*dve_.mark("kvc", tag))
        compress("p", kTcP, 1, vcP[0:NBP, :])

        for u in range(NU):
            kind, qt, h = UNITS[u]
            W = P * (qt + 1)
            c = 8 * (u % 2)
            mx, nm, den = small[:, 32:35], small[:, c:c + 3], small[:, 16 + c:19 + c]
            e = E[:, u % 2, :]
            if u == 0:
                dve.wait_ge(*act_.at("kvc", "p"))
            if u >= 2:
                dve.wait_ge(*pe_.at("pt", u - 2))
            dve.wait_ge(*pe_.at("s", u))
            if kind == "n":
                mask = const("causal")[:, 0:P] if qt == 0 else const("causal")[:, P:3 * P]
                for br in range(2):
                    v.tensor_tensor_reduce(e[:, br * W:(br + 1) * W], bank[0][:, br * W:(br + 1) * W], mask, 1.0, -3e38,
                                           ALU.add, ALU.max, mx[:, br:br + 1]).then_inc(*dve_.mark())
                v.tensor_tensor_reduce(e[:, 2 * W:2 * W + NBP], bank[1][:, 0:NBP], const("cmp_add")[:, qt * NBP:(qt + 1) * NBP],
                                       1.0, -3e38, ALU.add, ALU.max, mx[:, 2:3]).then_inc(*dve_.mark("max", u))
                dve.wait_ge(*dve_.last())
                v.tensor_scalar(nm, mx, -SC_N, None, ALU.mult).then_inc(*dve_.mark("nm", u))
                dve.wait_ge(*act_.at("e", u))
                link(v.tensor_tensor_reduce(e[:, 2 * W:2 * W + NBP], e[:, 2 * W:2 * W + NBP],
                                            const("cmp_mul")[:, qt * NBP:(qt + 1) * NBP], 1.0, 0.0, ALU.mult, ALU.add,
                                            den[:, 2:3]))
                link(v.tensor_scalar(den, den, 1e-30, None, ALU.max))
                link(v.reciprocal(den, den))
                g3 = gates[:, qt, :].rearrange("p (r h) -> p r h", h=H)[:, :, h]
                v.tensor_tensor(den[:, 0:2], den[:, 0:2], g3[:, 1:3], ALU.mult).then_inc(*dve_.mark())
                link(v.tensor_tensor(den[:, 2:3], den[:, 2:3], g3[:, 0:1], ALU.mult))
                for br in range(3):
                    a, z = (br * W, (br + 1) * W) if br < 2 else (2 * W, 2 * W + NBP)
                    v.tensor_scalar(e[:, a:z], e[:, a:z], den[:, br:br + 1], None, ALU.mult)\
                        .then_inc(*dve_.mark(*(("p", u) if br == 2 else ())))
            else:
                mask = const("dilmask")[:, 0:3 * P] if qt == 0 else const("dilmask")[:, 3 * P:9 * P]
                v.tensor_tensor_reduce(e[:, 0:2 * W], bank[0][:, 0:2 * W], mask[:, 0:2 * W], 1.0, -3e38, ALU.add, ALU.max,
                                       mx[:, 0:1]).then_inc(*dve_.mark())
                v.tensor_tensor_reduce(e[:, 2 * W:3 * W], bank[1][:, 0:W], mask[:, 2 * W:3 * W], 1.0, -3e38, ALU.add, ALU.max,
                                       mx[:, 1:2]).then_inc(*dve_.mark("max", u))
                dve.wait_ge(*dve_.last())
                link(v.tensor_tensor(mx[:, 0:1], mx[:, 0:1], mx[:, 1:2], ALU.max))
                v.tensor_scalar(nm[:, 0:1], mx[:, 0:1], -SC_D, None, ALU.mult).then_inc(*dve_.mark("nm", u))
                dve.wait_ge(*act_.at("e", u))
                link(v.reciprocal(den[:, 0:1], den[:, 0:1]))
                v.tensor_scalar(e[:, 0:3 * W], e[:, 0:3 * W], den[:, 0:1], None, ALU.mult).then_inc(*dve_.mark("p", u))

        dve.wait_ge(*pe_.at("pv", NU - 1))
        dve.wait_ge(*rows_stored.at("all"))
        dve.wait_ge(*cmp_stored.at("p_cmp"))
        v.memset(qbd, 0.0).then_inc(*dve_.mark())
        v.memset(imp[0:H, :], 0.0).then_inc(*dve_.mark())
        dve.wait_ge(pages_loaded, 8 * 16)
        v.scalar_tensor_tensor(out=runs[:], in0=pages[:], scalar=8.0, in1=const("part8").broadcast_to([P, B]),
                               op0=ALU.mult, op1=ALU.add).then_inc(*dve_.mark("runs"))
        link(v.memset(qfull, 0.0))
        q16 = qfull.rearrange("p (b h) -> p b h", h=H)
        for kv in range(2):
            r = slice(kv * DH, (kv + 1) * DH)
            v.tensor_copy(q16[r, :, kv * G:(kv + 1) * G], qK[r, :, TP:T].rearrange("p g b -> p b g")).then_inc(*dve_.mark())
        dve.wait_ge(*dve_.last())
        for b in range(B):
            v.tensor_copy(qbd[:, b, b * H:(b + 1) * H], q16[:, b, :]).then_inc(*dve_.mark())
        v.tensor_copy(dqnew, dqk[:, 0:DHEADS, TP:T]).then_inc(*dve_.mark())
        v.tensor_copy(dknew, dqk[:, DHEADS:2 * DHEADS, TP:T]).then_inc(*dve_.mark())
        v.tensor_copy(knew, kT[:, 1:3, TP:T]).then_inc(*dve_.mark("sample_q"))
        dve.wait_ge(*dve_.last())

        NX = 4 * B
        for x in range(NX + 3):
            if x < NX:
                dve.wait_ge(*pe_.at("cx", x, 1))
                for h, l in PARTS:
                    v.tensor_copy(pair_columns(x, 1, h, l), turned_tokens(x, 1, h, l)).then_inc(*dve_.mark(*(("cx", x) if (h, l) == (1, 1) else ())))
            if x >= 4 and x % 4 == 0:
                b = x // 4 - 1
                dve.wait_ge(*act_.at("bsh", b))
                for s in range(2):
                    v.scalar_tensor_tensor(out=chid[0:64].rearrange("p (j n) -> p j n", j=4)[:, 2 * s:2 * s + 2, 0:NBS],
                                           in0=bank[b % 2][0:64, :].rearrange("p (j n) -> p j n", j=4)[:, 2 * s:2 * s + 2, 0:NBS],
                                           scalar=peb[0:64, s:s + 1],
                                           in1=cbsh[0:64].rearrange("p (j n) -> p j n", j=4)[:, 2 * s:2 * s + 2, 0:NBS],
                                           op0=ALU.add, op1=ALU.add).then_inc(*dve_.mark(*(("hid", b) if s else ())))
        dve.wait_ge(*pe_.at("cs", B - 1))
        link(v.tensor_reduce(small[:, 0:1], bank[3][:, 0:NBS], AX.X, ALU.max))
        v.tensor_scalar(small[:, 1:2], small[:, 0:1], -SC_N, None, ALU.mult).then_inc(*dve_.mark("cm"))
        dve.wait_ge(*act_.at("ce"))
        link(v.tensor_scalar(small[:, 2:3], small[:, 2:3], 1e-30, None, ALU.max))
        link(v.reciprocal(small[:, 2:3], small[:, 2:3]))
        v.tensor_scalar(pcmp[:, 0:NBS], pcmp[:, 0:NBS], small[:, 2:3], None, ALU.mult).then_inc(*dve_.mark("cp"))
        dve.wait_ge(*pe_.at("imp"))
        v.tensor_scalar(pcmp[:, 0:NBS], pcmp[:, 0:NBS], gatesS[:, 0:1], None, ALU.mult).then_inc(*dve_.mark("cpg"))
        dve.wait_ge(sample_const, 32)
        link(v.tensor_copy(imp[0:H, 0:NBS], bank[0][0:H, 0:NBS]))
        sc, rank = sel[0:H, 1, :], sel[0:H, 2, :]
        link(v.tensor_reduce(sc, imp[0:H, :].rearrange("p (j r) -> p j r", r=4), AX.X, ALU.add))
        link(v.tensor_tensor(sel[0:H, 1, 1:NSEL], sel[0:H, 1, 1:NSEL],
                             imp[0:H, :].rearrange("p (j r) -> p j r", r=4)[:, 0:NSEL - 1, 3], ALU.add))
        link(v.tensor_tensor(sc, sc, const("keep")[0:H], ALU.mult))
        link(v.tensor_tensor(sc, sc, const("force")[0:H], ALU.add))
        mine = sc.unsqueeze(2).broadcast_to([H, NSEL, NSEL])
        other = sc.unsqueeze(1).broadcast_to([H, NSEL, NSEL])
        before = const("before")[0:H].rearrange("p (j i) -> p j i", i=NSEL)
        link(v.tensor_tensor(rk[0:H], other, mine, ALU.is_equal))
        link(v.tensor_tensor(rk[0:H], rk[0:H], before, ALU.mult))
        link(v.tensor_reduce(rank, rk[0:H], AX.X, ALU.add))
        link(v.tensor_tensor(rk[0:H], other, mine, ALU.is_gt))
        link(v.tensor_reduce(sel[0:H, 3, :], rk[0:H], AX.X, ALU.add))
        link(v.tensor_tensor(rank, rank, sel[0:H, 3, :], ALU.add))
        v.tensor_scalar(sel[0:H, 0, :], rank, float(TOPK), None, ALU.is_lt).then_inc(*dve_.mark("sel"))
        dve.wait_ge(*pe_.at("spread"))
        v.tensor_scalar(am, bank[0][:, 256:256 + NSEL], -1.0, -NEG, ALU.add, ALU.mult).then_inc(*dve_.mark("am"))
        dve.wait_ge(*dve_.last())

        for y in range(1, 5 * B, 2):
            dve.wait_ge(*pe_.at("ky", y))
            v.tensor_copy(KS[:, (y % 8) * 512:(y % 8 + 1) * 512], bank[4 + y % 3][:, :]).then_inc(*dve_.mark("ky", y))
        for i in range(4):
            dve.wait_ge(*pe_.at("sy", 5 * (B - 1) + i))
            mask = am[:, 0:32].unsqueeze(1).unsqueeze(3).broadcast_to([P, 4, 32, 4])
            v.tensor_tensor(SS[:, i * 512:(i + 1) * 512].rearrange("p (t j k) -> p t j k", t=4, k=4),
                            bank[i][:, :].rearrange("p (t j k) -> p t j k", t=4, k=4), mask, ALU.add).then_inc(*dve_.mark())
        dve.wait_ge(*pe_.at("sy", 5 * B - 1))
        v.tensor_copy(SS[:, 2056:2568], bank[7][:, :]).then_inc(*dve_.mark())
        dve.wait_ge(*pe_.at("snew"))
        for br, c in enumerate((2048, 2568)):
            v.tensor_tensor(SS[:, c:c + B], bank[4][:, br * B:(br + 1) * B], const("new_nsa"), ALU.add).then_inc(*dve_.mark())
        dve.wait_ge(*dve_.last())
        v.tensor_reduce(small[:, 8:9], SS[:, 0:2056], AX.X, ALU.max).then_inc(*dve_.mark())
        link(v.tensor_reduce(small[:, 9:10], SS[:, 2056:2576], AX.X, ALU.max))
        v.tensor_scalar(small[:, 10:12], small[:, 8:10], -SC_N, None, ALU.mult).then_inc(*dve_.mark("sm"))
        dve.wait_ge(*act_.at("se"))
        link(v.tensor_scalar(small[:, 12:14], small[:, 12:14], 1e-30, None, ALU.max))
        link(v.reciprocal(small[:, 12:14], small[:, 12:14]))
        link(v.tensor_tensor(small[:, 12:14], small[:, 12:14], gatesS[:, 1:3], ALU.mult))
        v.tensor_scalar(SS[:, 0:2056], SS[:, 0:2056], small[:, 12:13], None, ALU.mult).then_inc(*dve_.mark())
        v.tensor_scalar(SS[:, 2056:2576], SS[:, 2056:2576], small[:, 13:14], None, ALU.mult).then_inc(*dve_.mark("sp"))
        for i in (1, 3):
            dve.wait_ge(*pe_.at("spt", i))
            v.tensor_copy(PTn[:, 4 * i:4 * i + 4, :].rearrange("p j r -> p (j r)"), bank[5 + i % 3][:, :]).then_inc(*dve_.mark("pt", "s", i))
        dve.wait_ge(*pe_.at("spt", 5))
        v.tensor_copy(PTn[0:B, 20:22, :].rearrange("p j r -> p (j r)"), bank[4][0:B, 0:2 * P]).then_inc(*dve_.mark("pt", "s", 5))

        dve.wait_ge(*pe_.at("oT"))
        link(v.memset(qn, 0.0))
        for h in range(HG):
            v.tensor_copy(qn.rearrange("p j (b m) -> p j b m", m=HG)[:, h:DHEADS:HG, :, h], dqnew[:, h:DHEADS:HG, :])\
                .then_inc(*dve_.mark())
        link(v.memset(qpad, 0.0))
        for b in range(B):
            v.tensor_copy(qpad[:, :, b, b * HG:(b + 1) * HG], qn[:, :, b * HG:(b + 1) * HG])\
                .then_inc(*dve_.mark(*(("qpad",) if b == B - 1 else ())))
        for z in range(1, NG * B, 2):
            dve.wait_ge(*pe_.at("kz", z))
            v.tensor_copy(KS[:, (z % 8) * 512:(z % 8 + 1) * 512], bank[5 + z % 3][:, :]).then_inc(*dve_.mark("kz", z))
        dve.wait_ge(*pe_.at("dnew"))
        v.tensor_tensor(Ed[0:RD, 384:408].rearrange("p (g k) -> p g k", g=NG), bank[3][0:RD, 0:NG * B].rearrange("p (g k) -> p g k", g=NG),
                        const("new_dil")[0:RD].unsqueeze(1).broadcast_to([RD, NG, B]), ALU.add).then_inc(*dve_.mark())
        for g in range(NG):
            v.tensor_reduce(small[0:RD, 24 + g:25 + g], bank[g][0:RD, 0:P], AX.X, ALU.max).then_inc(*dve_.mark())
        dve.wait_ge(*dve_.last())
        link(v.tensor_reduce(small[0:RD, 27:28], Ed[0:RD, 384:408], AX.X, ALU.max))
        link(v.tensor_reduce(small[0:RD, 32:33], small[0:RD, 24:28], AX.X, ALU.max))
        v.tensor_scalar(small[0:RD, 24:25], small[0:RD, 32:33], -SC_D, None, ALU.mult).then_inc(*dve_.mark("dm"))
        dve.wait_ge(*act_.at("de"))
        link(v.tensor_reduce(small[0:RD, 33:34], small[0:RD, 28:32], AX.X, ALU.add))
        link(v.reciprocal(small[0:RD, 33:34], small[0:RD, 33:34]))
        v.tensor_scalar(Ed[0:RD, :], Ed[0:RD, :], small[0:RD, 33:34], None, ALU.mult).then_inc(*dve_.mark("dp"))
        dve.wait_ge(*pe_.at("dpt"))
        dve.wait_ge(sample_const, 48)
        for g in range(NG):
            v.tensor_tensor(PTm[:, g], bank[4][:, g * RD:(g + 1) * RD].unsqueeze(2).broadcast_to([P, RD, RD]),
                            const("eye").rearrange("p (r c) -> p r c", r=RD), ALU.mult).then_inc(*dve_.mark())
        for g in range(NG):
            v.tensor_tensor(Pn[0:B, g], bank[4][0:B, 96 + g * RD:96 + (g + 1) * RD].unsqueeze(1).broadcast_to([B, HG, RD]),
                            const("head_cols")[0:B].rearrange("p (h r) -> p h r", h=HG), ALU.mult)\
                .then_inc(*dve_.mark(*(("PTm",) if g == NG - 1 else ())))

        def merge(i):
            dve.wait_ge(mg_y, i + 1)
            dve.wait_ge(mg_sig, i * 4 + 4)
            for f in range(2):
                for s in range(2):
                    v.tensor_tensor(prod[:, 2 * f + s, :], tmp[:, 2 * s + f, :], bank[4 * f + 2 + s][:, 0:T], ALU.mult).then_inc(mg_t, 1)
            dve.wait_ge(mg_t, i * 4 + 4)
            for f in range(2):
                v.tensor_tensor(mT[:, bass.ds(i * 2 + f, 1), :], prod[:, 2 * f, :].unsqueeze(1), prod[:, 2 * f + 1, :].unsqueeze(1),
                                ALU.add).then_inc(mg_kept, 1)
            dve.wait_ge(mg_kept, i * 2 + 2)
        with dve.Fori(0, 8) as i:
            merge(i)

        def residual(j, z, gate, products, n_products, kept):
            one = bass.ds(j, 1)
            v.tensor_tensor(xs8, z[:, TP:T].unsqueeze(1), modT[:, bass.ds(j + gate * KT, 1), 1:9], ALU.mult).then_inc(products, 1)
            v.scalar_tensor_tensor(out=xT[:, one, 0:TP], in0=z[:, 0:TP].unsqueeze(1), scalar=modT[:, bass.ds(j + gate * KT, 1), 0],
                                   in1=xT[:, one, 0:TP], op0=ALU.mult, op1=ALU.add).then_inc(products, 1)
            dve.wait_ge(products, n_products)
            v.tensor_tensor(xT[:, one, TP:T], xT[:, one, TP:T], xs8, ALU.add).then_inc(kept, 1)
        for i in range(2):
            for s in range(4):
                dve.wait_ge(wo_done, 4 * i + s + 1)
                for f in range(2):
                    j = 8 * i + 2 * s + f
                    if j:
                        dve.wait_ge(wo_kept, j)
                    residual(j, bank[2 * s + f], 2, wo_t, 2 * (j + 1), wo_kept)
        dve.wait_ge(wo_kept, 16)
        norm("n2", 1, 3)

        def low_tile(a, raw, high_at):
            return v.tensor_tensor(half_tile(a), raw, half_tile(high_at).bitcast(F32), ALU.subtract)

        def low(a, buffer, f, k_tiles, done):
            raw = piece(a, SLOT, F32)[:, 0:k_tiles * CW].rearrange("p (k n) -> p k n", n=CW)[:, :, f * P:(f + 1) * P]
            v.tensor_tensor(half_chunk(a, k_tiles, f, CW), raw, half_chunk(buffer, k_tiles).bitcast(F32), ALU.subtract)\
                .then_inc(done, 1)

        def h_tiles():
            for k in range(KT):
                dve.wait_ge(*act_.at("h_high", k))
                low_tile(hT0 + k * T, hT[:, k, :], h_high[k]).then_inc(*dve_.mark("h_low", k))

        def hidden(i, g):
            dve.wait_ge(ff_half, i * 8 + (2 * g + 4))
            dve.wait_ge(ff_silu, i * 4 + (g + 2))
            for f in range(2):
                v.tensor_tensor(fT[:, bass.ds(i * 4 + g + f, 1), :], tmp[:, g + f, :].unsqueeze(1),
                                bank[2 * g + 2 + f][:, 0:T].unsqueeze(1), ALU.mult).then_inc(ff_kept, 1)

        def ffn(i, first):
            for s in range(4):
                for f in range(2):
                    dve.wait_ge(ff_high, i * 8 + (2 * s + f + 1))
                    low(slot_at(s), ffn_high[(2 * s + f) % 4], f, KT, ff_low)
                if first and s == 0:
                    h_tiles()
                if s == 0 and not first:
                    hidden(i + (-1), 2)
                if s == 3:
                    hidden(i, 0)
        ffn(0, True)
        with dve.Fori(1, 11) as i:
            ffn(i, False)
        hidden(10, 2)

        def down_low(i, u, s, very_first=False):
            for f in range(2):
                dve.wait_ge(dn_high, i * 16 + (8 * u + 2 * s + f + 1))
                low(slot_at(s), down_high[(2 * s + f) % 4], f, KD, dn_low)
                if very_first and f == 0:
                    for k in range(KD):
                        dve.wait_ge(*act_.at(f"f_high{s}", k))
                        low_tile(region + (s * KD + k) * T, fT[:, s * KD + k, :], f_high[s * KD + k])\
                            .then_inc(*dve_.mark(f"f_low{s}", k))

        def down_residual(c, kept_before):
            i, u = c
            dve.wait_ge(dn_half, i * 16 + (8 * u + 8))
            for f in range(2):
                if kept_before or f:
                    dve.wait_ge(dn_kept, i * 4 + (2 * u + f))
                residual(i * 4 + (2 * u + f), bank[2 * u + f], 5, dn_t, i * 8 + (4 * u + 2 * f + 2), dn_kept)

        def down(i, u, before, kept_before=True, very_first=False):
            for s in range(4):
                down_low(i, u, s, very_first)
                if s == 1 and before is not None:
                    down_residual(before, kept_before)
        down(0, 0, None, very_first=True)
        down(0, 1, (0, 0), False)
        with dve.Fori(1, 4) as i:
            down(i, 0, (i + (-1), 1))
            down(i, 1, (i, 0))
        down_residual((3, 1), True)
        dve.wait_ge(dn_kept, 16)
        norm("nf", 2, None)
        for k in range(1, KT, 2):
            dve.wait_ge(*pe_.at("y", k))
            z = bank[k % 4]
            v.tensor_copy(y_tm[:, :, k * P:(k + 1) * P], z[:, 0:TP].rearrange("p (q f) -> p q f", q=QT)).then_inc(*dve_.mark())
            v.tensor_copy(y_ts[0:B, k * P:(k + 1) * P], z[0:B, TP:TP + P]).then_inc(*dve_.mark("y", k))
        dve_.marks["y_out",] = dve_.n

    return {name: s.marks for name, s in signals.items()}


def kernel(**inputs):
    from concourse import bacc
    from concourse.bass_utils import run_bass_kernel_spmd

    seen = None
    for _ in range(2):
        nc = bacc.Bacc("TRN2", target_bir_lowering=False, num_devices=1)
        ins = {n: nc.dram_tensor("in_" + n, s, I32 if n == "page_table" else F32, kind="ExternalInput").ap()
               for n, s in INS.items()}
        ins["const"] = nc.dram_tensor("in_const", (P, CONST_W), F32, kind="ExternalInput").ap()
        outs = {n: nc.dram_tensor("out_" + n, s, F32, kind="ExternalOutput").ap() for n, s in OUTS.items()}
        with ExitStack() as ctx:
            seen = program(nc, ins, outs, ctx, seen)
    arrays = {"in_" + n: np.ascontiguousarray(inputs[n]) for n in INS}
    arrays["in_const"] = constants()
    r = run_bass_kernel_spmd(nc, [arrays], core_ids=[0])
    return tuple(r.results[0]["out_" + n] for n in OUTS)
```

```python
from contextlib import ExitStack

import numpy as np

import concourse.bass as bass
import concourse.mybir as mybir
from concourse.alu_op_type import AluOpType as ALU

F32 = mybir.dt.float32
F32R = mybir.dt.float32r
I32 = mybir.dt.int32
U32 = mybir.dt.uint32
ACT = mybir.ActivationFunctionType
AX = mybir.AxisListType

P = 128
D = 2048
KT = D // P
RD = 32
TP, B = 256, 8
T = TP + B
QT = TP // P
PAST, PAGE = 2048, 128
NPG = PAST // PAGE
H, KVH, DH = 16, 2, 64
G = H // KVH
BLK, STRIDE, SELB, TOPK = 32, 16, 64, 16
NBP = TP // STRIDE - 1
NBS = PAST // STRIDE - 1
NSEL = PAST // SELB + 1
WIN = 512
DIL = ((128, 1), (512, 4), (2048, 16))
NG, HG, DD = 3, 4, 128
DHEADS = NG * HG
FF = 5632
FT = FF // P
Q_W, KV_W, GATE_W = H * DH, 3 * 2 * KVH * DH, 3 * H
C_KV, C_GATE = Q_W, Q_W + KV_W
C_DIL = C_GATE + GATE_W
C_MERGE = C_DIL + 3 * DHEADS * DD
PROJ_W = C_MERGE + 2 * D
CW = 256
SLOT = KT * CW
NEG = -1e30
SC_N, SC_D = DH ** -0.5, DD ** -0.5
EPS = 1e-6

CONST = {}
S0 = "new_nsa"
_c = 0
for _n, _w in (("ident", P), ("rot_nsa", P), ("rot_dil", P), ("ones", P), ("cos_nsa", T), ("sin_nsa", T),
               ("cos_dil", T), ("sin_dil", T), ("causal", 3 * P), ("dilmask", 9 * P),
               ("cmp_add", QT * NBP), ("cmp_mul", QT * NBP), ("part8", 1), ("rowsel", P), ("head_of", H),
               ("new_nsa", B), ("new_dil", B), ("group", B * KVH), ("spread", P), ("keep", NSEL), ("force", NSEL),
               ("head_cols", HG * RD), ("before", NSEL * NSEL), ("eye", RD * RD)):
    CONST[_n] = (_c, _w)
    _c += _w
CONST_W = _c
CONST_P = CONST[S0][0]


def constants():
    out = np.zeros((P, CONST_W), np.float32)

    def put(name, a):
        a = np.asarray(a, np.float32).reshape(a.shape[0], -1)
        c, w = CONST[name]
        out[:a.shape[0], c:c + w] = a

    put("ident", np.eye(P))
    put("ones", np.ones((P, P)))
    pos = np.concatenate([np.arange(TP), np.full(B, PAST)]).astype(np.float32)
    for name, dh in (("nsa", DH), ("dil", DD)):
        rd = dh // 4
        half = rd // 2
        inv = np.float32(500000.0) ** (-np.arange(half, dtype=np.float32) * np.float32(2.0 / rd))
        ang = (pos[:, None] * inv[None, :].astype(np.float32)).astype(np.float32)
        rot, cos, sin = np.zeros((P, P)), np.ones((P, T)), np.zeros((P, T))
        for base in range(0, P, dh):
            for i in range(half):
                rot[base + i + half, base + i] = -1
                rot[base + i, base + i + half] = 1
                for r in (base + i, base + i + half):
                    cos[r], sin[r] = np.cos(ang[:, i]), np.sin(ang[:, i])
        put("rot_" + name, rot)
        put("cos_" + name, cos)
        put("sin_" + name, sin)
    q, k = np.arange(TP)[:, None], np.arange(TP)[None, :]
    ok = [k <= q] + [(k <= q) & (q - k <= w) & ((q - k) % d == 0) for w, d in DIL]
    add = [np.where(m, 0.0, NEG) for m in ok]
    put("causal", np.concatenate([add[0][:P, :P], add[0][P:, :]], 1))
    put("dilmask", np.concatenate([m[:P, :P] for m in add[1:]] + [m[P:, :] for m in add[1:]], 1))
    kend = np.arange(NBP) * STRIDE + BLK - 1
    seen = (kend[None, :] <= np.arange(TP)[:, None]).reshape(QT, P, NBP).transpose(1, 0, 2)
    put("cmp_add", np.where(seen, 0.0, NEG))
    put("cmp_mul", seen.astype(np.float32))
    own = np.where(np.eye(B, dtype=bool), 0.0, NEG)
    row = np.arange(P)
    put("part8", row[:, None] % 8)
    put("rowsel", row[None, :] // H == np.arange(B)[:, None])
    put("head_of", row[:, None] % H == np.arange(H)[None, :])
    put("new_nsa", own[row // H])
    rd = np.arange(RD)
    put("new_dil", own[rd // HG])
    group = (row // G)[:, None] == np.arange(B * KVH)[None, :]
    put("group", group)
    put("spread", group.T)
    forced = np.zeros(NSEL)
    forced[[0, NSEL - 2, NSEL - 1]] = 1
    put("keep", np.broadcast_to(1 - forced, (H, NSEL)))
    put("force", np.broadcast_to(forced * 1e6, (H, NSEL)))
    put("head_cols", np.broadcast_to(rd[None, :] % HG == np.arange(HG)[:, None], (B, HG, RD)))
    j = np.arange(NSEL)
    put("before", np.broadcast_to(j[None, :] < j[:, None], (H, NSEL, NSEL)))
    put("eye", np.broadcast_to(np.eye(RD), (P, RD, RD)))
    return out


class Signal:

    def __init__(self, sem, seen):
        self.sem, self.seen, self.marks, self.n = sem, seen, {}, 0

    def mark(self, *key, by=1):
        self.n += by
        if key:
            assert key not in self.marks, key
            self.marks[key] = self.n
        return self.sem, by

    def at(self, *key):
        if self.seen is None:
            return self.sem, 1
        return self.sem, self.seen[key]

    def last(self):
        return self.sem, self.n


INS = {"x_prompt": (1, TP, D), "x_sample": (B, 1, D), "cache_cmp_kv": (1, 160, PAGE, 2, KVH, DH),
       "cache_sel_kv": (1, 160, PAGE, 2, KVH, DH), "cache_win_kv": (1, B, WIN, 2, KVH, DH),
       "cache_dil1_kv": (1, B, 128, 2, HG, DD), "cache_dil2_kv": (1, B, 512, 2, HG, DD),
       "cache_dil3_kv": (1, B, 2048, 2, HG, DD), "page_table": (B, NPG), "c_prompt": (1, D),
       "c_sample": (B, D), "w_ada": (1, D, 6 * D), "b_ada": (1, 6 * D), "norm1_g": (1, D),
       "w_in": (1, D, PROJ_W), "cmp_w1": (1, 2, BLK, DH, 64), "cmp_w2": (1, 2, 64, DH),
       "cmp_pe": (1, 2, BLK, DH), "w_br_nsa": (1, H * DH, D), "w_br_dil": (1, HG * DD, D),
       "w_out": (1, D, D), "norm2_g": (1, D), "w_gate": (1, D, FF), "w_up": (1, D, FF),
       "w_down": (1, FF, D), "normf_g": (D,)}
NSA_ROW, DIL_ROW = (2, KVH, DH), (2, HG, DD)
OUTS = {"y_prompt": (1, TP, D), "y_sample": (B, 1, D), "p_cmp": (1, 1, TP) + NSA_ROW,
        "p_sel": (1, 1, TP) + NSA_ROW, "p_win": (1, 1, TP) + NSA_ROW, "p_dil1": (1, 1, P) + DIL_ROW,
        "p_dil2": (1, 1, TP) + DIL_ROW, "p_dil3": (1, 1, TP) + DIL_ROW,
        "s_cmp": (1, B, 1) + NSA_ROW, "s_sel": (1, B, 1) + NSA_ROW, "s_win": (1, B, WIN) + NSA_ROW,
        "s_dil1": (1, B, 128) + DIL_ROW, "s_dil2": (1, B, 512) + DIL_ROW, "s_dil3": (1, B, 2048) + DIL_ROW}


def program(nc, i_, o_, ctx, seen):
    signals = {}

    def sem(name):
        return ctx.enter_context(nc.semaphore(name))

    def signal(name):
        signals[name] = Signal(sem(name), None if seen is None else seen[name])
        return signals[name]

    WORDS = 53192
    mem_at = -(-nc.sbuf_base // 32) * 32
    mem = ctx.enter_context(nc.sbuf_tensor("mem", [P, WORDS], F32))
    pieces = {}

    def piece(a, words, dtype):
        if (a, words, dtype) not in pieces:
            pieces[a, words, dtype] = nc.alloc_sbuf_tensor_at(f"piece{len(pieces)}", [P, words], dtype, offset=mem_at + 4 * a)
        return pieces[a, words, dtype]
    top = [0]

    def part(words, at=None):
        a = top[0] if at is None else at
        if at is None:
            top[0] += -(-words // 8) * 8
        assert a + words <= WORDS, (a + words, WORDS)
        return mem[:, a:a + words]

    c_all = part(CONST_P)

    def const(name):
        c, w = CONST[name]
        if c < CONST_P:
            return c_all[:, c:c + w]
        return {"before": before_c, "eye": eye_c}.get(name) if name in ("before", "eye") \
            else c_sample[:, c - CONST_P:c - CONST_P + w]

    ident, ones = const("ident"), const("ones")
    biasT = part(96)
    gT = part(3 * KT)
    modT = part(96 * 9).rearrange("p (j c) -> p j c", c=9)
    facA = part(KT * 9).rearrange("p (j c) -> p j c", c=9)
    xT = part(KT * T).rearrange("p (j t) -> p j t", t=T)
    hT0 = top[0]
    hT = part(KT * T).rearrange("p (j t) -> p j t", t=T)
    rstd0 = top[0]
    rstd = part(T)
    tmp = part(4 * T).rearrange("p (j t) -> p j t", t=T)
    oN0 = top[0]
    oN = part(8 * T).rearrange("p (j t) -> p j t", t=T)
    oD = part(4 * T).rearrange("p (j t) -> p j t", t=T)
    ring0 = top[0]
    part(3 * SLOT)
    region = top[0]

    def slot(s, k=KT, n=CW):
        a = ring0 + s * SLOT if s < 3 else fourth
        return piece(a, SLOT, F32)[:, 0:k * n].rearrange("p (k n) -> p k n", n=n)

    qk0 = top[0]
    qK = part(G * T).rearrange("p (j t) -> p j t", t=T)
    kT = part(3 * T).rearrange("p (j t) -> p j t", t=T)
    dqk0 = top[0]
    dqk = part(2 * DHEADS * T).rearrange("p (j t) -> p j t", t=T)
    tmN = part(QT * 6 * P).rearrange("p (q j f) -> p q j f", q=QT, j=6)
    tmV0 = top[0]
    tmV = part(QT * DHEADS * P).rearrange("p (q j f) -> p q j f", q=QT, j=DHEADS)
    tmS = part(30 * P).rearrange("p (j f) -> p j f", f=P)
    gates = part(QT * 48).rearrange("p (q j) -> p q j", q=QT)
    gatesS = part(3)
    w1p = part(2 * 16 * 64).rearrange("p (s l j e) -> p s l j e", s=2, j=2, e=64)
    w2 = part(2 * 64).rearrange("p (s e) -> p s e", e=64)
    peT = part(32)
    peb = part(2)
    kcP, vcP = part(16), part(P)
    small = part(96)
    at0 = top[0]
    PB = 9 * P - 3 * P + 16
    E = part(2 * PB).rearrange("p (u k) -> p u k", u=2)
    PT = part(PB)
    rt = mem[:, at0 + 1024:at0 + 1024 + 2 * T].rearrange("p (j t) -> p j t", t=T)
    stage = mem[:, at0:at0 + 1024].rearrange("p (u q f) -> p u q f", u=2, q=QT)
    ctop = at0
    cbsh = mem[:, ctop:ctop + 508]
    chid = mem[:, ctop + 508:ctop + 1016]
    cgl = mem[:, ctop + 1016:ctop + 1524]
    flat = tmp.rearrange("p j t -> p (j t)")
    kTcP = flat[:, 0:512].rearrange("p (j n) -> p j n", j=4)
    pairsP = flat[:, 512:1024].rearrange("p (t f) -> p t f", t=1)

    sbase = [qk0]

    def spart(words):
        a = sbase[0]
        sbase[0] += words
        assert sbase[0] <= tmV0 + QT * DHEADS * P, sbase[0] - tmV0 - QT * DHEADS * P
        return mem[:, a:a + words]
    KS = spart(4096)
    wide = spart(3072)
    SS = wide[:, 0:2576]
    rk = wide[:, 0:NSEL * NSEL].rearrange("p (j i) -> p j i", i=NSEL)
    qpad = wide.rearrange("p (j b r) -> p j b r", j=DHEADS, b=B)
    wide2 = spart(3072)
    before_c = wide2[:, 0:NSEL * NSEL]
    PTn = wide2[:, 0:22 * P].rearrange("p (j r) -> p j r", r=P)
    PTm = wide2.rearrange("p (g r c) -> p g r c", g=NG, r=RD)
    c_sample = spart(CONST["before"][0] - CONST_P)
    vcS = spart(B * P).rearrange("p (b f) -> p b f", f=P)
    qbd = spart(B * P).rearrange("p (b r) -> p b r", r=P)
    ptc = spart(P)
    pcmp = spart(P)
    kcS = spart(P)
    am = spart(NSEL)
    imp = spart(4 * NSEL)
    sel = spart(4 * NSEL).rearrange("p (j i) -> p j i", i=NSEL)
    eye_c = w1p.rearrange("p s l j e -> p (s l j e)")[:, 0:RD * RD]
    late = mem[:, at0 + 1540:at0 + 2352]
    qfull, dqnew = late[:, 0:P], late[:, P:P + 96].rearrange("p (j b) -> p j b", b=B)
    dknew = late[:, 224:320].rearrange("p (j b) -> p j b", b=B)
    knew = late[:, 320:336].rearrange("p (j b) -> p j b", b=B)
    Ed = late[:, 336:336 + 408]
    qn = mem[:, at0:at0 + 384].rearrange("p (j r) -> p j r", r=RD)
    Pn = mem[:, at0 + 384:at0 + 768].rearrange("p (g h r) -> p g h r", g=NG, h=HG)
    oR = wide[:, 0:B * P].rearrange("p (b f) -> p b f", f=P)
    win = mem[:, at0:at0 + 1024].rearrange("p (u t f) -> p u t f", u=2, t=4)
    oRd = mem[:, at0 + 768:at0 + 768 + P]

    prod = mem[:, region + KT * T:region + (KT + 4) * T].rearrange("p (j t) -> p j t", t=T)
    xs8 = rstd[:, 0:B].unsqueeze(1)
    mT = mem[:, region:region + KT * T].rearrange("p (j t) -> p j t", t=T)
    fT = mem[:, region:region + FT * T].rearrange("p (j t) -> p j t", t=T)
    fourth = region + FT * T
    assert fourth + SLOT <= WORDS
    spare = fourth + SLOT
    dead_consts = CONST["cos_nsa"][0]

    def tiles_at(*runs):
        return [a + j * T for a, n in runs for j in range(n)]
    ffn_high = [spare, spare + 2048, spare + 4096 + 4 * T, dead_consts]
    h_high = tiles_at((oN0, 12), (spare + 4096, 4))
    ada_buffer = [spare, spare + 2048, spare + 4096, oN0]
    silu_high, silu_low = spare + 6144, spare + 6144 + KT * 9

    def ada_piece(a, h=None):
        words = KT * CW if h is not None else 2048
        t = piece(a, words, F32R)[:, :].rearrange("p (k n) -> p k n", n=CW)
        return t if h is None else t[:, 8 * h:8 * h + 8, :]

    def silu_part(a):
        return piece(a, KT * 9, F32R)[:, :]
    merge_high, wout_high = ffn_high[0:3], ffn_high[3:] + ffn_high[0:3]
    x_high = tiles_at((region + (KT + 4) * T, 24), (spare + 4096, 4))
    x_low = tiles_at((hT0, KT), (oN0, 12))
    m_low = tiles_at((region, KT))
    KD = FT // 4
    down_high = [spare, spare + KD * P, dead_consts, dead_consts + KD * P]
    f_high = tiles_at((hT0, 16), (oN0, 12), (spare + 2 * KD * P, 16))
    assert ffn_high[2] + 2048 <= WORDS and f_high[-1] + T <= WORDS
    assert dead_consts + 2 * KD * P <= CONST_P + 96

    def half_chunk(a, k, f=0, n=P):
        return piece(a, k * n, F32R)[:, :].rearrange("p (k n) -> p k n", n=n)[:, :, f * P:(f + 1) * P]

    def half_tile(a):
        return piece(a, T, F32R)[:, :]

    def slot_at(s):
        return ring0 + s * SLOT if s < 3 else fourth
    c_rows = mem[:, region:region + D]
    c_silu = mem[:, region + D:region + 2 * D]
    x_tm = mem[:, region + 2 * D:region + 4 * D].rearrange("p (q f) -> p q f", q=QT)
    x_ts = mem[:, region + 4 * D:region + 5 * D]
    vec_rows = mem[:, region + 5 * D:region + 5 * D + 2 * P].rearrange("p (u f) -> p u f", u=2)
    siluT = mem[:, region + 5 * D + 256:region + 5 * D + 256 + KT * 9].rearrange("p (j c) -> p j c", c=9)
    assert region + 5 * D + 512 <= fourth
    ada_row = tmp.rearrange("p j t -> p (j t)")[:, 0:4 * CW].rearrange("p (s n) -> p s n", s=4)
    y_tm, y_ts = x_tm, x_ts
    pages = ctx.enter_context(nc.sbuf_tensor("pages", [P, B], I32))
    runs = ctx.enter_context(nc.sbuf_tensor("runs", [P, B], U32))

    bank = [ctx.enter_context(nc.psum_tensor(f"bank{n}", [P, 512], F32)) for n in range(8)]

    const_loaded = sem("const_loaded")
    rows_loaded = sem("rows_loaded")
    loaded = [signal(f"slot{s}_loaded") for s in range(4)]
    pe_, act_, dve_ = signal("pe_step"), signal("act_step"), signal("dve_step")
    outs_stored = signal("outs_stored")
    stage_stored = [signal(f"stage{s}_stored") for s in range(2)]
    cmp_stored, rows_stored = signal("cmp_stored"), signal("rows_stored")
    sample_const = sem("sample_const")
    pairs_loaded = signal("pairs_loaded")
    pages_loaded = sem("pages_loaded")
    proj_in = [signal(f"projection_weights{s}_in") for s in range(4)]
    pages_in = [signal(f"pages{s}_in") for s in range(3)]
    win_in = [signal(f"window{s}_in") for s in range(2)]
    caches_copied = signal("caches_copied")
    ada_high, ada_low, ada_half = sem("ada_high_parts"), sem("ada_low_parts"), sem("ada_halves_used")
    ada_kept, ada_rows, ada_turned = sem("ada_kept"), sem("ada_rows"), sem("ada_turned")
    mg_high, mg_low, mg_half = sem("merge_high_parts"), sem("merge_low_parts"), sem("merge_halves_used")
    mg_sig, mg_kept = sem("merge_sigmoids"), sem("merge_kept")
    mg_t = sem("merge_products")
    wo_high, wo_low, wo_half = sem("wout_high_parts"), sem("wout_low_parts"), sem("wout_halves_used")
    wo_t, wo_kept = sem("wout_products"), sem("wout_kept")
    ff_silu, ff_kept = sem("ffn_silu"), sem("ffn_kept")
    ff_high, ff_low, ff_half = sem("ffn_high_parts"), sem("ffn_low_parts"), sem("ffn_halves_used")
    nf_sq, nf_used = sem("last_norm_squares"), sem("last_norm_squares_used")
    dn_high, dn_low, dn_half = sem("down_high_parts"), sem("down_low_parts"), sem("down_halves_used")
    dn_t, dn_kept = sem("down_products"), sem("down_kept")
    w_ld = {ph: [sem(f"{ph}_loaded{s}") for s in range(4)] for ph in ("ada", "merge", "wout", "ffn", "down")}

    w_ada, w_in, w_out = i_["w_ada"][0], i_["w_in"][0], i_["w_out"][0]
    w_gate, w_up, w_down = i_["w_gate"][0], i_["w_up"][0], i_["w_down"][0]
    w_bn, w_bd = i_["w_br_nsa"][0], i_["w_br_dil"][0]

    def rows(w, c, n=CW):
        return w[:, c].rearrange("(k p) n -> p k n", p=P)

    CHUNKS = [(C_GATE, 48)] + [(C_KV + P * j, P) for j in range(6)] + [(P * j, P) for j in range(8)] \
        + [(C_DIL + P * j, P) for j in range(3 * DHEADS)]
    TILES = [("gate", 0)] + [(("k", "v")[j % 2], j // 2) for j in range(6)] + [("q", j) for j in range(8)] \
        + [(k, h) for k in ("dq", "dk", "dv") for h in range(DHEADS)]
    NT = len(TILES)

    def chunk_low(n):
        return ring0 + n % 4 * 2048

    def chunk_high(n):
        return ring0 + (4 + n % 2) * 2048

    def chunk_piece(a, n, dtype):
        w = CHUNKS[n][1]
        return piece(a, KT * w, dtype)[:, :].rearrange("p (k n) -> p k n", n=w)
    n1_high = tiles_at((oN0, 12), (at0 + 1024 + 2 * T, 3), (rstd0, 1))
    n1_low = tiles_at((hT0, KT))

    ROPED = ("k", "q", "dq", "dk")
    TURNED = ("k", "v", "dk", "dv")

    def made(n):
        return dve_.at("roped", n) if TILES[n][0] in ROPED else act_.at("raw", n)

    LASTN = NT - 1
    UNITS = [("n", qt, h) for h in range(H) for qt in range(QT)] + [("d", qt, h) for h in range(HG) for qt in range(QT)]
    NU = len(UNITS)

    def blocks(u):
        kind, qt, h = UNITS[u]
        W = P * (qt + 1)
        if kind == "n":
            kv = h // G
            out = [(br * W + kb * P, P, tmN[:, kb, 2 * (br + 1) + 1, kv * DH:(kv + 1) * DH])
                   for br in range(2) for kb in range(qt + 1)]
            return out + [(2 * W, NBP, vcP[0:NBP, kv * DH:(kv + 1) * DH])]
        return [(g * W + kb * P, P, tmV[:, kb, g * HG + h, :]) for g in range(NG) for kb in range(qt + 1)]

    block = ctx.enter_context(nc.Block())

    @block.sync
    def _(sp):
        sp.dma_start(c_all, i_["const"][:, 0:CONST_P]).then_inc(const_loaded, 16)
        sp.dma_start(c_rows[0:1, :], i_["c_prompt"]).then_inc(rows_loaded, 16)
        sp.dma_start(c_rows[1:1 + B, :], i_["c_sample"]).then_inc(rows_loaded, 16)
        sp.dma_start(vec_rows[0:96, 0, :], i_["b_ada"][0].rearrange("(j f) -> j f", f=P)).then_inc(rows_loaded, 16)
        for n, v in enumerate((i_["norm1_g"][0], i_["norm2_g"][0], i_["normf_g"])):
            sp.dma_start(vec_rows[KT * n:KT * (n + 1), 1, :], v.rearrange("(j f) -> j f", f=P)).then_inc(rows_loaded, 16)
        sp.dma_start(x_tm, i_["x_prompt"][0].rearrange("(q p) f -> p q f", p=P)).then_inc(rows_loaded, 16)
        sp.dma_start(x_ts[0:B, :], i_["x_sample"].rearrange("b o f -> (b o) f")).then_inc(rows_loaded, 16)

        for s in range(4):
            sp.dma_start(slot(s), rows(w_ada, bass.ds(s * CW, CW))).then_inc(w_ld["ada"][s], 16)
        with sp.Fori(1, 12) as i:
            cols = [sp.snap(i * (4 * CW) + s * CW) for s in range(4)]
            for s in range(4):
                sp.wait_ge(ada_half, i * 8 + (2 * s - 6))
                sp.dma_start(slot(s), rows(w_ada, bass.ds(cols[s], CW))).then_inc(w_ld["ada"][s], 16)
        for c, (col, n) in enumerate(CHUNKS):
            if c < 4:
                sp.wait_ge(ada_half, 90 + c // 2 * 2)
            else:
                sp.wait_ge(*pe_.at("acc", c - 4))
            sp.dma_start(chunk_piece(chunk_low(c), c, F32), rows(w_in, slice(col, col + n))).then_inc(*proj_in[c % 4].mark("proj", c, by=16))
            if c == 3:
                sp.wait_ge(*dve_.at("x_in"))
                sp.wait_ge(ada_half, 96)
                for j in range(8):
                    sp.dma_start(pages[j:P:8, :], i_["page_table"].rearrange("b n -> n b"),
                                 allow_slow_non_contiguous=True).then_inc(pages_loaded, 16)
                w1 = i_["cmp_w1"][0].rearrange("s (m l) d e -> (l d) s m e", l=2)
                for s in range(2):
                    for j in range(2):
                        sp.dma_start(w1p[:, s, :, j, :], w1[:, s, 8 * j:8 * j + 8, :]).then_inc(rows_loaded, 16)
                sp.dma_start(w2[0:64], i_["cmp_w2"][0].rearrange("s e d -> e s d")).then_inc(rows_loaded, 16)
                sp.dma_start(peT[:, 0:32], i_["cmp_pe"][0].rearrange("s (m l) d -> (l d) (s m)", l=2),
                             allow_slow_non_contiguous=True).then_inc(rows_loaded, 16)
        sp.wait_ge(*pe_.at("tm", LASTN))
        sp.wait_ge(*cmp_stored.at("p_cmp"))
        for l in range(2):
            sp.dma_start(pairsP[:, 0, :].rearrange("p (j l d) -> p j l d", j=4, l=2)[:, :, l, :],
                         o_["p_cmp"][0, 0].rearrange("(n l) s h d -> n l (s h) d", l=2)[:, l])\
                .then_inc(*pairs_loaded.mark(*(("p",) if l else ()), by=16))
        sp.wait_ge(*dve_.at("sample_q"))
        before_at, eye_at = CONST["before"][0], CONST["eye"][0]
        sp.dma_start(c_sample, i_["const"][:, CONST_P:before_at]).then_inc(sample_const, 16)
        sp.dma_start(before_c, i_["const"][:, before_at:eye_at]).then_inc(sample_const, 16)

        for u in range(5 * B):
            s, b, kind = u % 3, u % B, u // B
            flat = slot(s).rearrange("p k n -> p (k n)")
            if kind in (1, 2):
                kv, w = kind - 1, u % 2
                if u < B + 2:
                    sp.wait_ge(*pe_.at("kvc", B - 1))
                else:
                    sp.wait_ge(*pe_.at("win_used", u - 2))
                sp.dma_start(win[:, w], i_["cache_win_kv"][0, b].rearrange("(p t) s h d -> p t s (h d)", t=4)[:, :, kv])\
                    .then_inc(*win_in[w].mark("use", u, by=16))
            elif kind >= 3:
                sp.wait_ge(*pe_.at("used", u - 3))
                kv = kind - 3
                for g, (w, d) in enumerate(DIL):
                    src = i_[f"cache_dil{g + 1}_kv"][0, b].rearrange("(n r) s h d -> n r s (h d)", r=d)[:, 0, kv]
                    sp.dma_start(flat[:, g * 512:(g + 1) * 512], src)\
                        .then_inc(*loaded[s].mark(*(("use", u) if g == 2 else ()), by=16))
            if u == B:
                sp.wait_ge(*pe_.at("hid", B - 1))
                sp.dma_start(eye_c, i_["const"][:, eye_at:CONST_W]).then_inc(sample_const, 16)
        def merge_load(s, col):
            if s < 2:
                sp.dma_start(slot(s), rows(w_in, bass.ds(col, CW))).then_inc(w_ld["merge"][s], 16)
            else:
                sp.dma_start(slot(2)[:, 0:8, :], rows(w_bn, slice(0, CW))).then_inc(w_ld["merge"][2], 16)
                sp.dma_start(slot(2)[:, 8:12, :], rows(w_bd, slice(0, CW))).then_inc(w_ld["merge"][2], 16)
        for s in range(3):
            sp.wait_ge(*pe_.at("used", 5 * B - 1 - (5 * B - 1 - s) % 3))
            merge_load(s, (C_MERGE, C_MERGE + D, 0)[s])
        with sp.Fori(1, 8) as i:
            cols = [sp.snap(i * CW + C_MERGE), sp.snap(i * CW + (C_MERGE + D))]
            sp.wait_ge(mg_half, i * 6 - 4)
            merge_load(0, cols[0])
            sp.wait_ge(mg_half, i * 6 - 2)
            merge_load(1, cols[1])
        for i in range(2):
            for s in range(4):
                if i == 0:
                    if s < 3:
                        sp.wait_ge(mg_half, 44 + 2 * s)
                else:
                    sp.wait_ge(wo_half, 2 * s + 2)
                sp.dma_start(slot(s), rows(w_out, slice((4 * i + s) * CW, (4 * i + s + 1) * CW))).then_inc(w_ld["wout"][s], 16)
        for s in range(4):
            sp.wait_ge(wo_half, 10 + 2 * s)
            sp.dma_start(slot(s), rows((w_gate, w_up)[s % 2], bass.ds((s // 2) * CW, CW))).then_inc(w_ld["ffn"][s], 16)
        with sp.Fori(1, 11) as i:
            cols = [sp.snap(i * (2 * CW)), sp.snap(i * (2 * CW) + CW)]
            for s in range(4):
                sp.wait_ge(ff_half, i * 8 + (2 * s - 6))
                sp.dma_start(slot(s), rows((w_gate, w_up)[s % 2], bass.ds(cols[s // 2], CW)))\
                    .then_inc(w_ld["ffn"][s], 16)

        def down_load(s, col):
            sp.dma_start(slot(s, KD), w_down[s * KD * P:(s + 1) * KD * P, col].rearrange("(k p) n -> p k n", p=P))\
                .then_inc(w_ld["down"][s], 16)
        for s in range(4):
            sp.wait_ge(ff_half, 80 + 2 * s + 2)
            down_load(s, bass.ds(0, CW))
        with sp.Fori(1, 8) as i:
            col = sp.snap(i * CW)
            for s in range(4):
                sp.wait_ge(dn_half, i * 8 + (2 * s - 6))
                down_load(s, bass.ds(col, CW))
        for k in range(0, KT, 4):
            sp.wait_ge(*act_.at("y", k + 2))
            sp.wait_ge(*dve_.at("y", k + 3))
            cols = slice(k * P, (k + 4) * P)
            sp.dma_start(o_["y_prompt"][0].rearrange("(q p) f -> p q f", p=P)[:, :, cols], y_tm[:, :, cols])\
                .then_inc(*outs_stored.mark(by=16))
        sp.dma_start(o_["y_sample"].rearrange("b o f -> (b o) f"), y_ts[0:B, :]).then_inc(*outs_stored.mark("y", by=16))
        sp.wait_ge(*outs_stored.at("y"))
        sp.wait_ge(*caches_copied.at("all"))
        for s in range(2):
            sp.wait_ge(*stage_stored[s].at("last"))
        sp.wait_ge(*rows_stored.at("all"))

    @block.gpsimd
    def _(pool):
        def gathers(uses):
            for u in uses:
                s, b = u % 3, u % B
                if u < 3:
                    pool.wait_ge(*pe_.at("acc", NT - 1))
                else:
                    pool.wait_ge(*pe_.at("used", u - 3))
                flat = slot(s).rearrange("p k n -> p (k n)")
                src = i_[("cache_cmp_kv", "cache_sel_kv")[min(u // B, 1)]][0].rearrange("n (j t) s h d -> (n j) (t s h d)", j=8)
                pool.indirect_dma_start(flat, None, src, bass.IndirectOffsetOnAxis(runs[:, b:b + 1], 0))\
                    .then_inc(*pages_in[s].mark("use", u, by=16))
        for name, n in (("dil3", 2048), ("dil2", 512), ("dil1", 128), ("win", WIN)):
            src, dst = i_[f"cache_{name}_kv"][0], o_[f"s_{name}"][0]
            for c in range(B):
                if (name, c) == ("dil3", B // 2):
                    pool.wait_ge(*dve_.at("runs"))
                    gathers(range(3))
                if (name, c) == ("dil2", 0):
                    gathers(range(3, 3 * B))
                if name == "dil2":
                    pool.wait_ge(ff_half, 4 + 8 * c)
                f = "t s h d -> (t s h d)"
                a, z = src[c, 1:n].rearrange(f), dst[c, 0:n - 1].rearrange(f)
                a, z = a.rearrange("(q n) -> q n", q=16), z.rearrange("(q n) -> q n", q=16)
                parts = 8 if name == "dil3" else 1
                w = (n - 1) * 2 * HG * DD // 16 // parts if name == "dil3" else None
                for eighth in range(parts):
                    if name == "dil3" and c < B // 2:
                        pool.wait_ge(*pe_.at("acc", 3 + (8 * c + eighth) * (NT - 4) // 32))
                    elif name == "dil3":
                        pool.wait_ge(*pe_.at("s", (8 * (c - B // 2) + eighth) * NU // 36))
                    cols = slice(eighth * w, (eighth + 1) * w) if w else slice(None)
                    pool.dma_start(z[:, cols], a[:, cols])\
                        .then_inc(*caches_copied.mark(*(("all",) if (name, c) == ("win", B - 1) else ()), by=16))

    @block.tensor
    def _(pe):
        mm, turn = nc.tensor.matmul, nc.tensor.transpose
        pe.wait_ge(const_loaded, 16)
        pe.wait_ge(rows_loaded, 8 * 16)
        pe.wait_ge(*dve_.at("silu"))
        for k in range(KT):
            last = turn(bank[0][:, 9 * k:9 * k + 9], c_silu[0:9, k * P:(k + 1) * P], ident[0:9, 0:9])
        last.then_inc(*pe_.mark("siluT"))
        turn(bank[1][:, 0:96], vec_rows[0:96, 0, :], ident[0:96, 0:96])
        turn(bank[1][:, 96:144], vec_rows[0:48, 1, :], ident[0:48, 0:48]).then_inc(*pe_.mark("vecT"))
        for k in range(KT):
            if k >= 4:
                pe.wait_ge(*(dve_ if k % 2 else act_).at("xT", k - 4))
            z = bank[2 + k % 4]
            for q in range(QT):
                turn(z[:, q * P:(q + 1) * P], x_tm[:, q, k * P:(k + 1) * P], ident)
            turn(z[:, TP:T], x_ts[0:B, k * P:(k + 1) * P], ident[0:B, 0:B]).then_inc(*pe_.mark("xT", k))
        pe.wait_ge(*act_.at("siluT"))
        pe.wait_ge(*dve_.at("silu_low"))
        pe.wait_ge(*dve_.at("vecT"))
        pe.wait_ge(*dve_.at("xT", KT - 1))
        pe.wait_ge(*act_.at("xT", KT - 2))

        def ada(i, s, first):
            if not first:
                pe.wait_ge(ada_kept, i * 4 + (s - 3))
            out = bank[s][0:9, 0:CW]
            for h in range(2):
                pe.wait_ge(ada_low, i * 8 + (2 * s + h + 1))
                w_high, w_low = ada_piece(ada_buffer[(2 * s + h) % 4]), ada_piece(slot_at(s), h)
                for k in range(8):
                    row = slice((8 * h + k) * 9, (8 * h + k + 1) * 9)
                    mm(out, silu_part(silu_high)[:, row], w_high[:, k, :], start=(h == k == 0), stop=False)
                    mm(out, silu_part(silu_high)[:, row], w_low[:, k, :], start=False, stop=False)
                    last = mm(out, silu_part(silu_low)[:, row], w_high[:, k, :], start=False, stop=(h == 1 and k == 7))
                last.then_inc(ada_half, 1)

        def ada_turn(i, s):
            pe.wait_ge(const_loaded, 16)
            pe.wait_ge(ada_rows, i * 4 + (s + 1))
            for f in range(2):
                last = turn(bank[4 + s][:, f * P:(f + 1) * P], ada_row[:, s, f * P:(f + 1) * P], ident)
            last.then_inc(ada_turned, 1)
        for s in range(4):
            ada(0, s, True)
            if s >= 2:
                ada_turn(0, s - 2)
        with pe.Fori(1, 12) as i:
            for s in range(4):
                ada(i, s, False)
                ada_turn(i + (-1 if s < 2 else 0), (s - 2) % 4)
        ada_turn(11, 2)
        ada_turn(11, 3)

        def stat(tag, k):
            pe.wait_ge(*dve_.at("sq", tag, k))
            mm(bank[7][:, 0:T], ones, tmp[:, k % 4, :], start=(k == 0), stop=(k == KT - 1)).then_inc(*pe_.mark("sq", tag, k))
        for k in range(KT):
            stat("n1", k)

        pe.wait_ge(*act_.at("h", "n1"))
        pe.wait_ge(*dve_.at("h", "n1"))

        def rope(n):
            kind = TILES[n][0]
            if kind not in ROPED:
                return
            pe.wait_ge(*act_.at("raw", n))
            if n >= 2:
                pe.wait_ge(*dve_.at("rope_bank", n))
            mm(bank[4 + n % 2][:, 0:T], const("rot_nsa" if kind in "kq" else "rot_dil"), tmp[:, n % 3, :],
               start=True, stop=True).then_inc(*pe_.mark("rot", n))

        def source(n):
            kind, j = TILES[n]
            return {"k": lambda: kT[:, j, :], "dk": lambda: dqk[:, DHEADS + j, :]}.get(kind, lambda: tmp[:, n % 3, :])()

        def token_major(n):
            kind = TILES[n][0]
            if kind not in TURNED:
                return
            pe.wait_ge(*made(n))
            pe.wait_ge(*act_.at("tm_bank", n))
            for q in range(QT):
                turn(bank[6 + n % 2][:, q * P:(q + 1) * P], source(n)[:, q * P:(q + 1) * P], ident)
            turn(bank[6 + n % 2][0:B, TP:TP + P], source(n)[:, TP:T], ident).then_inc(*pe_.mark("tm", n))

        for n in range(NT + 2):
            if n < NT:
                kind = TILES[n][0]
                m = 48 if n == 0 else P
                pe.wait_ge(*dve_.at("w_low", n))
                if n >= 4:
                    pe.wait_ge(*act_.at("raw", n - 4))
                w_high, w_low = chunk_piece(chunk_high(n), n, F32R), chunk_piece(chunk_low(n), n, F32R)
                out = bank[n % 4][0:m, 0:T]
                for k in range(KT):
                    if n == 0:
                        pe.wait_ge(*dve_.at("n1_low", k))
                    mm(out, w_high[:, k, :], half_tile(n1_high[k]), start=(k == 0), stop=False)
                    mm(out, w_high[:, k, :], half_tile(n1_low[k]), start=False, stop=False)
                    last = mm(out, w_low[:, k, :], half_tile(n1_high[k]), start=False, stop=(k == KT - 1))
                last.then_inc(*pe_.mark("acc", n))
            if n == 1:
                pe.wait_ge(*act_.at("raw", 0))
                for q in range(QT):
                    turn(bank[6][:, q * 48:(q + 1) * 48], tmp[0:48, 0, q * P:(q + 1) * P], ident[0:48, 0:48])
                turn(bank[6][0:B, 128:176], tmp[0:48, 0, TP:T], ident[0:48, 0:48]).then_inc(*pe_.mark("gateT"))
                pe.wait_ge(*act_.at("gateS"))
                mm(bank[7][:, 0:48], const("rowsel")[0:B, :], small[0:B, 0:48], start=True, stop=True)\
                    .then_inc(*pe_.mark("gateS"))
            if 1 <= n <= NT:
                rope(n - 1)
            if n >= 2:
                token_major(n - 2)

        def compress_turns(tag, pairs, kTc, nt):
            for sh in range(4):
                for half in range(max(1, nt // 4)):
                    i = sh * max(1, nt // 4) + half
                    for t in range(min(nt, 4)):
                        tt = half * 4 + t
                        src = pairs[:, tt, sh * P:(sh + 1) * P]
                        if t == 0:
                            e = (act_, dve_)[i % 2]
                            if i >= 2:
                                pe.wait_ge(*e.at("ctr", tag, i - 2))
                        last = turn(bank[4 + i % 2][:, t * P:(t + 1) * P], src, ident)
                    last.then_inc(*pe_.mark("ctr", tag, i))

        def compress(tag, kTc, nt):
            n_chunk = nt * 16
            nb = n_chunk - 1
            per = max(1, nt // 4)
            for sh in range(4):
                for i in range(sh * per, (sh + 1) * per):
                    pe.wait_ge(*(act_, dve_)[i % 2].at("ctr", tag, i))
                for l in range(8):
                    last = mm(bank[0][:, sh * P:sh * P + n_chunk],
                              w1p[:, sh // 2, l, :, :].rearrange("p j e -> p (j e)"), kTc[:, sh, 0:nt * P].rearrange("p (n l) -> p l n", l=8)[:, l, :],
                              start=(l == 0), stop=(l == 7))
            last.then_inc(*pe_.mark("hid", tag))
            pe.wait_ge(*act_.at("gelu", tag))
            gl = cgl[0:64].rearrange("p (j n) -> p j n", j=4)
            for h in range(2):
                mm(bank[1][h * 64:(h + 1) * 64, 0:nb], w2[0:64, 0, :], gl[:, h, 0:nb], start=True, stop=True)
            for h in range(2):
                last = mm(bank[2][0:nb, h * 64:(h + 1) * 64], gl[:, 2 + h, 0:nb], w2[0:64, 1, :], start=True, stop=True)
            last.then_inc(*pe_.mark("kvc", tag))

        pe.wait_ge(rows_loaded, 14 * 16)
        for s in range(2):
            for m in range(16):
                last = mm(bank[3][0:64, s:s + 1], w1p[:, s, m % 8, m // 8, :], peT[:, s * 16 + m:s * 16 + m + 1],
                          start=(m == 0), stop=(m == 15))
        last.then_inc(*pe_.mark("pe"))
        pe.wait_ge(*pairs_loaded.at("p"))
        pe.wait_ge(*act_.at("raw", LASTN))
        pe.wait_ge(*dve_.at("roped", NT - DHEADS - 1))
        compress_turns("p", pairsP, kTcP, 1)
        compress("p", kTcP, 1)

        def scores(u):
            kind, qt, h = UNITS[u]
            W = P * (qt + 1)
            if u >= 1:
                pe.wait_ge(*dve_.at("max", u - 1))
            if kind == "n":
                kv, g = h // G, h % G
                r = slice(kv * DH, (kv + 1) * DH)
                q = qK[r, g, qt * P:(qt + 1) * P]
                for br in range(2):
                    mm(bank[0][:, br * W:(br + 1) * W], q, kT[r, br + 1, 0:W], start=True, stop=True)
                mm(bank[1][:, 0:NBP], q, kcP[r, 0:NBP], start=True, stop=True).then_inc(*pe_.mark("s", u))
            else:
                for g in range(NG):
                    z = bank[0][:, g * W:(g + 1) * W] if g < 2 else bank[1][:, 0:W]
                    last = mm(z, dqk[:, g * HG + h, qt * P:(qt + 1) * P], dqk[:, DHEADS + g * HG + h, 0:W], start=True, stop=True)
                last.then_inc(*pe_.mark("s", u))

        def probs(u):
            pe.wait_ge(*dve_.at("p", u))
            if u >= 1:
                pe.wait_ge(*act_.at("pt", u - 1))
            for n, (c, k, _) in enumerate(blocks(u)):
                last = turn(bank[2 + n // 4][0:k, (n % 4) * P:(n % 4 + 1) * P], E[:, u % 2, c:c + k], ident)
            last.then_inc(*pe_.mark("pt", u))

        def pv(u):
            kind, qt, h = UNITS[u]
            pe.wait_ge(*act_.at("pt", u))
            if u >= 2:
                pe.wait_ge(*act_.at("o", u - 2))
            z = bank[4 + u % 2]
            out = z[(h % 2) * DH:(h % 2 + 1) * DH, 0:P] if kind == "n" else z[:, 0:P]
            bl = blocks(u)
            for n, (c, k, v) in enumerate(bl):
                last = mm(out, v, PT[0:k, n * P:(n + 1) * P], start=(n == 0), stop=(n == len(bl) - 1))
            last.then_inc(*pe_.mark("pv", u))

        pe.wait_ge(*act_.at("kvc", "p"))
        pe.wait_ge(*dve_.at("kvc", "p"))
        pe.wait_ge(*act_.at("tm", LASTN))
        for u in range(NU + 2):
            if u < NU:
                scores(u)
            if 1 <= u <= NU:
                probs(u - 1)
            if u >= 2:
                pv(u - 2)

        pe.wait_ge(sample_const, 32)
        pe.wait_ge(*act_.at("o", NU - 1))
        pe.wait_ge(*dve_.at("sample_q"))
        NX = 4 * B
        for x in range(NX + 2):
            if x < NX:
                b, kv, eighth = x // 4, x % 4 // 2, x % 2
                if x % 4 == 0:
                    pe.wait_ge(*pages_in[b % 3].at("use", b))
                for half, e in enumerate((act_, dve_)):
                    if x >= 2:
                        pe.wait_ge(*e.at("cx", x - 2))
                    for t in range(4):
                        last = turn(bank[4 + 2 * (x % 2) + half][:, t * P:(t + 1) * P],
                                    slot(b % 3)[:, 8 * eighth + 4 * half + t, kv * P:(kv + 1) * P], ident)
                    last.then_inc(*pe_.mark("cx", x, half))
                if x % 4 == 3:
                    pe_.marks["used", b] = pe_.n
            if x >= 2 and x % 2 == 0:
                b, kv = (x - 2) // 4, (x - 2) % 4 // 2
                for e in (act_, dve_):
                    pe.wait_ge(*e.at("cx", x - 1))
                for sh in (2 * kv, 2 * kv + 1):
                    for l in range(8):
                        last = mm(bank[b % 2][:, sh * P:(sh + 1) * P], w1p[:, kv, l, :, :].rearrange("p j e -> p (j e)"),
                                  KS[:, sh * 1024 + l * P:sh * 1024 + (l + 1) * P], start=(l == 0), stop=(l == 7))
                last.then_inc(*pe_.mark("hid" if kv else "hx", b))
            if x >= 5 and (x - 5) % 4 == 0 and (x - 5) // 4 < B:
                b = (x - 5) // 4
                pe.wait_ge(*act_.at("gelu", b))
                gl = cgl[0:64].rearrange("p (j n) -> p j n", j=4)
                for h in range(2):
                    mm(bank[2][h * 64:(h + 1) * 64, 0:NBS], w2[0:64, 0, :], gl[:, h, 0:NBS], start=True, stop=True)
                for h in range(2):
                    last = mm(bank[2][0:NBS, P + h * 64:P + (h + 1) * 64], gl[:, 2 + h, 0:NBS], w2[0:64, 1, :], start=True, stop=True)
                last.then_inc(*pe_.mark("kvc", b))
            if x >= 6 and (x - 6) % 4 == 0 and (x - 6) // 4 < B - 1:
                b = (x - 6) // 4
                pe.wait_ge(*act_.at("kvc", b))
                mm(bank[3][:, 0:NBS], qbd[:, b, :], kcS[:, 0:NBS], start=(b == 0), stop=(b == B - 1)).then_inc(*pe_.mark("cs", b))
        b = B - 1
        pe.wait_ge(*act_.at("kvc", b))
        mm(bank[3][:, 0:NBS], qbd[:, b, :], kcS[:, 0:NBS], start=False, stop=True).then_inc(*pe_.mark("cs", b))
        pe.wait_ge(*dve_.at("cp"))
        mm(bank[0][0:H, 0:NBS], const("group"), pcmp[:, 0:NBS], start=True, stop=True).then_inc(*pe_.mark("imp"))
        pe.wait_ge(*dve_.at("cpg"))
        turn(bank[1][0:NBS, 0:P], pcmp[:, 0:NBS], ident).then_inc(*pe_.mark("cpt"))
        pe.wait_ge(*dve_.at("sel"))
        mm(bank[0][:, 256:256 + NSEL], const("spread")[0:H, :], sel[0:H, 0, :], start=True, stop=True).then_inc(*pe_.mark("spread"))
        pe.wait_ge(*dve_.at("am"))
        pe.wait_ge(*act_.at("cpt"))

        NY = 5 * B
        for y in range(NY + 2):
            if y < NY:
                b, i = y // 5, y % 5
                u = B + b
                if i == 0:
                    pe.wait_ge(*pages_in[u % 3].at("use", u))
                if i == 4:
                    pe.wait_ge(*win_in[u % 2].at("use", u))
                if y >= 3:
                    pe.wait_ge(*(act_, dve_)[(y - 3) % 2].at("ky", y - 3))
                for t in range(4):
                    keys = slot(u % 3)[:, 4 * i + t, 0:P] if i < 4 else win[:, u % 2, t, :]
                    last = turn(bank[4 + y % 3][:, t * P:(t + 1) * P], keys, ident)
                last.then_inc(*pe_.mark("ky", y))
                if i == 3:
                    pe_.marks["used", u] = pe_.n
                if i == 4:
                    pe_.marks["win_used", u] = pe_.n
            if y >= 2:
                x = y - 2
                b, i = x // 5, x % 5
                pe.wait_ge(*(act_, dve_)[x % 2].at("ky", x))
                last = mm(bank[i if i < 4 else 7][:, :], qbd[:, b, :], KS[:, (x % 8) * 512:(x % 8 + 1) * 512],
                          start=(b == 0), stop=(b == B - 1))
                last.then_inc(*pe_.mark("sy", x))
        for br in range(2):
            last = mm(bank[4][:, br * B:(br + 1) * B], qfull, knew[:, br, :], start=True, stop=True)
        last.then_inc(*pe_.mark("snew"))
        pe.wait_ge(*dve_.at("sp"))
        for i in range(5):
            if i >= 3:
                pe.wait_ge(*(act_, dve_)[(i - 3) % 2].at("pt", "s", i - 3))
            for t in range(4):
                c = (4 * i + t) * P if i < 4 else 2056 + t * P
                last = turn(bank[5 + i % 3][:, t * P:(t + 1) * P], SS[:, c:c + P], ident)
            last.then_inc(*pe_.mark("spt", i))
        pe.wait_ge(*dve_.at("sp"))
        for br, c in enumerate((2048, 2568)):
            last = turn(bank[4][0:B, br * P:(br + 1) * P], SS[:, c:c + B], ident)
        last.then_inc(*pe_.mark("spt", 5))
        for i in range(5):
            pe.wait_ge(*(act_, dve_)[i % 2].at("pt", "s", i))
        pe.wait_ge(*dve_.at("pt", "s", 5))
        for b in range(B):
            u = 2 * B + b
            pe.wait_ge(*pages_in[u % 3].at("use", u))
            pe.wait_ge(*win_in[u % 2].at("use", u))
            out = bank[b // 4][0:H, (b % 4) * P:(b % 4 + 1) * P]
            rows_b = slice(b * H, (b + 1) * H)
            for t in range(20):
                values = slot(u % 3)[:, t, P:2 * P] if t < 16 else win[:, u % 2, t - 16, :]
                mm(out, PTn[:, t, rows_b], values, start=(t == 0), stop=False)
            pe_.marks["used", u] = pe_.marks["win_used", u] = pe_.n + 1
            for br in range(2):
                mm(out, PTn[0:B, 20 + br, rows_b], tmS[0:B, 2 * (br + 1) + 1, :], start=False, stop=False)
            mm(out, ptc[0:NBS, rows_b], vcS[0:NBS, b, :], start=False, stop=True).then_inc(*pe_.mark("pvS", b))
        pe.wait_ge(*act_.at("oR"))
        for b in range(B):
            last = turn(bank[4][:, b * H:(b + 1) * H], oR[0:H, b, :], ident[0:H, 0:H])
        last.then_inc(*pe_.mark("oT"))

        pe.wait_ge(*dve_.at("qpad"))
        NZ = NG * B
        for z in range(NZ + 2):
            if z < NZ:
                b, g = z // NG, z % NG
                u = 3 * B + b
                if g == 0:
                    pe.wait_ge(*loaded[u % 3].at("use", u))
                if z >= 3:
                    pe.wait_ge(*(act_, dve_)[(z - 3) % 2].at("kz", z - 3))
                for h in range(HG):
                    last = turn(bank[5 + z % 3][:, h * P:(h + 1) * P],
                                slot(u % 3).rearrange("p k n -> p (k n)")[:, (g * HG + h) * P:(g * HG + h + 1) * P], ident)
                last.then_inc(*pe_.mark("kz", z))
                if g == NG - 1:
                    pe_.marks["used", u] = pe_.n
            if z >= 2:
                x = z - 2
                b, g = x // NG, x % NG
                pe.wait_ge(*(act_, dve_)[x % 2].at("kz", x))
                for h in range(HG):
                    last = mm(bank[g][0:RD, 0:P], qpad[:, g * HG + h, b, :], KS[:, (x % 8) * 512 + h * P:(x % 8) * 512 + (h + 1) * P],
                              start=(b == 0 and h == 0), stop=(b == B - 1 and h == HG - 1))
                last.then_inc(*pe_.mark("sz", x))
        for g in range(NG):
            for h in range(HG):
                last = mm(bank[3][0:RD, g * B:(g + 1) * B], qn[:, g * HG + h, :], dknew[:, g * HG + h, :],
                          start=(h == 0), stop=(h == HG - 1))
        last.then_inc(*pe_.mark("dnew"))
        pe.wait_ge(*dve_.at("dp"))
        pe.wait_ge(*act_.at("oN"))
        for g in range(NG):
            turn(bank[4][:, g * RD:(g + 1) * RD], Ed[0:RD, g * P:(g + 1) * P], ident[0:RD, 0:RD])
        for g in range(NG):
            last = turn(bank[4][0:B, 96 + g * RD:96 + (g + 1) * RD], Ed[0:RD, 384 + g * B:384 + (g + 1) * B], ident[0:RD, 0:RD])
        last.then_inc(*pe_.mark("dpt"))
        pe.wait_ge(*dve_.at("PTm"))
        for b in range(B):
            u = 4 * B + b
            pe.wait_ge(*loaded[u % 3].at("use", u))
            for g in range(NG):
                for h in range(HG):
                    last = mm(bank[0][0:RD, 0:P], PTm[:, g, b * HG + h, :],
                              slot(u % 3).rearrange("p k n -> p (k n)")[:, (g * HG + h) * P:(g * HG + h + 1) * P],
                              start=(b == g == h == 0), stop=False)
            last.then_inc(*pe_.mark("used", u))
        for g in range(NG):
            for h in range(HG):
                last = mm(bank[0][0:RD, 0:P], Pn[0:B, g, h, :], tmS[0:B, 6 + DHEADS + g * HG + h, :],
                          start=False, stop=(g == NG - 1 and h == HG - 1))
        last.then_inc(*pe_.mark("pvD"))
        pe.wait_ge(*act_.at("oRd"))
        turn(bank[1][:, 0:RD], oRd[0:RD, :], ident[0:RD, 0:RD]).then_inc(*pe_.mark("oTd"))

        pe.wait_ge(*act_.at("oD"))

        def split_products(out, a, high, f, k_tiles, x_high, x_low, start, stop, tiles_ready=None, first_tile=0):
            w_low = half_chunk(a, k_tiles, f, CW)
            w_high = half_chunk(high, k_tiles)
            for k in range(first_tile, len(x_high)):
                if tiles_ready is not None:
                    pe.wait_ge(*dve_.at(tiles_ready, k))
                mm(out, w_high[:, k, :], half_tile(x_high[k]), start=(start and k == first_tile), stop=False)
                mm(out, w_high[:, k, :], half_tile(x_low[k]), start=False, stop=False)
                last = mm(out, w_low[:, k, :], half_tile(x_high[k]), start=False, stop=(stop and k == len(x_high) - 1))
            return last

        def merge(i, first):
            for s in range(3):
                for f in range(2):
                    n = 2 * s + f
                    pe.wait_ge(mg_low, i * 6 + (n + 1))
                    if not first and s < 2:
                        pe.wait_ge(mg_sig, i * 4 + (2 * s + f - 3))
                    elif not first and f == 0:
                        pe.wait_ge(mg_t, i * 4)
                    if s < 2:
                        split_products(bank[4 * f + s][:, 0:T], slot_at(s), merge_high[n % 3], f, KT, x_high[0:KT], x_low[0:KT],
                                       True, True, "x_low" if first and n == 0 else None).then_inc(mg_half, 1)
                        continue
                    if first and f == 0:
                        pe.wait_ge(*dve_.at("x_low", KT + 11))
                    for b, (k0, k1) in enumerate(((0, 8), (8, 12))):
                        last = split_products(bank[4 * f + 2 + b][:, 0:T], slot_at(2), merge_high[n % 3], f, 12,
                                              [None] * k0 + x_high[KT + k0:KT + k1], [None] * k0 + x_low[KT + k0:KT + k1],
                                              True, True, None, k0)
                    last.then_inc(mg_half, 1)
        merge(0, True)
        with pe.Fori(1, 8) as i:
            merge(i, False)
        pe.wait_ge(mg_sig, 32)
        for i in range(2):
            for s in range(4):
                for f in range(2):
                    n = 8 * i + 2 * s + f
                    pe.wait_ge(wo_low, n + 1)
                    if n >= 7:
                        pe.wait_ge(wo_kept, n - 6)
                    elif n == 2:
                        pe.wait_ge(mg_t, 32)
                    split_products(bank[n % 7][:, 0:T], slot_at(s), wout_high[n % 4], f, KT, x_high[0:KT], m_low,
                                   True, True, "m_low" if n == 0 else None).then_inc(wo_half, 1)
                    if n >= 4:
                        stat("n2", n - 4)
        for k in range(12, KT):
            stat("n2", k)

        h_low = tiles_at((hT0, KT))
        f_low = tiles_at((region, FT))

        def ffn(i, first):
            for s in range(4):
                if not first:
                    if s % 2:
                        pe.wait_ge(ff_kept, i * 4 + (s - 3))
                    else:
                        pe.wait_ge(ff_silu, i * 4 + (s - 2))
                for f in range(2):
                    pe.wait_ge(ff_low, i * 8 + (2 * s + f + 1))
                    split_products(bank[2 * s + f][:, 0:T], slot_at(s), ffn_high[(2 * s + f) % 4], f, KT, h_high, h_low,
                                   True, True, "h_low" if first and s == f == 0 else None).then_inc(ff_half, 1)
        ffn(0, True)
        with pe.Fori(1, 11) as i:
            ffn(i, False)

        def down(i, u, first, very_first=False):
            if not first:
                pe.wait_ge(dn_kept, i * 4 + (2 * u - 2))
            for s in range(4):
                for f in range(2):
                    pe.wait_ge(dn_low, i * 16 + (8 * u + 2 * s + f + 1))
                    split_products(bank[2 * u + f][:, 0:T], slot_at(s), down_high[(2 * s + f) % 4], f, KD,
                                   f_high[s * KD:(s + 1) * KD], f_low[s * KD:(s + 1) * KD], s == 0, s == 3,
                                   f"f_low{s}" if very_first and f == 0 else None).then_inc(dn_half, 1)

        def last_stat(i, u, start=False, stop=False):
            for f in range(2):
                pe.wait_ge(nf_sq, i * 4 + (2 * u + f + 1))
                mm(bank[7][:, 0:T], ones, tmp[:, 2 * u + f, :], start=(start and f == 0), stop=(stop and f == 1)).then_inc(nf_used, 1)
        down(0, 0, True, True)
        down(0, 1, True)
        last_stat(0, 0, start=True)
        with pe.Fori(1, 4) as i:
            down(i, 0, False)
            last_stat(i + (-1), 1)
            down(i, 1, False)
            last_stat(i, 0)
        last_stat(3, 1, stop=True)
        for k in range(KT):
            pe.wait_ge(*dve_.at("yT", k))
            if k >= 8:
                pe.wait_ge(*(dve_ if k % 2 else act_).at("y", k - 8))
            z = bank[k % 8]
            for q in range(QT):
                turn(z[:, q * P:(q + 1) * P], hT[:, k, q * P:(q + 1) * P], ident)
            turn(z[0:B, TP:TP + P], hT[:, k, TP:T], ident).then_inc(*pe_.mark("y", k))

    PARTS = [(h, l) for h in range(2) for l in range(2)]

    def pair_columns(x, half, h, l):
        sh, m = 2 * (x % 4 // 2) + h, 4 * (x % 2) + 2 * half
        return KS[l * DH:(l + 1) * DH, sh * 1024 + m * P:sh * 1024 + (m + 2) * P].rearrange("p (m n) -> p m n", n=P)

    def turned_tokens(x, half, h, l):
        return bank[4 + 2 * (x % 2) + half][h * DH:(h + 1) * DH, :].rearrange("p (m l n) -> p m l n", m=2, l=2)[:, :, l, :]

    @block.scalar
    def _(act):
        A, cp = nc.scalar.activation, nc.scalar.copy
        act.wait_ge(rows_loaded, 8 * 16)
        A(c_silu[0:9, :], c_rows[0:9, :], ACT.Sigmoid).then_inc(*act_.mark("sig"))
        act.wait_ge(*pe_.at("siluT"))
        cp(silu_part(silu_high), bank[0][:, 0:KT * 9]).then_inc(*act_.mark())
        cp(siluT.rearrange("p j c -> p (j c)"), bank[0][:, 0:KT * 9]).then_inc(*act_.mark("siluT"))
        for k in range(0, KT, 2):
            act.wait_ge(*pe_.at("xT", k))
            cp(xT[:, k, :], bank[2 + k % 4][:, 0:T]).then_inc(*act_.mark("xT", k))

        act.wait_ge(*dve_.at("ada_row"))

        def ada_halves(i, s, first):
            act.wait_ge(w_ld["ada"][s], i * 16 + 16)
            for h in range(2):
                if not first or s >= 2:
                    act.wait_ge(ada_half, i * 8 + (2 * s + h - 3))
                cp(ada_piece(ada_buffer[(2 * s + h) % 4]), slot(s)[:, 8 * h:8 * h + 8, :]).then_inc(ada_high, 1)

        def ada_out(i, s):
            act.wait_ge(ada_half, i * 8 + (2 * s + 2))
            cp(ada_row[0:9, s, :], bank[s][0:9, 0:CW]).then_inc(ada_rows, 1)
        for s in range(4):
            ada_halves(0, s, True)
            if s >= 2:
                ada_out(0, s - 2)
        with act.Fori(1, 12) as i:
            for s in range(4):
                ada_halves(i, s, False)
                ada_out(i + (-1 if s < 2 else 0), (s - 2) % 4)
        ada_out(11, 2)
        ada_out(11, 3)

        def norm(tag, gate):
            act.wait_ge(*dve_.at("ms", tag))
            A(rstd, rstd, ACT.Sqrt).then_inc(*act_.mark("root", tag))
            if gate is None:
                return
            for k in range(KT):
                act.wait_ge(*dve_.at("hs", tag, k))
                A(hT[:, k, 0:TP], hT[:, k, 0:TP], ACT.Identity, bias=modT[:, gate * KT + k, 0:1])\
                    .then_inc(*act_.mark(*(("h", tag) if k == KT - 1 else ("h", tag, k))))

        def weights_high(n):
            act.wait_ge(*proj_in[n % 4].at("proj", n))
            if n >= 2:
                act.wait_ge(*pe_.at("acc", n - 2))
            cp(chunk_piece(chunk_high(n), n, F32R), chunk_piece(chunk_low(n), n, F32)).then_inc(*act_.mark("w_high", n))
        act.wait_ge(ada_half, 96)
        weights_high(0)
        weights_high(1)
        norm("n1", 0)
        act.wait_ge(*dve_.at("h", "n1"))
        for k in range(KT):
            act.wait_ge(*(act_.at("h", "n1", k) if k < KT - 1 else act_.at("h", "n1")))
            cp(half_tile(n1_high[k]), hT[:, k, :]).then_inc(*act_.mark("n1_high", k))

        tiles = dict(enumerate(TILES))
        stores = [0, 0]

        def tm(n):
            kind, j = TILES[n]
            if kind not in TURNED:
                return
            act.wait_ge(*pe_.at("tm", n))
            z = bank[6 + n % 2]
            zq = z[:, 0:TP].rearrange("p (q f) -> p q f", q=QT)
            if kind in "kv":
                dst, row = tmN[:, :, 2 * j + (kind == "v"), :], 2 * j + (kind == "v")
            elif kind == "dv":
                dst, row = tmV[:, :, j, :], 6 + DHEADS + j
            else:
                u = (j // 2) % 2
                if j >= 4 and j % 2 == 0:
                    act.wait_ge(*stage_stored[u].last())
                dst, row = stage[:, u, :, (j % 2) * P:(j % 2 + 1) * P], 6 + j
            cp(dst, zq).then_inc(*act_.mark())
            cp(tmS[0:B, row, :], z[0:B, TP:TP + P]).then_inc(*act_.mark("tm", n))
            if kind == "dk" and j % 2:
                u, g, hh = (j // 2) % 2, j // HG, (j % HG) - 1
                act.wait_ge(*act_.last())
                o = o_[f"p_dil{g + 1}"][0, 0]
                if g == 0:
                    act.dma_start(o[:, 0, hh:hh + 2, :].rearrange("t h d -> t (h d)"), stage[:, u, 1, :])\
                        .then_inc(*stage_stored[u].mark(by=16))
                else:
                    act.dma_start(o[:, 0, hh:hh + 2, :].rearrange("(q p) h d -> p q (h d)", p=P), stage[:, u, :, :])\
                        .then_inc(*stage_stored[u].mark(*(("last",) if j >= DHEADS - 4 else ()), by=16))
            if kind == "v":
                act.wait_ge(*act_.last())
                name = ("cmp", "sel", "win")[j]
                act.dma_start(o_["p_" + name][0, 0].rearrange("(q p) s h d -> p q (s h d)", p=P),
                              tmN[:, :, 2 * j:2 * j + 2, :].rearrange("p q j f -> p q (j f)"))\
                    .then_inc(*(cmp_stored.mark("p_cmp", by=16) if j == 0 else rows_stored.mark(by=16)))
                dst = o_["s_" + name][0, :, 0] if j < 2 else o_["s_win"][0, :, WIN - 1]
                act.dma_start(dst.rearrange("b s h d -> b (s h d)"),
                              tmS[0:B, 2 * j:2 * j + 2, :].rearrange("p j f -> p (j f)")).then_inc(*rows_stored.mark(by=16))
            if kind == "dv" and j % HG == HG - 1:
                g = j // HG
                act.wait_ge(*act_.last())
                o = o_[f"p_dil{g + 1}"][0, 0, :, 1]
                if g == 0:
                    act.dma_start(o.rearrange("t h d -> t (h d)"), tmV[:, 1, 0:HG, :].rearrange("p j f -> p (j f)"))\
                        .then_inc(*rows_stored.mark(by=16))
                else:
                    act.dma_start(o.rearrange("(q p) h d -> p q (h d)", p=P),
                                  tmV[:, :, g * HG:(g + 1) * HG, :].rearrange("p q j f -> p q (j f)"))\
                        .then_inc(*rows_stored.mark(by=16))
                for kv in range(2):
                    r = 6 + kv * DHEADS + g * HG
                    act.dma_start(o_[f"s_dil{g + 1}"][0, :, DIL[g][0] - 1, kv].rearrange("b h d -> b (h d)"),
                                  tmS[0:B, r:r + HG, :].rearrange("p j f -> p (j f)"))\
                        .then_inc(*rows_stored.mark(*(("all",) if (g, kv) == (NG - 1, 1) else ()), by=16))

        for n in range(NT + 2):
            if n < NT:
                act.wait_ge(*pe_.at("acc", n))
                if n + 2 < NT:
                    weights_high(n + 2)
                if n >= 3:
                    kind = TILES[n - 3][0]
                    if kind in ROPED:
                        act.wait_ge(*dve_.at("roped", n - 3))
                    elif kind in ("v", "dv"):
                        act.wait_ge(*pe_.at("tm", n - 3))
                    else:
                        act.wait_ge(*pe_.at("gateT"))
                m = 48 if n == 0 else P
                cp(tmp[0:m, n % 3, :], bank[n % 4][0:m, 0:T]).then_inc(*act_.mark("raw", n))
            if n == 1:
                act.wait_ge(*pe_.at("gateT"))
                A(gates.rearrange("p q j -> p (q j)"), bank[6][:, 0:96], ACT.Sigmoid).then_inc(*act_.mark())
                A(small[0:B, 0:48], bank[6][0:B, 128:176], ACT.Sigmoid).then_inc(*act_.mark("gateS"))
            if n >= 2:
                tm(n - 2)
        used = {}
        for n in range(NT):
            if TILES[n][0] in TURNED:
                act_.marks["tm_bank", n] = act_.marks[used.get(n % 2, ("gateS",))]
                used[n % 2] = ("tm", n)

        def compress(tag, kTc, nt, kc):
            per = max(1, nt // 4)
            for i in range(0, 4 * per, 2):
                act.wait_ge(*pe_.at("ctr", tag, i))
                w = min(nt, 4) * P
                sh, half = i // per, i % per
                cp(kTc[:, sh, half * 512:half * 512 + w], bank[4 + i % 2][:, 0:w]).then_inc(*act_.mark("ctr", tag, i))
            nb = nt * 16 - 1
            act.wait_ge(*pe_.at("hid", tag))
            cp(cbsh[0:64].rearrange("p (j n) -> p j n", j=4)[:, :, 0:nb],
               bank[0][64:128, :].rearrange("p (j n) -> p j n", j=4)[:, :, 1:nb + 1]).then_inc(*act_.mark("bsh", tag))
            act.wait_ge(*dve_.at("hid", tag))
            A(cgl[0:64].rearrange("p (j n) -> p j n", j=4)[:, :, 0:nb],
              chid[0:64].rearrange("p (j n) -> p j n", j=4)[:, :, 0:nb], ACT.Gelu_apprx_tanh).then_inc(*act_.mark("gelu", tag))
            act.wait_ge(*pe_.at("kvc", tag))
            cp(kc, bank[1][:, 0:nb]).then_inc(*act_.mark("kvc", tag))
        for s in range(2):
            act.wait_ge(*stage_stored[s].last())
        act.wait_ge(*pe_.at("pe"))
        cp(peb[0:64, :], bank[3][0:64, 0:2]).then_inc(*act_.mark("peb"))
        compress("p", kTcP, 1, kcP[:, 0:NBP])

        def pt_copy(u):
            act.wait_ge(*pe_.at("pt", u))
            if u >= 1:
                act.wait_ge(*pe_.at("pv", u - 1))
            bl = blocks(u)
            full = sum(k == P for _, k, _ in bl)
            marks = []
            for c in range(0, full, 4):
                w = min(4, full - c) * P
                marks.append((PT[:, c * P:c * P + w], bank[2 + c // 4][:, 0:w]))
            if full < len(bl):
                n = len(bl) - 1
                marks.append((PT[0:NBP, n * P:(n + 1) * P], bank[2 + n // 4][0:NBP, (n % 4) * P:(n % 4 + 1) * P]))
            for n, (o, s) in enumerate(marks):
                cp(o, s).then_inc(*act_.mark(*(("pt", u) if n == len(marks) - 1 else ())))

        def o_copy(u):
            kind, qt, h = UNITS[u]
            act.wait_ge(*pe_.at("pv", u))
            z = bank[4 + u % 2]
            if kind == "n":
                r = slice((h % 2) * DH, (h % 2 + 1) * DH)
                cp(oN[r, h // 2, qt * P:(qt + 1) * P], z[r, 0:P]).then_inc(*act_.mark("o", u))
            else:
                cp(oD[:, h, qt * P:(qt + 1) * P], z[:, 0:P]).then_inc(*act_.mark("o", u))

        for u in range(NU + 2):
            if u < NU:
                kind, qt, h = UNITS[u]
                W = P * (qt + 1)
                act.wait_ge(*dve_.at("nm", u))
                e = E[:, u % 2, :]
                if kind == "n":
                    for br in range(3):
                        a, z = (br * W, (br + 1) * W) if br < 2 else (2 * W, 2 * W + NBP)
                        A(e[:, a:z], e[:, a:z], ACT.Exp, bias=small[:, 8 * (u % 2) + br:8 * (u % 2) + br + 1], scale=SC_N,
                          accum_out=small[:, 16 + 8 * (u % 2) + br:17 + 8 * (u % 2) + br])\
                            .then_inc(*act_.mark(*(("e", u) if br == 2 else ())))
                else:
                    A(e[:, 0:3 * W], e[:, 0:3 * W], ACT.Exp, bias=small[:, 8 * (u % 2):8 * (u % 2) + 1], scale=SC_D,
                      accum_out=small[:, 16 + 8 * (u % 2):17 + 8 * (u % 2)]).then_inc(*act_.mark("e", u))
            if 1 <= u <= NU:
                pt_copy(u - 1)
            if u >= 2:
                o_copy(u - 2)

        act.wait_ge(*dve_.at("sample_q"))
        NX = 4 * B
        for x in range(NX + 3):
            if x < NX:
                act.wait_ge(*pe_.at("cx", x, 0))
                for h, l in PARTS:
                    cp(pair_columns(x, 0, h, l), turned_tokens(x, 0, h, l)).then_inc(*act_.mark(*(("cx", x) if (h, l) == (1, 1) else ())))
            if x >= 4 and x % 4 == 0:
                b = x // 4 - 1
                act.wait_ge(*pe_.at("hid", b))
                cp(cbsh[0:64].rearrange("p (j n) -> p j n", j=4)[:, :, 0:NBS],
                   bank[b % 2][64:128, :].rearrange("p (j n) -> p j n", j=4)[:, :, 1:NBS + 1]).then_inc(*act_.mark("bsh", b))
                act.wait_ge(*dve_.at("hid", b))
                A(cgl[0:64].rearrange("p (j n) -> p j n", j=4)[:, :, 0:NBS],
                  chid[0:64].rearrange("p (j n) -> p j n", j=4)[:, :, 0:NBS], ACT.Gelu_apprx_tanh).then_inc(*act_.mark("gelu", b))
            if x >= 5 and x % 4 == 1:
                b = x // 4 - 1
                act.wait_ge(*pe_.at("kvc", b))
                cp(kcS[:, 0:NBS], bank[2][:, 0:NBS]).then_inc(*act_.mark())
                cp(vcS[0:NBS, b, :], bank[2][0:NBS, P:2 * P]).then_inc(*act_.mark("kvc", b))
        act.wait_ge(*dve_.at("cm"))
        A(pcmp[:, 0:NBS], bank[3][:, 0:NBS], ACT.Exp, bias=small[:, 1:2], scale=SC_N,
          accum_out=small[:, 2:3]).then_inc(*act_.mark("ce"))
        act.wait_ge(*pe_.at("cpt"))
        cp(ptc[0:NBS, :], bank[1][0:NBS, 0:P]).then_inc(*act_.mark("cpt"))
        for y in range(0, 5 * B, 2):
            act.wait_ge(*pe_.at("ky", y))
            cp(KS[:, (y % 8) * 512:(y % 8 + 1) * 512], bank[4 + y % 3][:, :]).then_inc(*act_.mark("ky", y))
        act.wait_ge(*dve_.at("sm"))
        for br, (a, z) in enumerate(((0, 2056), (2056, 2576))):
            A(SS[:, a:z], SS[:, a:z], ACT.Exp, bias=small[:, 10 + br:11 + br], scale=SC_N,
              accum_out=small[:, 12 + br:13 + br]).then_inc(*act_.mark(*(("se",) if br else ())))
        for i in (0, 2, 4):
            act.wait_ge(*pe_.at("spt", i))
            cp(PTn[:, 4 * i:4 * i + 4, :].rearrange("p j r -> p (j r)"), bank[5 + i % 3][:, :]).then_inc(*act_.mark("pt", "s", i))
        act.wait_ge(*pe_.at("pvS", B - 1))
        for n in range(2):
            cp(oR[0:H, 4 * n:4 * n + 4, :].rearrange("p b f -> p (b f)"), bank[n][0:H, :]).then_inc(*act_.mark())
        act_.marks["oR",] = act_.n
        act.wait_ge(*pe_.at("oT"))
        for kv in range(2):
            for odd in range(2):
                cp(oN[odd * DH:(odd + 1) * DH, kv * 4:kv * 4 + 4, TP:T],
                   bank[4][kv * DH:(kv + 1) * DH, 0:P].rearrange("p (b h) -> p h b", b=B)[:, kv * G + odd:(kv + 1) * G:2, :])\
                    .then_inc(*act_.mark(*(("oN",) if (kv, odd) == (1, 1) else ())))
        for z in range(0, NG * B, 2):
            act.wait_ge(*pe_.at("kz", z))
            cp(KS[:, (z % 8) * 512:(z % 8 + 1) * 512], bank[5 + z % 3][:, :]).then_inc(*act_.mark("kz", z))
        act.wait_ge(*dve_.at("dm"))
        for g in range(NG):
            A(Ed[0:RD, g * P:(g + 1) * P], bank[g][0:RD, 0:P], ACT.Exp, bias=small[0:RD, 24:25], scale=SC_D,
              accum_out=small[0:RD, 28 + g:29 + g]).then_inc(*act_.mark())
        A(Ed[0:RD, 384:408], Ed[0:RD, 384:408], ACT.Exp, bias=small[0:RD, 24:25], scale=SC_D,
          accum_out=small[0:RD, 31:32]).then_inc(*act_.mark("de"))
        act.wait_ge(*pe_.at("pvD"))
        cp(oRd[0:RD, :], bank[0][0:RD, 0:P]).then_inc(*act_.mark("oRd"))
        act.wait_ge(*pe_.at("oTd"))
        cp(oD[:, :, TP:T], bank[1][:, 0:RD].rearrange("p (b h) -> p h b", b=B)).then_inc(*act_.mark("oD"))

        def high(a, buffer, f, k_tiles, done):
            raw = piece(a, SLOT, F32)[:, 0:k_tiles * CW].rearrange("p (k n) -> p k n", n=CW)[:, :, f * P:(f + 1) * P]
            cp(half_chunk(buffer, k_tiles), raw).then_inc(done, 1)

        def sigmoids(i, s, first):
            for f in range(2):
                act.wait_ge(mg_half, i * 6 + (2 * s + f + 1))
                if not first and s == f == 0:
                    act.wait_ge(mg_t, i * 4)
                A(sig[:, 2 * s + f, :], bank[4 * f + s][:, 0:T], ACT.Sigmoid).then_inc(mg_sig, 1)

        def merge(i, first):
            for s in range(3):
                act.wait_ge(w_ld["merge"][s], i * (32 if s == 2 else 16) + (32 if s == 2 else 16))
                for f in range(2):
                    n = 2 * s + f
                    if not first or n >= 3:
                        act.wait_ge(mg_half, i * 6 + (n - 2))
                    high(slot_at(s), merge_high[n % 3], f, 12 if s == 2 else KT, mg_high)
                    if first and n in (0, 2):
                        for k in range(KT) if n == 0 else range(KT, KT + 12):
                            cp(half_tile(x_high[k]), xs[k]).then_inc(*act_.mark("x_high", k))
                if s == 0 and not first:
                    act.wait_ge(mg_half, i * 6)
                    act.dma_start(slot(2)[:, 0:8, :], rows(w_bn, bass.ds(i * CW, CW))).then_inc(w_ld["merge"][2], 16)
                    act.dma_start(slot(2)[:, 8:12, :], rows(w_bd, bass.ds(i * CW, CW))).then_inc(w_ld["merge"][2], 16)
                if s == 2:
                    sigmoids(i, 0, first)
                    sigmoids(i, 1, first)
        xs = [hT[:, k, :] for k in range(KT)] + [oN[:, k, :] for k in range(8)] + [oD[:, k, :] for k in range(4)]
        sig = tmp
        act.wait_ge(*act_.at("oD"))
        act.wait_ge(*pe_.at("oTd"))
        merge(0, True)
        with act.Fori(1, 8) as i:
            merge(i, False)
        for n in range(16):
            s, f = n % 8 // 2, n % 2
            if f == 0:
                act.wait_ge(w_ld["wout"][s], 16 * (n // 8) + 16)
            if n >= 4:
                act.wait_ge(wo_half, n - 3)
            elif n:
                act.wait_ge(mg_half, 45 + n)
            high(slot_at(s), wout_high[n % 4], f, KT, wo_high)
            if n == 0:
                act.wait_ge(mg_half, 48)
                for k in range(KT):
                    act.wait_ge(mg_kept, k + 1)
                    cp(half_tile(x_high[k]), mT[:, k, :]).then_inc(*act_.mark("m_high", k))
        def ffn_first():
            for n in range(4):
                act.wait_ge(w_ld["ffn"][n // 2], 16)
                act.wait_ge(wo_half, (14, 15, 16, 13)[n])
                high(slot_at(n // 2), ffn_high[n], n % 2, KT, ff_high)
        ffn_first()
        norm("n2", 3)

        for k in range(KT):
            act.wait_ge(*(act_.at("h", "n2", k) if k < KT - 1 else act_.at("h", "n2")))
            act.wait_ge(*dve_.at("h", "n2"))
            cp(half_tile(h_high[k]), hT[:, k, :]).then_inc(*act_.mark("h_high", k))

        def ffn(i, first):
            for s in range(4):
                act.wait_ge(w_ld["ffn"][s], i * 16 + 16)
                for f in range(2):
                    n = 2 * s + f
                    if first and n < 4:
                        continue
                    if not first or n >= 4:
                        act.wait_ge(ff_half, i * 8 + (n - 3))
                    high(slot_at(s), ffn_high[n % 4], f, KT, ff_high)
                if s < 2:
                    continue
                g = 2 * (s - 2)
                for f in range(2):
                    act.wait_ge(ff_half, i * 8 + (2 * g + f + 1))
                    if not first:
                        act.wait_ge(ff_kept, i * 4 + (g + f - 3))
                    A(tmp[:, g + f, :], bank[2 * g + f][:, 0:T], ACT.Silu).then_inc(ff_silu, 1)
        ffn(0, True)
        with act.Fori(1, 11) as i:
            ffn(i, False)

        def down(i, u, very_first=False):
            for s in range(4):
                act.wait_ge(w_ld["down"][s], i * 32 + (16 * u + 16))
                for f in range(2):
                    n = 2 * s + f
                    if not very_first or n >= 4:
                        act.wait_ge(dn_half, i * 16 + (8 * u + n - 3))
                    high(slot_at(s), down_high[n % 4], f, KD, dn_high)
                    if very_first and f == 0:
                        for k in range(KD):
                            cp(half_tile(f_high[s * KD + k]), fT[:, s * KD + k, :]).then_inc(*act_.mark(f"f_high{s}", k))
        act.wait_ge(ff_half, 88)
        act.wait_ge(ff_kept, 44)
        down(0, 0, True)
        down(0, 1)
        with act.Fori(1, 4) as i:
            down(i, 0)
            down(i, 1)
        norm("nf", None)
        for k in range(0, KT, 2):
            act.wait_ge(*pe_.at("y", k))
            z = bank[k % 8]
            cp(y_tm[:, :, k * P:(k + 1) * P], z[:, 0:TP].rearrange("p (q f) -> p q f", q=QT)).then_inc(*act_.mark())
            cp(y_ts[0:B, k * P:(k + 1) * P], z[0:B, TP:TP + P]).then_inc(*act_.mark("y", k))

    @block.vector
    def _(dve):
        v = nc.vector

        def link(ins):
            ins.then_inc(*dve_.mark())
            dve.wait_ge(*dve_.last())

        v.memset(ada_row, 0.0).then_inc(*dve_.mark("ada_row"))
        dve.wait_ge(rows_loaded, 8 * 16)
        dve.wait_ge(*act_.at("sig"))
        v.tensor_tensor(c_silu[0:9, :], c_rows[0:9, :], c_silu[0:9, :], ALU.mult).then_inc(*dve_.mark("silu"))
        dve.wait_ge(*pe_.at("vecT"))
        v.tensor_copy(biasT, bank[1][:, 0:96]).then_inc(*dve_.mark())
        v.tensor_copy(gT, bank[1][:, 96:144]).then_inc(*dve_.mark("vecT"))
        dve.wait_ge(*act_.at("siluT"))
        v.tensor_tensor(silu_part(silu_low), siluT.rearrange("p j c -> p (j c)"), silu_part(silu_high).bitcast(F32),
                        ALU.subtract).then_inc(*dve_.mark("silu_low"))
        for k in range(1, KT, 2):
            dve.wait_ge(*pe_.at("xT", k))
            v.tensor_copy(xT[:, k, :], bank[2 + k % 4][:, 0:T]).then_inc(*dve_.mark("xT", k))
        dve_.marks["x_in",] = dve_.n
        dve.wait_ge(*dve_.at("vecT"))

        def ada(i, s):
            dve.wait_ge(ada_turned, i * 4 + (s + 1))
            v.tensor_tensor(modT[:, bass.ds(i * 8 + 2 * s, 2), :], bank[4 + s][:, 0:CW].rearrange("p (f c) -> p f c", f=2)[:, :, 0:9],
                            biasT[:, bass.ds(i * 8 + 2 * s, 2)].unsqueeze(2).broadcast_to([P, 2, 9]), ALU.add).then_inc(ada_kept, 1)

        def ada_low_halves(i, s):
            for h in range(2):
                dve.wait_ge(ada_high, i * 8 + (2 * s + h + 1))
                v.tensor_tensor(ada_piece(slot_at(s), h), slot(s)[:, 8 * h:8 * h + 8, :],
                                ada_piece(ada_buffer[(2 * s + h) % 4]).bitcast(F32), ALU.subtract).then_inc(ada_low, 1)
        for s in range(4):
            ada_low_halves(0, s)
            if s == 3:
                ada(0, 0)
        with dve.Fori(1, 12) as i:
            for s in range(4):
                ada_low_halves(i, s)
                ada(i + (-1 if s < 3 else 0), (s - 3) % 4)
        for s in (1, 2, 3):
            ada(11, s)
        dve.wait_ge(ada_kept, 48)
        dve.wait_ge(*act_.at("xT", KT - 2))
        dve.wait_ge(*dve_.at("xT", KT - 1))

        def square(tag, k):
            if k >= 4:
                dve.wait_ge(*pe_.at("sq", tag, k - 4))
            v.tensor_tensor(tmp[:, k % 4, :], xT[:, k, :], xT[:, k, :], ALU.mult).then_inc(*dve_.mark("sq", tag, k))

        def norm(tag, g, shift):
            if tag == "n1":
                for k in range(KT):
                    square(tag, k)
            if tag == "nf":
                dve.wait_ge(nf_used, 16)
            else:
                dve.wait_ge(*pe_.at("sq", tag, KT - 1))
            v.tensor_scalar(rstd, bank[7][:, 0:T], 1.0 / D, EPS, ALU.mult, ALU.add).then_inc(*dve_.mark("ms", tag))
            if shift is not None:
                scale = modT[:, (shift + 1) * KT:(shift + 2) * KT, :]
                link(v.scalar_tensor_tensor(out=facA, in0=scale, scalar=1.0,
                                            in1=gT[:, g * KT:(g + 1) * KT].unsqueeze(2).broadcast_to([P, KT, 9]),
                                            op0=ALU.add, op1=ALU.mult))
            dve.wait_ge(*act_.at("root", tag))
            link(v.reciprocal(rstd, rstd))
            if shift is None:
                return
            for k in range(KT):
                v.scalar_tensor_tensor(out=hT[:, k, 0:TP], in0=xT[:, k, 0:TP], scalar=facA[:, k, 0:1],
                                       in1=rstd[:, 0:TP], op0=ALU.mult, op1=ALU.mult).then_inc(*dve_.mark("hs", tag, k))
            hS = hT[:, :, TP:T]
            link(v.tensor_tensor(hS, xT[:, :, TP:T], facA[:, :, 1:9], ALU.mult))
            link(v.tensor_tensor(hS, hS, rstd[:, TP:T].unsqueeze(1).broadcast_to([P, KT, B]), ALU.mult))
            v.tensor_tensor(hS, hS, modT[:, shift * KT:(shift + 1) * KT, 1:9], ALU.add).then_inc(*dve_.mark("h", tag))

        def weights_low(n):
            dve.wait_ge(*act_.at("w_high", n))
            a = chunk_low(n)
            v.tensor_tensor(chunk_piece(a, n, F32R), chunk_piece(a, n, F32), chunk_piece(chunk_high(n), n, F32R).bitcast(F32),
                            ALU.subtract).then_inc(*dve_.mark("w_low", n))
        norm("n1", 0, 0)
        weights_low(0)
        for k in range(KT):
            dve.wait_ge(*act_.at("n1_high", k))
            v.tensor_tensor(half_tile(n1_low[k]), hT[:, k, :], half_tile(n1_high[k]).bitcast(F32), ALU.subtract)\
                .then_inc(*dve_.mark("n1_low", k))
        weights_low(1)

        roped = []
        for n in range(NT):
            kind, j = TILES[n]
            if n + 2 < NT:
                weights_low(n + 2)
            if n == 1:
                dve.wait_ge(*pe_.at("gateS"))
                g48 = rt[:, 0, 0:48].rearrange("p (j h) -> p j h", j=3)
                link(v.tensor_tensor(g48, bank[7][:, 0:48].rearrange("p (j h) -> p j h", j=3),
                                     const("head_of").unsqueeze(1).broadcast_to([P, 3, H]), ALU.mult))
                link(v.tensor_reduce(gatesS, g48, AX.X, ALU.add))
            if kind not in ROPED:
                continue
            c = "nsa" if kind in "kq" else "dil"
            dve.wait_ge(*act_.at("raw", n))
            if roped:
                dve.wait_ge(*dve_.at("roped", roped[-1]))
            v.tensor_tensor(rt[:, 0, :], tmp[:, n % 3, :], const("cos_" + c), ALU.mult).then_inc(*dve_.mark())
            dve.wait_ge(*pe_.at("rot", n))
            link(v.tensor_tensor(rt[:, 1, :], bank[4 + n % 2][:, 0:T], const("sin_" + c), ALU.mult))
            if kind == "q":
                kv = j // 4
                for odd in range(2):
                    r = slice(odd * DH, (odd + 1) * DH)
                    last = v.tensor_tensor(qK[kv * DH:(kv + 1) * DH, (2 * j + odd) % G, :], rt[r, 0, :], rt[r, 1, :], ALU.add)
                    last.then_inc(*dve_.mark(*(("roped", n) if odd else ())))
            else:
                dst = {"k": lambda: kT[:, j, :], "dq": lambda: dqk[:, j, :], "dk": lambda: dqk[:, DHEADS + j, :]}[kind]()
                v.tensor_tensor(dst, rt[:, 0, :], rt[:, 1, :], ALU.add).then_inc(*dve_.mark("roped", n))
            roped.append(n)
        for n in roped:
            before = [m for m in roped if m < n and m % 2 == n % 2]
            dve_.marks["rope_bank", n] = dve_.marks["roped", before[-1]] if before else 1

        def compress(tag, kTc, nt, vc):
            per = max(1, nt // 4)
            for i in range(1, 4 * per, 2):
                dve.wait_ge(*pe_.at("ctr", tag, i))
                w = min(nt, 4) * P
                sh, half = i // per, i % per
                v.tensor_copy(kTc[:, sh, half * 512:half * 512 + w], bank[4 + i % 2][:, 0:w]).then_inc(*dve_.mark("ctr", tag, i))
            nb = nt * 16 - 1
            dve.wait_ge(*act_.at("bsh", tag))
            dve.wait_ge(*act_.at("peb"))
            for s in range(2):
                v.scalar_tensor_tensor(out=chid[0:64].rearrange("p (j n) -> p j n", j=4)[:, 2 * s:2 * s + 2, 0:nb],
                                       in0=bank[0][0:64, :].rearrange("p (j n) -> p j n", j=4)[:, 2 * s:2 * s + 2, 0:nb],
                                       scalar=peb[0:64, s:s + 1],
                                       in1=cbsh[0:64].rearrange("p (j n) -> p j n", j=4)[:, 2 * s:2 * s + 2, 0:nb],
                                       op0=ALU.add, op1=ALU.add).then_inc(*dve_.mark(*(("hid", tag) if s else ())))
            dve.wait_ge(*pe_.at("kvc", tag))
            v.tensor_copy(vc, bank[2][0:nb, 0:P]).then_inc(*dve_.mark("kvc", tag))
        compress("p", kTcP, 1, vcP[0:NBP, :])

        dve.wait_ge(pages_loaded, 8 * 16)
        v.scalar_tensor_tensor(out=runs[:], in0=pages[:], scalar=8.0, in1=const("part8").broadcast_to([P, B]),
                               op0=ALU.mult, op1=ALU.add).then_inc(*dve_.mark("runs"))
        dve.wait_ge(*pe_.at("acc", NT - 1))
        for k in range(KT):
            v.tensor_tensor(hT[:, k, :], half_tile(n1_low[k]).bitcast(F32), half_tile(n1_high[k]).bitcast(F32), ALU.add)\
                .then_inc(*dve_.mark("h_whole", k))
        for u in range(NU):
            kind, qt, h = UNITS[u]
            W = P * (qt + 1)
            c = 8 * (u % 2)
            mx, nm, den = small[:, 32:35], small[:, c:c + 3], small[:, 16 + c:19 + c]
            e = E[:, u % 2, :]
            if u == 0:
                dve.wait_ge(*act_.at("kvc", "p"))
            if u >= 2:
                dve.wait_ge(*pe_.at("pt", u - 2))
            dve.wait_ge(*pe_.at("s", u))
            if kind == "n":
                mask = const("causal")[:, 0:P] if qt == 0 else const("causal")[:, P:3 * P]
                for br in range(2):
                    v.tensor_tensor_reduce(e[:, br * W:(br + 1) * W], bank[0][:, br * W:(br + 1) * W], mask, 1.0, -3e38,
                                           ALU.add, ALU.max, mx[:, br:br + 1]).then_inc(*dve_.mark())
                v.tensor_tensor_reduce(e[:, 2 * W:2 * W + NBP], bank[1][:, 0:NBP], const("cmp_add")[:, qt * NBP:(qt + 1) * NBP],
                                       1.0, -3e38, ALU.add, ALU.max, mx[:, 2:3]).then_inc(*dve_.mark("max", u))
                dve.wait_ge(*dve_.last())
                v.tensor_scalar(nm, mx, -SC_N, None, ALU.mult).then_inc(*dve_.mark("nm", u))
                dve.wait_ge(*act_.at("e", u))
                link(v.tensor_tensor_reduce(e[:, 2 * W:2 * W + NBP], e[:, 2 * W:2 * W + NBP],
                                            const("cmp_mul")[:, qt * NBP:(qt + 1) * NBP], 1.0, 0.0, ALU.mult, ALU.add,
                                            den[:, 2:3]))
                link(v.tensor_scalar(den, den, 1e-30, None, ALU.max))
                link(v.reciprocal(den, den))
                g3 = gates[:, qt, :].rearrange("p (r h) -> p r h", h=H)[:, :, h]
                v.tensor_tensor(den[:, 0:2], den[:, 0:2], g3[:, 1:3], ALU.mult).then_inc(*dve_.mark())
                link(v.tensor_tensor(den[:, 2:3], den[:, 2:3], g3[:, 0:1], ALU.mult))
                for br in range(3):
                    a, z = (br * W, (br + 1) * W) if br < 2 else (2 * W, 2 * W + NBP)
                    v.tensor_scalar(e[:, a:z], e[:, a:z], den[:, br:br + 1], None, ALU.mult)\
                        .then_inc(*dve_.mark(*(("p", u) if br == 2 else ())))
            else:
                mask = const("dilmask")[:, 0:3 * P] if qt == 0 else const("dilmask")[:, 3 * P:9 * P]
                v.tensor_tensor_reduce(e[:, 0:2 * W], bank[0][:, 0:2 * W], mask[:, 0:2 * W], 1.0, -3e38, ALU.add, ALU.max,
                                       mx[:, 0:1]).then_inc(*dve_.mark())
                v.tensor_tensor_reduce(e[:, 2 * W:3 * W], bank[1][:, 0:W], mask[:, 2 * W:3 * W], 1.0, -3e38, ALU.add, ALU.max,
                                       mx[:, 1:2]).then_inc(*dve_.mark("max", u))
                dve.wait_ge(*dve_.last())
                link(v.tensor_tensor(mx[:, 0:1], mx[:, 0:1], mx[:, 1:2], ALU.max))
                v.tensor_scalar(nm[:, 0:1], mx[:, 0:1], -SC_D, None, ALU.mult).then_inc(*dve_.mark("nm", u))
                dve.wait_ge(*act_.at("e", u))
                link(v.reciprocal(den[:, 0:1], den[:, 0:1]))
                v.tensor_scalar(e[:, 0:3 * W], e[:, 0:3 * W], den[:, 0:1], None, ALU.mult).then_inc(*dve_.mark("p", u))

        dve.wait_ge(*pe_.at("pv", NU - 1))
        dve.wait_ge(*rows_stored.at("all"))
        dve.wait_ge(*cmp_stored.at("p_cmp"))
        v.memset(qbd, 0.0).then_inc(*dve_.mark())
        v.memset(imp[0:H, :], 0.0).then_inc(*dve_.mark())
        link(v.memset(qfull, 0.0))
        q16 = qfull.rearrange("p (b h) -> p b h", h=H)
        for kv in range(2):
            r = slice(kv * DH, (kv + 1) * DH)
            v.tensor_copy(q16[r, :, kv * G:(kv + 1) * G], qK[r, :, TP:T].rearrange("p g b -> p b g")).then_inc(*dve_.mark())
        dve.wait_ge(*dve_.last())
        for b in range(B):
            v.tensor_copy(qbd[:, b, b * H:(b + 1) * H], q16[:, b, :]).then_inc(*dve_.mark())
        v.tensor_copy(dqnew, dqk[:, 0:DHEADS, TP:T]).then_inc(*dve_.mark())
        v.tensor_copy(dknew, dqk[:, DHEADS:2 * DHEADS, TP:T]).then_inc(*dve_.mark())
        v.tensor_copy(knew, kT[:, 1:3, TP:T]).then_inc(*dve_.mark("sample_q"))
        dve.wait_ge(*dve_.last())

        NX = 4 * B
        for x in range(NX + 3):
            if x < NX:
                dve.wait_ge(*pe_.at("cx", x, 1))
                for h, l in PARTS:
                    v.tensor_copy(pair_columns(x, 1, h, l), turned_tokens(x, 1, h, l)).then_inc(*dve_.mark(*(("cx", x) if (h, l) == (1, 1) else ())))
            if x >= 4 and x % 4 == 0:
                b = x // 4 - 1
                dve.wait_ge(*act_.at("bsh", b))
                for s in range(2):
                    v.scalar_tensor_tensor(out=chid[0:64].rearrange("p (j n) -> p j n", j=4)[:, 2 * s:2 * s + 2, 0:NBS],
                                           in0=bank[b % 2][0:64, :].rearrange("p (j n) -> p j n", j=4)[:, 2 * s:2 * s + 2, 0:NBS],
                                           scalar=peb[0:64, s:s + 1],
                                           in1=cbsh[0:64].rearrange("p (j n) -> p j n", j=4)[:, 2 * s:2 * s + 2, 0:NBS],
                                           op0=ALU.add, op1=ALU.add).then_inc(*dve_.mark(*(("hid", b) if s else ())))
        dve.wait_ge(*pe_.at("cs", B - 1))
        link(v.tensor_reduce(small[:, 0:1], bank[3][:, 0:NBS], AX.X, ALU.max))
        v.tensor_scalar(small[:, 1:2], small[:, 0:1], -SC_N, None, ALU.mult).then_inc(*dve_.mark("cm"))
        dve.wait_ge(*act_.at("ce"))
        link(v.tensor_scalar(small[:, 2:3], small[:, 2:3], 1e-30, None, ALU.max))
        link(v.reciprocal(small[:, 2:3], small[:, 2:3]))
        v.tensor_scalar(pcmp[:, 0:NBS], pcmp[:, 0:NBS], small[:, 2:3], None, ALU.mult).then_inc(*dve_.mark("cp"))
        dve.wait_ge(*pe_.at("imp"))
        v.tensor_scalar(pcmp[:, 0:NBS], pcmp[:, 0:NBS], gatesS[:, 0:1], None, ALU.mult).then_inc(*dve_.mark("cpg"))
        dve.wait_ge(sample_const, 32)
        link(v.tensor_copy(imp[0:H, 0:NBS], bank[0][0:H, 0:NBS]))
        sc, rank = sel[0:H, 1, :], sel[0:H, 2, :]
        link(v.tensor_reduce(sc, imp[0:H, :].rearrange("p (j r) -> p j r", r=4), AX.X, ALU.add))
        link(v.tensor_tensor(sel[0:H, 1, 1:NSEL], sel[0:H, 1, 1:NSEL],
                             imp[0:H, :].rearrange("p (j r) -> p j r", r=4)[:, 0:NSEL - 1, 3], ALU.add))
        link(v.tensor_tensor(sc, sc, const("keep")[0:H], ALU.mult))
        link(v.tensor_tensor(sc, sc, const("force")[0:H], ALU.add))
        mine = sc.unsqueeze(2).broadcast_to([H, NSEL, NSEL])
        other = sc.unsqueeze(1).broadcast_to([H, NSEL, NSEL])
        before = const("before")[0:H].rearrange("p (j i) -> p j i", i=NSEL)
        link(v.tensor_tensor(rk[0:H], other, mine, ALU.is_equal))
        link(v.tensor_tensor(rk[0:H], rk[0:H], before, ALU.mult))
        link(v.tensor_reduce(rank, rk[0:H], AX.X, ALU.add))
        link(v.tensor_tensor(rk[0:H], other, mine, ALU.is_gt))
        link(v.tensor_reduce(sel[0:H, 3, :], rk[0:H], AX.X, ALU.add))
        link(v.tensor_tensor(rank, rank, sel[0:H, 3, :], ALU.add))
        v.tensor_scalar(sel[0:H, 0, :], rank, float(TOPK), None, ALU.is_lt).then_inc(*dve_.mark("sel"))
        dve.wait_ge(*pe_.at("spread"))
        v.tensor_scalar(am, bank[0][:, 256:256 + NSEL], -1.0, -NEG, ALU.add, ALU.mult).then_inc(*dve_.mark("am"))
        dve.wait_ge(*dve_.last())

        for y in range(1, 5 * B, 2):
            dve.wait_ge(*pe_.at("ky", y))
            v.tensor_copy(KS[:, (y % 8) * 512:(y % 8 + 1) * 512], bank[4 + y % 3][:, :]).then_inc(*dve_.mark("ky", y))
        for i in range(4):
            dve.wait_ge(*pe_.at("sy", 5 * (B - 1) + i))
            mask = am[:, 0:32].unsqueeze(1).unsqueeze(3).broadcast_to([P, 4, 32, 4])
            v.tensor_tensor(SS[:, i * 512:(i + 1) * 512].rearrange("p (t j k) -> p t j k", t=4, k=4),
                            bank[i][:, :].rearrange("p (t j k) -> p t j k", t=4, k=4), mask, ALU.add).then_inc(*dve_.mark())
        dve.wait_ge(*pe_.at("sy", 5 * B - 1))
        v.tensor_copy(SS[:, 2056:2568], bank[7][:, :]).then_inc(*dve_.mark())
        dve.wait_ge(*pe_.at("snew"))
        for br, c in enumerate((2048, 2568)):
            v.tensor_tensor(SS[:, c:c + B], bank[4][:, br * B:(br + 1) * B], const("new_nsa"), ALU.add).then_inc(*dve_.mark())
        dve.wait_ge(*dve_.last())
        v.tensor_reduce(small[:, 8:9], SS[:, 0:2056], AX.X, ALU.max).then_inc(*dve_.mark())
        link(v.tensor_reduce(small[:, 9:10], SS[:, 2056:2576], AX.X, ALU.max))
        v.tensor_scalar(small[:, 10:12], small[:, 8:10], -SC_N, None, ALU.mult).then_inc(*dve_.mark("sm"))
        dve.wait_ge(*act_.at("se"))
        link(v.tensor_scalar(small[:, 12:14], small[:, 12:14], 1e-30, None, ALU.max))
        link(v.reciprocal(small[:, 12:14], small[:, 12:14]))
        link(v.tensor_tensor(small[:, 12:14], small[:, 12:14], gatesS[:, 1:3], ALU.mult))
        v.tensor_scalar(SS[:, 0:2056], SS[:, 0:2056], small[:, 12:13], None, ALU.mult).then_inc(*dve_.mark())
        v.tensor_scalar(SS[:, 2056:2576], SS[:, 2056:2576], small[:, 13:14], None, ALU.mult).then_inc(*dve_.mark("sp"))
        for i in (1, 3):
            dve.wait_ge(*pe_.at("spt", i))
            v.tensor_copy(PTn[:, 4 * i:4 * i + 4, :].rearrange("p j r -> p (j r)"), bank[5 + i % 3][:, :]).then_inc(*dve_.mark("pt", "s", i))
        dve.wait_ge(*pe_.at("spt", 5))
        v.tensor_copy(PTn[0:B, 20:22, :].rearrange("p j r -> p (j r)"), bank[4][0:B, 0:2 * P]).then_inc(*dve_.mark("pt", "s", 5))

        dve.wait_ge(*pe_.at("oT"))
        link(v.memset(qn, 0.0))
        for h in range(HG):
            v.tensor_copy(qn.rearrange("p j (b m) -> p j b m", m=HG)[:, h:DHEADS:HG, :, h], dqnew[:, h:DHEADS:HG, :])\
                .then_inc(*dve_.mark())
        link(v.memset(qpad, 0.0))
        for b in range(B):
            v.tensor_copy(qpad[:, :, b, b * HG:(b + 1) * HG], qn[:, :, b * HG:(b + 1) * HG])\
                .then_inc(*dve_.mark(*(("qpad",) if b == B - 1 else ())))
        for z in range(1, NG * B, 2):
            dve.wait_ge(*pe_.at("kz", z))
            v.tensor_copy(KS[:, (z % 8) * 512:(z % 8 + 1) * 512], bank[5 + z % 3][:, :]).then_inc(*dve_.mark("kz", z))
        dve.wait_ge(*pe_.at("dnew"))
        v.tensor_tensor(Ed[0:RD, 384:408].rearrange("p (g k) -> p g k", g=NG), bank[3][0:RD, 0:NG * B].rearrange("p (g k) -> p g k", g=NG),
                        const("new_dil")[0:RD].unsqueeze(1).broadcast_to([RD, NG, B]), ALU.add).then_inc(*dve_.mark())
        for g in range(NG):
            v.tensor_reduce(small[0:RD, 24 + g:25 + g], bank[g][0:RD, 0:P], AX.X, ALU.max).then_inc(*dve_.mark())
        dve.wait_ge(*dve_.last())
        link(v.tensor_reduce(small[0:RD, 27:28], Ed[0:RD, 384:408], AX.X, ALU.max))
        link(v.tensor_reduce(small[0:RD, 32:33], small[0:RD, 24:28], AX.X, ALU.max))
        v.tensor_scalar(small[0:RD, 24:25], small[0:RD, 32:33], -SC_D, None, ALU.mult).then_inc(*dve_.mark("dm"))
        dve.wait_ge(*act_.at("de"))
        link(v.tensor_reduce(small[0:RD, 33:34], small[0:RD, 28:32], AX.X, ALU.add))
        link(v.reciprocal(small[0:RD, 33:34], small[0:RD, 33:34]))
        v.tensor_scalar(Ed[0:RD, :], Ed[0:RD, :], small[0:RD, 33:34], None, ALU.mult).then_inc(*dve_.mark("dp"))
        dve.wait_ge(*pe_.at("dpt"))
        dve.wait_ge(sample_const, 48)
        for g in range(NG):
            v.tensor_tensor(PTm[:, g], bank[4][:, g * RD:(g + 1) * RD].unsqueeze(2).broadcast_to([P, RD, RD]),
                            const("eye").rearrange("p (r c) -> p r c", r=RD), ALU.mult).then_inc(*dve_.mark())
        for g in range(NG):
            v.tensor_tensor(Pn[0:B, g], bank[4][0:B, 96 + g * RD:96 + (g + 1) * RD].unsqueeze(1).broadcast_to([B, HG, RD]),
                            const("head_cols")[0:B].rearrange("p (h r) -> p h r", h=HG), ALU.mult)\
                .then_inc(*dve_.mark(*(("PTm",) if g == NG - 1 else ())))

        def low_tile(a, raw, high_at):
            return v.tensor_tensor(half_tile(a), raw, half_tile(high_at).bitcast(F32), ALU.subtract)

        def low(a, buffer, f, k_tiles, done):
            raw = piece(a, SLOT, F32)[:, 0:k_tiles * CW].rearrange("p (k n) -> p k n", n=CW)[:, :, f * P:(f + 1) * P]
            v.tensor_tensor(half_chunk(a, k_tiles, f, CW), raw, half_chunk(buffer, k_tiles).bitcast(F32), ALU.subtract)\
                .then_inc(done, 1)

        def merge(i, first=False):
            dve.wait_ge(mg_half, i * 6 + 6)
            dve.wait_ge(mg_sig, i * 4 + 4)
            for f in range(2):
                for s in range(2):
                    v.tensor_tensor(prod[:, 2 * f + s, :], tmp[:, 2 * s + f, :], bank[4 * f + 2 + s][:, 0:T], ALU.mult).then_inc(mg_t, 1)
            dve.wait_ge(mg_t, i * 4 + 4)
            for f in range(2):
                v.tensor_tensor(mT[:, bass.ds(i * 2 + f, 1), :], prod[:, 2 * f, :].unsqueeze(1), prod[:, 2 * f + 1, :].unsqueeze(1),
                                ALU.add).then_inc(mg_kept, 1)
            dve.wait_ge(mg_kept, i * 2 + 2)

        def merge_low(i, halves, first=False):
            for n in halves:
                s, f = n // 2, n % 2
                dve.wait_ge(mg_high, i * 6 + (n + 1))
                low(slot_at(s), merge_high[n % 3], f, 12 if s == 2 else KT, mg_low)
                if first and n in (0, 2):
                    for k in range(KT) if n == 0 else range(KT, KT + 12):
                        dve.wait_ge(*act_.at("x_high", k))
                        low_tile(x_low[k], xs[k], x_high[k]).then_inc(*dve_.mark("x_low", k))
        xs = [hT[:, k, :] for k in range(KT)] + [oN[:, k, :] for k in range(8)] + [oD[:, k, :] for k in range(4)]
        merge_low(0, range(6), True)
        with dve.Fori(1, 8) as i:
            merge_low(i, range(2))
            merge(i + (-1))
            merge_low(i, range(2, 6))

        def wout_low(n):
            s, f = n % 8 // 2, n % 2
            dve.wait_ge(wo_high, n + 1)
            low(slot_at(s), wout_high[n % 4], f, KT, wo_low)
        wout_low(0)
        merge(7)
        for k in range(KT):
            dve.wait_ge(*act_.at("m_high", k))
            low_tile(m_low[k], mT[:, k, :], x_high[k]).then_inc(*dve_.mark("m_low", k))

        def residual(j, z, gate, products, n_products, kept):
            one = bass.ds(j, 1)
            v.tensor_tensor(xs8, z[:, TP:T].unsqueeze(1), modT[:, bass.ds(j + gate * KT, 1), 1:9], ALU.mult).then_inc(products, 1)
            v.scalar_tensor_tensor(out=xT[:, one, 0:TP], in0=z[:, 0:TP].unsqueeze(1), scalar=modT[:, bass.ds(j + gate * KT, 1), 0],
                                   in1=xT[:, one, 0:TP], op0=ALU.mult, op1=ALU.add).then_inc(products, 1)
            dve.wait_ge(products, n_products)
            v.tensor_tensor(xT[:, one, TP:T], xT[:, one, TP:T], xs8, ALU.add).then_inc(kept, 1)
        for n in range(1, 16 + 3):
            if n < 16:
                wout_low(n)
            if n >= 3:
                j = n - 3
                dve.wait_ge(wo_half, j + 1)
                if j:
                    dve.wait_ge(wo_kept, j)
                residual(j, bank[j % 7], 2, wo_t, 2 * (j + 1), wo_kept)
                dve.wait_ge(wo_kept, j + 1)
                square("n2", j)
        for n in range(4):
            dve.wait_ge(ff_high, n + 1)
            low(slot_at(n // 2), ffn_high[n], n % 2, KT, ff_low)
        dve.wait_ge(wo_kept, 16)
        norm("n2", 1, 3)

        def h_tiles():
            for k in range(KT):
                dve.wait_ge(*act_.at("h_high", k))
                low_tile(hT0 + k * T, hT[:, k, :], h_high[k]).then_inc(*dve_.mark("h_low", k))

        def hidden(i, g):
            dve.wait_ge(ff_half, i * 8 + (2 * g + 4))
            dve.wait_ge(ff_silu, i * 4 + (g + 2))
            for f in range(2):
                v.tensor_tensor(fT[:, bass.ds(i * 4 + g + f, 1), :], tmp[:, g + f, :].unsqueeze(1),
                                bank[2 * g + 2 + f][:, 0:T].unsqueeze(1), ALU.mult).then_inc(ff_kept, 1)

        def ffn(i, first):
            for s in range(4):
                for f in range(2):
                    if first and s < 2:
                        continue
                    dve.wait_ge(ff_high, i * 8 + (2 * s + f + 1))
                    low(slot_at(s), ffn_high[(2 * s + f) % 4], f, KT, ff_low)
                if first and s == 0:
                    h_tiles()
                if s == 0 and not first:
                    hidden(i + (-1), 2)
                if s == 3:
                    hidden(i, 0)
        ffn(0, True)
        with dve.Fori(1, 11) as i:
            ffn(i, False)
        hidden(10, 2)

        def down_low(i, u, s, very_first=False):
            for f in range(2):
                dve.wait_ge(dn_high, i * 16 + (8 * u + 2 * s + f + 1))
                low(slot_at(s), down_high[(2 * s + f) % 4], f, KD, dn_low)
                if very_first and f == 0:
                    for k in range(KD):
                        dve.wait_ge(*act_.at(f"f_high{s}", k))
                        low_tile(region + (s * KD + k) * T, fT[:, s * KD + k, :], f_high[s * KD + k])\
                            .then_inc(*dve_.mark(f"f_low{s}", k))

        def down_residual(c, kept_before, squares_before=True):
            i, u = c
            dve.wait_ge(dn_half, i * 16 + (8 * u + 8))
            for f in range(2):
                if kept_before or f:
                    dve.wait_ge(dn_kept, i * 4 + (2 * u + f))
                residual(i * 4 + (2 * u + f), bank[2 * u + f], 5, dn_t, i * 8 + (4 * u + 2 * f + 2), dn_kept)
                dve.wait_ge(dn_kept, i * 4 + (2 * u + f + 1))
                if squares_before:
                    dve.wait_ge(nf_used, i * 4 + (2 * u + f - 3))
                one = bass.ds(i * 4 + (2 * u + f), 1)
                v.tensor_tensor(tmp[:, 2 * u + f, :].unsqueeze(1), xT[:, one, :], xT[:, one, :], ALU.mult).then_inc(nf_sq, 1)

        def down(i, u, before, kept_before=True, very_first=False, squares_before=True):
            for s in range(4):
                down_low(i, u, s, very_first)
                if s == 1 and before is not None:
                    down_residual(before, kept_before, squares_before)
        down(0, 0, None, very_first=True)
        down(0, 1, (0, 0), False, squares_before=False)
        down(1, 0, (0, 1), squares_before=False)
        down(1, 1, (1, 0))
        with dve.Fori(2, 4) as i:
            down(i, 0, (i + (-1), 1))
            down(i, 1, (i, 0))
        down_residual((3, 1), True)
        dve.wait_ge(dn_kept, 16)
        norm("nf", 2, None)
        for n in range(KT + 2):
            if n < KT:
                v.scalar_tensor_tensor(out=hT[:, n, :], in0=xT[:, n, :], scalar=gT[:, 2 * KT + n:2 * KT + n + 1],
                                       in1=rstd, op0=ALU.mult, op1=ALU.mult).then_inc(*dve_.mark("yT", n))
            k = n - 2
            if k < 0 or k % 2 == 0:
                continue
            dve.wait_ge(*pe_.at("y", k))
            z = bank[k % 8]
            v.tensor_copy(y_tm[:, :, k * P:(k + 1) * P], z[:, 0:TP].rearrange("p (q f) -> p q f", q=QT)).then_inc(*dve_.mark())
            v.tensor_copy(y_ts[0:B, k * P:(k + 1) * P], z[0:B, TP:TP + P]).then_inc(*dve_.mark("y", k))

    return {name: s.marks for name, s in signals.items()}


def kernel(**inputs):
    from concourse import bacc
    from concourse.bass_utils import run_bass_kernel_spmd

    seen = None
    for _ in range(2):
        nc = bacc.Bacc("TRN2", target_bir_lowering=False, num_devices=1)
        ins = {n: nc.dram_tensor("in_" + n, s, I32 if n == "page_table" else F32, kind="ExternalInput").ap()
               for n, s in INS.items()}
        ins["const"] = nc.dram_tensor("in_const", (P, CONST_W), F32, kind="ExternalInput").ap()
        outs = {n: nc.dram_tensor("out_" + n, s, F32, kind="ExternalOutput").ap() for n, s in OUTS.items()}
        with ExitStack() as ctx:
            seen = program(nc, ins, outs, ctx, seen)
    arrays = {"in_" + n: np.ascontiguousarray(inputs[n]) for n in INS}
    arrays["in_const"] = constants()
    r = run_bass_kernel_spmd(nc, [arrays], core_ids=[0])
    return tuple(r.results[0]["out_" + n] for n in OUTS)
```
